# Optimizing a Trainium2 kernel written in Bass

```python
import math
import jax, jax.numpy as jnp
from jax import lax
import numpy as np

D_MODEL = 1024
BATCH = 1
SEQ = 512
DEPTH = 1

S5_WIDTH = D_MODEL // 2
S5_GROUP = 16
S5_GROUPS = S5_WIDTH // S5_GROUP
S5_STATE = 64
HGRN_WIDTH = D_MODEL // 2
HGRN_HEAD_DIM = 128
HGRN_HEADS = HGRN_WIDTH // HGRN_HEAD_DIM
HGRN_CHUNK = 64
PEER_HEADS = 8
PEER_TOPK = 16
PEER_NKEYS = 128
PEER_NEXPERTS = PEER_NKEYS * PEER_NKEYS
PEER_QDIM = 256
PEER_TOKEN_BLOCK = 128
IN_COLS = S5_WIDTH + 4 * HGRN_WIDTH + 2 * D_MODEL
DEEPNORM_ALPHA = (2.0 * DEPTH) ** 0.25
DEEPNORM_BETA = (8.0 * DEPTH) ** -0.25
LN_EPS = 1e-5
RMS_EPS = 1e-6

kernel_name = "hybrid_s5_hgrn2_peer_deepnorm"

def layer_norm(x, g, b):
    xf = x.astype(jnp.float32)
    mu = jnp.mean(xf, axis=-1, keepdims=True)
    var = jnp.mean(jnp.square(xf - mu), axis=-1, keepdims=True)
    y = (xf - mu) * lax.rsqrt(var + LN_EPS) * g.astype(jnp.float32) + b.astype(jnp.float32)
    return y.astype(x.dtype)

def s5_branch(u, lam_re, lam_im, b_re, b_im, c_re, c_im, d_skip, log_step, w_glu, b_glu):
    bsz, seq, _ = u.shape
    uf = u.astype(jnp.float32).reshape(bsz, seq, S5_GROUPS, S5_GROUP)
    lam = lax.complex(lam_re.astype(jnp.float32), lam_im.astype(jnp.float32))
    dt = jnp.exp(log_step.astype(jnp.float32))[:, None]
    lam_bar = jnp.exp(lam * dt)
    b_mat = lax.complex(b_re.astype(jnp.float32), b_im.astype(jnp.float32))
    b_bar = ((lam_bar - 1.0) / lam)[..., None] * b_mat
    bu = jnp.einsum('bsgh,gph->sbgp', uf.astype(jnp.complex64), b_bar)
    a = jnp.broadcast_to(lam_bar, (seq, 1, S5_GROUPS, S5_STATE))

    def combine(left, right):
        a_l, b_l = left
        a_r, b_r = right
        return a_r * a_l, a_r * b_l + b_r

    _, states = lax.associative_scan(combine, (a, bu), axis=0)
    c_mat = lax.complex(c_re.astype(jnp.float32), c_im.astype(jnp.float32))
    y = jnp.real(jnp.einsum('sbgp,ghp->bsgh', states, c_mat)) + d_skip.astype(jnp.float32) * uf
    y = jax.nn.gelu(y.reshape(bsz, seq, S5_WIDTH))
    y = y * jax.nn.sigmoid(y @ w_glu.astype(jnp.float32) + b_glu.astype(jnp.float32))
    return y.astype(u.dtype)

def hgrn2_branch(q, f_pre, i_in, g, lb, gnorm_w):
    bsz, seq, _ = q.shape
    n_chunks = seq // HGRN_CHUNK
    lbf = lb.astype(jnp.float32)
    f = lbf + (1.0 - lbf) * jax.nn.sigmoid(f_pre.astype(jnp.float32))
    log_f = jnp.log(f)
    k = 1.0 - f
    qf = jax.nn.silu(q.astype(jnp.float32))
    v = i_in.astype(jnp.float32)

    def to_chunks(t):
        return t.reshape(bsz, n_chunks, HGRN_CHUNK, HGRN_HEADS, HGRN_HEAD_DIM).transpose(1, 0, 3, 2, 4)

    causal = jnp.tril(jnp.ones((HGRN_CHUNK, HGRN_CHUNK), dtype=bool))[:, :, None]

    def step(state, inp):
        qc, kc, vc, lc = inp
        bcum = jnp.cumsum(lc, axis=-2)
        inter = jnp.einsum('bhck,bhkv->bhcv', qc * jnp.exp(bcum), state)
        diff = bcum[:, :, :, None, :] - bcum[:, :, None, :, :]
        decay = jnp.exp(jnp.where(causal, diff, -jnp.inf))
        scores = jnp.einsum('bhtk,bhsk,bhtsk->bhts', qc, kc, decay)
        intra = jnp.einsum('bhts,bhsv->bhtv', scores, vc)
        blast = bcum[:, :, -1:, :]
        new_state = (jnp.exp(blast[:, :, 0, :])[..., None] * state
                     + jnp.einsum('bhsk,bhsv->bhkv', kc * jnp.exp(blast - bcum), vc))
        return new_state, inter + intra

    s0 = jnp.zeros((bsz, HGRN_HEADS, HGRN_HEAD_DIM, HGRN_HEAD_DIM), jnp.float32)
    _, o = lax.scan(step, s0, (to_chunks(qf), to_chunks(k), to_chunks(v), to_chunks(log_f)))
    o = o.transpose(1, 0, 3, 2, 4).reshape(bsz, seq, HGRN_HEADS, HGRN_HEAD_DIM)
    o = o * lax.rsqrt(jnp.mean(jnp.square(o), axis=-1, keepdims=True) + RMS_EPS)
    o = o * gnorm_w.astype(jnp.float32).reshape(HGRN_HEADS, HGRN_HEAD_DIM)
    o = o.reshape(bsz, seq, HGRN_WIDTH) * jax.nn.silu(g.astype(jnp.float32))
    return o.astype(q.dtype)

def peer_layer(x, w_pq, sub_keys, peer_u, peer_v):
    bsz, seq, d = x.shape
    xt = x.reshape(-1, PEER_TOKEN_BLOCK, d)
    half = PEER_QDIM // 2

    def block(xb):
        q = (xb @ w_pq).reshape(PEER_TOKEN_BLOCK, PEER_HEADS, 2, half)
        s = jnp.einsum('thpd,hpnd->thpn', q, sub_keys).astype(jnp.float32)
        s1, i1 = lax.top_k(s[:, :, 0], PEER_TOPK)
        s2, i2 = lax.top_k(s[:, :, 1], PEER_TOPK)
        cand = (s1[..., :, None] + s2[..., None, :]).reshape(PEER_TOKEN_BLOCK, PEER_HEADS, PEER_TOPK * PEER_TOPK)
        top, flat = lax.top_k(cand, PEER_TOPK)
        e = (jnp.take_along_axis(i1, flat // PEER_TOPK, axis=-1) * PEER_NKEYS
             + jnp.take_along_axis(i2, flat % PEER_TOPK, axis=-1))
        gates = jax.nn.softmax(top, axis=-1)
        u = peer_u[e]
        act = jax.nn.gelu(jnp.einsum('thkd,td->thk', u, xb).astype(jnp.float32))
        return jnp.einsum('thk,thkd->td', (gates * act).astype(xb.dtype), peer_v[e])

    y = lax.map(block, xt)
    return y.reshape(bsz, seq, d)

def setup_inputs(seed: int = 0) -> dict:
    key = jax.random.key(seed)
    ks = jax.random.split(key, 32)
    nrm = lambda k, shape, scale: jax.random.normal(k, shape, jnp.float32) * scale
    L = DEPTH
    G, P, H, W = S5_GROUPS, S5_STATE, S5_GROUP, S5_WIDTH
    x = nrm(ks[0], (BATCH, SEQ, D_MODEL), 1.0)
    w_in = nrm(ks[1], (L, D_MODEL, IN_COLS), D_MODEL ** -0.5)
    s5_lam_re = -0.5 * jnp.exp(nrm(ks[2], (L, G, P), 0.01))
    s5_lam_im = math.pi * jnp.arange(P, dtype=jnp.float32)[None, None, :] + nrm(ks[3], (L, G, P), 0.01)
    s5_b_re = nrm(ks[4], (L, G, P, H), (2.0 * H) ** -0.5)
    s5_b_im = nrm(ks[5], (L, G, P, H), (2.0 * H) ** -0.5)
    s5_c_re = nrm(ks[6], (L, G, H, P), (2.0 * P) ** -0.5)
    s5_c_im = nrm(ks[7], (L, G, H, P), (2.0 * P) ** -0.5)
    s5_d = nrm(ks[8], (L, G, H), 1.0)
    s5_log_step = jax.random.uniform(ks[9], (L, G), jnp.float32, math.log(1e-3), math.log(1e-1))
    s5_w_glu = nrm(ks[10], (L, W, W), W ** -0.5)
    s5_b_glu = nrm(ks[11], (L, W), 0.01)
    hgrn_lb_logits = 1.0 + nrm(ks[12], (L + 1, HGRN_WIDTH), 0.1)
    hgrn_gnorm_w = 1.0 + nrm(ks[13], (L, HGRN_WIDTH), 0.01)
    w_pa = nrm(ks[14], (L, S5_WIDTH, D_MODEL), S5_WIDTH ** -0.5)
    w_pb = nrm(ks[15], (L, HGRN_WIDTH, D_MODEL), HGRN_WIDTH ** -0.5)
    w_o = nrm(ks[16], (L, D_MODEL, D_MODEL), D_MODEL ** -0.5 * DEEPNORM_BETA)
    ln1_g = 1.0 + nrm(ks[17], (L, D_MODEL), 0.01)
    ln1_b = nrm(ks[18], (L, D_MODEL), 0.01)
    peer_w_q = nrm(ks[19], (L, D_MODEL, PEER_HEADS * PEER_QDIM), D_MODEL ** -0.5)
    peer_sub_keys = nrm(ks[20], (L, PEER_HEADS, 2, PEER_NKEYS, PEER_QDIM // 2), (PEER_QDIM // 2) ** -0.5)
    peer_u = nrm(ks[21], (L, PEER_NEXPERTS, D_MODEL), D_MODEL ** -0.5)
    peer_v = nrm(ks[22], (L, PEER_NEXPERTS, D_MODEL), DEEPNORM_BETA)
    ln2_g = 1.0 + nrm(ks[23], (L, D_MODEL), 0.01)
    ln2_b = nrm(ks[24], (L, D_MODEL), 0.01)
    return {"x": x, "w_in": w_in, "s5_lam_re": s5_lam_re, "s5_lam_im": s5_lam_im,
            "s5_b_re": s5_b_re, "s5_b_im": s5_b_im, "s5_c_re": s5_c_re, "s5_c_im": s5_c_im,
            "s5_d": s5_d, "s5_log_step": s5_log_step, "s5_w_glu": s5_w_glu, "s5_b_glu": s5_b_glu,
            "hgrn_lb_logits": hgrn_lb_logits, "hgrn_gnorm_w": hgrn_gnorm_w,
            "w_pa": w_pa, "w_pb": w_pb, "w_o": w_o, "ln1_g": ln1_g, "ln1_b": ln1_b,
            "peer_w_q": peer_w_q, "peer_sub_keys": peer_sub_keys, "peer_u": peer_u, "peer_v": peer_v,
            "ln2_g": ln2_g, "ln2_b": ln2_b}

def reference(x, w_in, s5_lam_re, s5_lam_im, s5_b_re, s5_b_im, s5_c_re, s5_c_im,
              s5_d, s5_log_step, s5_w_glu, s5_b_glu, hgrn_lb_logits, hgrn_gnorm_w,
              w_pa, w_pb, w_o, ln1_g, ln1_b, peer_w_q, peer_sub_keys, peer_u, peer_v,
              ln2_g, ln2_b):
    lb_all = jnp.cumsum(jax.nn.softmax(hgrn_lb_logits.astype(jnp.float32), axis=0), axis=0)[:DEPTH]
    sizes = [S5_WIDTH, HGRN_WIDTH, HGRN_WIDTH, HGRN_WIDTH, HGRN_WIDTH, D_MODEL, D_MODEL]
    split_at = np.cumsum(sizes)[:-1].tolist()
    for l in range(DEPTH):
        proj = x @ w_in[l]
        u_s5, q_h, f_h, i_h, g_h, gate_a, gate_b = jnp.split(proj, split_at, axis=-1)
        y_a = s5_branch(u_s5, s5_lam_re[l], s5_lam_im[l], s5_b_re[l], s5_b_im[l],
                        s5_c_re[l], s5_c_im[l], s5_d[l], s5_log_step[l], s5_w_glu[l], s5_b_glu[l])
        y_b = hgrn2_branch(q_h, f_h, i_h, g_h, lb_all[l], hgrn_gnorm_w[l])
        merged = jax.nn.sigmoid(gate_a) * (y_a @ w_pa[l]) + jax.nn.sigmoid(gate_b) * (y_b @ w_pb[l])
        mix = merged @ w_o[l]
        x = layer_norm(DEEPNORM_ALPHA * x + mix, ln1_g[l], ln1_b[l])
        ffn = peer_layer(x, peer_w_q[l], peer_sub_keys[l], peer_u[l], peer_v[l])
        x = layer_norm(DEEPNORM_ALPHA * x + ffn, ln2_g[l], ln2_b[l])
    return x


_drawn_inputs = setup_inputs


def setup_inputs(seed=0):
    import zlib

    import numpy as np

    out = dict(_drawn_inputs(seed))
    spreads = {}
    factors = {'s5_lam_re': 200.0,
     's5_lam_im': 92.424,
     's5_b_re': 129.72,
     's5_b_im': 148.376,
     's5_c_re': 146.296,
     's5_c_im': 133.144,
     's5_log_step': 89.744,
     's5_b_glu': 35.448,
     'hgrn_lb_logits': 4.527,
     'hgrn_gnorm_w': 5.929,
     'ln2_g': 196.554,
     'ln2_b': 192.549}
    for name, (base, spread) in spreads.items():
        noise = np.random.default_rng([zlib.crc32(name.encode()), seed]).standard_normal(out[name].shape)
        drawn = base * np.exp(spread * noise) if base else spread * noise
        out[name] = __import__('jax').numpy.asarray(drawn.astype(out[name].dtype))
    for name, factor in factors.items():
        out[name] = (out[name] * factor).astype(out[name].dtype)
    return out
```

```python
from contextlib import ExitStack

import numpy as np
import concourse.bass as bass
from concourse import mybir

ALU = mybir.AluOpType
ACT = mybir.ActivationFunctionType
F32 = mybir.dt.float32
U32 = mybir.dt.uint32
U8 = mybir.dt.uint8
AX_X = mybir.AxisListType.X

P = 128
T = 512
D = 1024
NT = T // P
KD = D // P
W2 = 512
CH = W2 // P
G, NS, GH, L = 32, 64, 16, 8
NC = T // L
SCAN = 6
LEVELS = 7
HEADS = 8
K = 16
BLOCKS = NT * HEADS
NBUF = 8
ALPHA = 2.0 ** 0.25
LN_EPS = 1e-5
RMS_EPS = 1e-6
LOW = -3.0e38
ROUND = 1.5 * 2.0 ** 23
TWO_PI_A, TWO_PI_B, TWO_PI_C = 6.28125, 1.93500518798828125e-3, 3.0199159819e-7
PI = 3.1415925

CHUNK = 256
RING = 4
U_S5, U_F, U_Q, U_V, U_G, U_GA, U_GB, U_END = 0, 4, 8, 12, 16, 20, 28, 36
COL = {"u": 0, "q": 512, "f": 1024, "v": 1536, "g": 2048, "ga": 2560, "gb": 3584}
CHUNK_COLS = [COL[n] + CHUNK * i for n, m in
              (("u", 2), ("f", 2), ("q", 2), ("v", 2), ("g", 2), ("ga", 4), ("gb", 4)) for i in range(m)]


def hybrid_layer(nc, x, xT, w_in, lam_re, lam_im, b_re, b_im, c_re, c_im, d_skip, log_step, w_glu, b_glu,
                 lb_logits, gnorm, w_pa, w_pb, w_o, ln1_g, ln1_b, w_pq, keysT, peer_u, peer_v, ln2_g, ln2_b,
                 square_consts, sign_consts, iota16, level_masks, out):
    with ExitStack() as ctx:
        def sb(name, shape, dt=F32):
            return ctx.enter_context(nc.sbuf_tensor(name, shape, dt))

        def sem(name):
            return ctx.enter_context(nc.semaphore(name))

        arena = sb("arena", [P, 200 * 256])

        def part(kb, shape):
            n = int(np.prod(shape))
            v = arena[:, int(kb * 256):int(kb * 256) + n]
            if len(shape) == 1:
                return v
            names = "abcd"[:len(shape)]
            return v.rearrange(f"p ({' '.join(names)}) -> p {' '.join(names)}", **dict(zip(names, shape)))

        ring = part(0, [RING, KD, CHUNK])
        qT, fT, vS, gT = (part(32 + 8 * i, [CH, T]) for i in range(4))
        xTs = part(128, [KD, T])
        sga = part(144, [KD, T])
        sgb = part(160, [KD, T])
        WinT = part(64, [G, P])
        Toe = part(80, [G, P])
        Wout = part(96, [G, L + 1, GH])
        Uc = part(114, [G, NC])
        wtmp = part(122, [8, L + 1, GH])
        Ksb = part(144, [G, P])
        X, Xs, CX, CXs, BB, BBs = (part(160 + 2 * i, [G, GH]) for i in range(6))
        small = part(172, [G * 32])
        Wnat = [part(176 + 4 * i, [8, L, GH]) for i in range(2)]
        uT = part(184, [CH, L, NC])
        S = part(176, [G, NC])
        scan1 = part(64, [G, NC])
        scan2 = part(72, [G, NC])
        Yc = part(64, [G, NC])
        wglu = part(72, [CH, W2])
        yT = part(176, [CH, L, NC])
        zT = part(184, [CH, L, NC])
        yaT = part(192, [CH, T])
        masks_in = part(196, [LEVELS + 1, P])
        kT = part(80, [CH, T])
        bT = part(88, [CH, T])
        dec = [part(96, [CH, T]), part(104, [CH, T])]
        K0T = part(112, [CH, NT, P])
        sc = part(120, [CH, T])
        oT = fT
        wpa = part(64, [CH, D])
        wpb = part(80, [CH, D])
        wo = part(96, [KD, D])
        mT = part(176, [KD, T])
        x1 = part(128, [NT, D])
        yac = part(144, [NT, D])
        g1, b1 = part(160, [D]), part(164, [D])
        xin = [part(168, [D]), part(172, [D])]
        wq = part(0, [KD, 2048])
        keys = part(192, [2 * HEADS, P])
        ubuf = [part(64 + 4 * i, [D]) for i in range(NBUF)]
        vbuf = [part(96 + 4 * i, [D]) for i in range(NBUF)]
        diag = part(160, [K, P])
        x1c = [part(168, [D]), part(172, [D])]
        x1Tc = part(176, [KD, P])
        qs = part(180, [256])
        qTs = part(181, [2, P])
        srep = part(182, [P])
        cand = part(183, [K, K])
        crep = part(184, [K * K])
        eq = part(185, [2, K, K])
        v16 = part(187, [2, K])
        i16f = part(187.25, [2, K])
        taf = part(187.5, [2, K])
        e12 = part(187.75, [2, K])
        tv = part(188, [K])
        ex = part(188.25, [K])
        ga16 = part(188.5, [K])
        g2, b2 = part(64, [D]), part(68, [D])
        i16 = sb("i16", [P, 2, K], U32)
        ti = sb("ti", [P, K], U32)
        ta = sb("ta", [P, 2, K], U32)
        idxU = [sb(f"idxU{i}", [P, K], U32) for i in range(2)]
        idxV = [sb(f"idxV{i}", [P, K], U32) for i in range(2)]
        gates = [sb(f"gates{i}", [P, K]) for i in range(2)]
        acts = [sb(f"acts{i}", [P, K]) for i in range(2)]
        coef = [sb(f"coef{i}", [P, K]) for i in range(2)]
        nmax = sb("nmax", [P, 1])
        esum = sb("esum", [P, 1])
        erec = sb("erec", [P, 1])
        sq = sb("sq", [P, 3, P])
        ident, JT, mean = sq[:, 0, :], sq[:, 1, :], sq[:, 2, :]
        sgn2 = sb("sgn2", [P, 2])
        sgn, nsgn = sgn2[:, 0:1], sgn2[:, 1:2]
        iot = sb("iot", [P, K])
        masks = sb("masks", [P, LEVELS + 1, P], U8)
        eps = sb("eps", [P, 2])
        dsk = sb("dsk", [P, CH])
        bgl = sb("bgl", [P, CH])
        gnw = sb("gnw", [P, CH])
        lbl = sb("lbl", [P, 2, CH])
        lbs = sb("lbs", [P, 4, CH])
        lb, olb = lbs[:, 0, :], lbs[:, 1, :]
        cp = sb("cp", [P, 2, SCAN, G])
        state = part(96, [CH, P])
        stats = sb("stats", [P, 2, 6])
        mv = sb("mv", [P, 2])
        rstd = sb("rstd", [P, 2])
        PS = ctx.enter_context(nc.psum_tensor("PS", [P, 8, 512], F32))

        def sm(i):
            return small[:, G * i:G * (i + 1)]

        pw = small[:, G * 10:G * 10 + 2 * G * (L + 1)].rearrange("p (a g k) -> p a g k", a=2, g=G)
        prw, piw = pw[:, 0], pw[:, 1]

        s_cst = sem("s_cst"); s_msk = sem("s_msk"); s_par = sem("s_par"); s_xT = sem("s_xT")
        s_w = [sem(f"s_w{i}") for i in range(RING)]
        s_proj = sem("s_proj"); s_pev = sem("s_pev")
        s_dve = sem("s_dve")
        s_act = sem("s_act")
        s_dt = sem("s_dt"); s_ath = sem("s_ath"); s_trig = sem("s_trig")
        s_wnat = sem("s_wnat"); s_wtp = sem("s_wtp"); s_wev = sem("s_wev")
        s_wout = sem("s_wout"); s_kps = sem("s_kps"); s_kev = sem("s_kev")
        s_toe0 = sem("s_toe0"); s_toe = sem("s_toe"); s_uc = sem("s_uc")
        s_sin = sem("s_sin"); s_S = sem("s_S"); s_cp = sem("s_cp")
        s_js = sem("s_js"); s_t1 = sem("s_t1"); s_su = sem("s_su")
        s_y = sem("s_y"); s_yc = sem("s_yc"); s_yT = sem("s_yT"); s_yd = sem("s_yd"); s_yg = sem("s_yg")
        s_glu = sem("s_glu"); s_wg = sem("s_wg"); s_z = sem("s_z"); s_ya = sem("s_ya")
        s_lbe = sem("s_lbe"); s_f = sem("s_f"); s_lf = sem("s_lf"); s_b = sem("s_b");
        s_df = sem("s_df"); s_de = sem("s_de"); s_qk = sem("s_qk"); s_sp = sem("s_sp"); s_sc = sem("s_sc")
        s_k0p = sem("s_k0p"); s_k0e = sem("s_k0e"); s_o = sem("s_o"); s_kv = sem("s_kv"); s_st = sem("s_st")
        s_oe = sem("s_oe"); s_ms = sem("s_ms"); s_rt = sem("s_rt"); s_yb = sem("s_yb")
        s_wab = sem("s_wab"); s_wbb = sem("s_wbb"); s_wo = sem("s_wo")
        s_pa = sem("s_pa"); s_m = sem("s_m"); s_mix = sem("s_mix"); s_x1r = sem("s_x1r")
        s_ln = sem("s_ln"); s_xi = [sem(f"s_xi{i}") for i in range(2)]; s_lv = sem("s_lv"); s_ls = sem("s_ls")
        s_x1 = sem("s_x1"); s_y0 = sem("s_y0")
        s_wq = sem("s_wq"); s_key = sem("s_key")
        m_x1c = sem("m_x1c"); m_xp = sem("m_xp"); m_xe = sem("m_xe"); m_q = sem("m_q"); m_qe = sem("m_qe")
        m_qt = sem("m_qt"); m_qte = sem("m_qte"); m_s = sem("m_s"); m_tk = sem("m_tk")
        m_tv = sem("m_tv"); m_ex = sem("m_ex"); m_idx = sem("m_idx")
        m_gU = [sem(f"m_gU{i}") for i in range(NBUF)]
        m_gV = [sem(f"m_gV{i}") for i in range(NBUF)]
        m_dot = sem("m_dot"); m_ge = sem("m_ge"); m_co = sem("m_co"); m_dg = sem("m_dg")
        m_v = sem("m_v"); m_ya = sem("m_ya")
        s_ln2 = sem("s_ln2"); s_l2v = sem("s_l2v"); s_l2s = sem("s_l2s"); s_res = sem("s_res"); s_out = sem("s_out")

        N_PAR = 4 + 8 + 2 + 4
        N_CST = 4

        block = ctx.enter_context(nc.Block())

        def kp(w):
            return w.rearrange("(k p) n -> p k n", p=P)

        @block.sync
        def _(sp):
            for half in range(2):
                rows = slice(NS * half, NS * half + NS)
                sp.dma_start(sm(0)[rows, :], lam_re).then_inc(s_par, 16)
                sp.dma_start(sm(1)[rows, :], lam_im).then_inc(s_par, 16)
                sp.dma_start(X[rows], (b_re, b_im)[half]).then_inc(s_par, 16)
                sp.dma_start(Xs[rows], (b_im, b_re)[half]).then_inc(s_par, 16)
                sp.dma_start(CX[rows], (c_re, c_im)[half]).then_inc(s_par, 16)
                sp.dma_start(CXs[rows], (c_im, c_re)[half]).then_inc(s_par, 16)
            sp.dma_start(sm(2), log_step.partition_broadcast(P)).then_inc(s_par, 16)
            sp.dma_start(lbl[:, :, :], lb_logits).then_inc(s_par, 16)
            sp.dma_start(dsk[:, :], d_skip).then_inc(s_par, 16)
            sp.dma_start(bgl[:, :], b_glu).then_inc(s_par, 16)
            sp.dma_start(gnw[:, :], gnorm).then_inc(s_par, 16)
            sp.dma_start(sgn2[:, :], sign_consts).then_inc(s_par, 16)
            sp.dma_start(xTs, kp(xT)).then_inc(s_xT, 16)

            def load_chunk(c):
                if c >= RING:
                    sp.wait_ge(s_proj, 2 * (c - RING) + 2)
                col = CHUNK_COLS[c]
                sp.dma_start(ring[:, c % RING], kp(w_in[:, col:col + CHUNK])).then_inc(s_w[c % RING], 16)

            load_chunk(0)
            sp.dma_start(sq[:, :, :], square_consts).then_inc(s_cst, 16)
            sp.dma_start(iot[:, :], iota16).then_inc(s_cst, 16)
            sp.dma_start(masks_in, level_masks).then_inc(s_cst, 16)
            for c in range(1, len(CHUNK_COLS)):
                load_chunk(c)
            sp.wait_ge(s_su, 4 * SCAN)
            sp.dma_start(wglu, kp(w_glu)).then_inc(s_wg, 16)
            sp.wait_ge(s_glu, CH)
            sp.wait_ge(s_yT, 16 * 64)
            sp.dma_start(wpa, kp(w_pa)).then_inc(s_wab, 16)
            sp.wait_ge(s_proj, U_END)
            for k in range(4):
                sp.dma_start(wq[:, k], w_pq[k * P:(k + 1) * P, :]).then_inc(s_wq, 16)
            sp.wait_ge(s_o, CH * NT)
            sp.wait_ge(s_k0e, CH)
            sp.wait_ge(s_st, CH * (NT - 1))
            sp.dma_start(wpb, kp(w_pb)).then_inc(s_wbb, 16)
            sp.dma_start(wo, kp(w_o)).then_inc(s_wo, 16)
            sp.wait_ge(s_pa, 2 * KD)
            for k in range(4, KD):
                sp.dma_start(wq[:, k], w_pq[k * P:(k + 1) * P, :]).then_inc(s_wq, 16)
            sp.dma_start(keys, keysT).then_inc(s_key, 16)
            sp.wait_ge(s_m, KD)
            sp.dma_start(g1, ln1_g.partition_broadcast(P)).then_inc(s_ln, 16)
            sp.dma_start(b1, ln1_b.partition_broadcast(P)).then_inc(s_ln, 16)
            for i in range(NT):
                if i >= 2:
                    sp.wait_ge(s_x1r, 2 * (i - 1))
                sp.dma_start(xin[i % 2], x[i * P:(i + 1) * P, :]).then_inc(s_xi[i % 2], 16)
            sp.wait_ge(m_dot, K * BLOCKS)
            sp.dma_start(g2, ln2_g.partition_broadcast(P)).then_inc(s_ln2, 16)
            sp.dma_start(b2, ln2_b.partition_broadcast(P)).then_inc(s_ln2, 16)
            for i in range(NT):
                sp.wait_ge(s_res, i + 1)
                sp.dma_start(out[i * P:(i + 1) * P, :], yac[:, i]).then_inc(s_out, 16)
            sp.wait_ge(s_out, 16 * NT)

        @block.gpsimd
        def _(pool):
            pool.memset(eps[:, 0:1], LN_EPS).then_inc(s_cst, 8)
            pool.memset(eps[:, 1:2], RMS_EPS).then_inc(s_cst, 8)
            pool.memset(Toe, 0.0).then_inc(s_toe0, 1)
            pool.wait_ge(s_cst, 16 * N_CST)
            pool.tensor_copy(masks[:, :, :], masks_in).then_inc(s_msk, 1)
            pool.wait_ge(s_pev, U_S5 + 4)
            for j in range(8):
                for tau in range(L):
                    pool.dma_start(Uc[GH * tau:GH * tau + GH].rearrange("p (q j) c -> p j q c", j=8)[:, j],
                                   uT[GH * j:GH * j + GH, :, tau, :]).then_inc(s_uc, 16)
            pool.wait_ge(s_toe0, 1)
            pool.wait_ge(s_kev, 8)
            for tau in range(L):
                n = GH * (L - tau)
                pool.dma_start(Toe[GH * tau:GH * tau + GH, :, GH * tau:P], Ksb[0:GH, :, 0:n]).then_inc(s_toe, 16)
            for lv in range(SCAN):
                w = 1 << lv
                for j in range(4):
                    gs = slice(8 * j, 8 * j + 8)
                    if lv == 0:
                        pool.wait_ge(s_S, j + 1)
                        pool.wait_ge(s_cp, 1)
                    else:
                        pool.wait_ge(s_su, 4 * (lv - 1) + j + 1)
                    pool.tensor_tensor(scan1[:, gs, w:], S[:, gs, 0:NC - w],
                                       cp[:, 0, lv, gs].unsqueeze(2).to_broadcast([P, 8, NC - w]),
                                       ALU.mult).then_inc(s_t1, 1)
            pool.wait_ge(s_yc, 4)
            for j in range(8):
                for tau in range(L):
                    pool.dma_start(yT[GH * j:GH * j + GH, :, tau, :],
                                   Yc[GH * tau:GH * tau + GH].rearrange("p (q j) c -> p j q c", j=8)[:, j]
                                   ).then_inc(s_yT, 16)

            def until(s, value):
                pool.wait_ge(s, value)
                pool.nop(nofuse=True)

            def gather_u(n, par, k):
                if k == 0:
                    until(m_idx, n + 1)
                if not (isinstance(n, int) and n == 0 and k < NBUF):
                    until(m_dot, K * n + (k - NBUF + 1))
                pool.indirect_dma_start(ubuf[k % NBUF], None, peer_u,
                                        bass.IndirectOffsetOnAxis(idxU[par][:, k:k + 1], 0)
                                        ).then_inc(m_gU[k % NBUF], 16)

            def gather_v(n, par, k):
                if k == 0:
                    until(m_co, n + 1)
                if not (isinstance(n, int) and n == 0 and k < NBUF):
                    until(m_v, K * n + (k - NBUF + 1))
                pool.indirect_dma_start(vbuf[k % NBUF], None, peer_v,
                                        bass.IndirectOffsetOnAxis(idxV[par][:, k:k + 1], 0)
                                        ).then_inc(m_gV[k % NBUF], 16)

            def gathers(n, par, u=True, v=True):
                lead = 4
                for k in range(K + lead):
                    if u and k < K:
                        gather_u(n, par, k)
                    if v and k >= lead:
                        gather_v(n - 1, 1 - par, k - lead)

            pool.wait_ge(s_mix, 2 * NT)
            gathers(0, 0, v=False)
            gathers(1, 1)
            with pool.Fori(2, BLOCKS, 2) as n:
                gathers(n, 0)
                gathers(n + 1, 1)
            gathers(BLOCKS, 0, u=False)

        @block.scalar
        def _(act):
            count = [0]

            def chain(ins):
                count[0] += 1
                ins.then_inc(s_act, 1)
                act.wait_ge(s_act, count[0])

            act.wait_ge(s_par, 16 * N_PAR)
            act.activation(sm(3), sm(2), ACT.Exp).then_inc(s_dt, 1)
            act.wait_ge(s_lbe, 1)
            act.activation(lbs[:, 2:4, :], lbs[:, 2:4, :], ACT.Exp).then_inc(s_lbe, 1)
            act.wait_ge(s_ath, 1)
            act.activation(sm(6), sm(4), ACT.Exp).then_inc(s_trig, 1)
            act.wait_ge(s_ath, 2)
            act.activation(sm(7), sm(5), ACT.Sin, scale=0.5).then_inc(s_trig, 1)
            act.activation(sm(8), sm(5), ACT.Sin).then_inc(s_trig, 1)

            def unit(m):
                act.wait_ge(s_proj, m + 1)
                bank = PS[:, m % 2]
                if m < U_F:
                    act.activation(uT[:, m], bank.rearrange("p (c t) -> p t c", t=L), ACT.Copy).then_inc(s_pev, 1)
                elif m < U_Q:
                    act.activation(fT[:, m - U_F], bank, ACT.Sigmoid).then_inc(s_pev, 1)
                elif m < U_V:
                    act.activation(qT[:, m - U_Q], bank, ACT.Silu).then_inc(s_pev, 1)
                elif m < U_G:
                    c, th = (m - U_V) // 2, (m - U_V) % 2
                    act.activation(vS[:, 2 * th:2 * th + 2, CHUNK * c:CHUNK * c + CHUNK],
                                   bank.rearrange("p (a c) -> p a c", a=2), ACT.Copy).then_inc(s_pev, 1)
                elif m < U_GA:
                    act.activation(gT[:, m - U_G], bank, ACT.Silu).then_inc(s_pev, 1)
                elif m < U_GB:
                    if m == U_GA:
                        act.wait_ge(s_toe, 16 * L)
                    act.activation(sga[:, m - U_GA], bank, ACT.Sigmoid).then_inc(s_pev, 1)
                else:
                    if m == U_GB:
                        act.wait_ge(s_wout, 4)
                    act.activation(sgb[:, m - U_GB], bank, ACT.Sigmoid).then_inc(s_pev, 1)

            for m in range(U_S5, U_V):
                unit(m)
            for q in range(8):
                act.wait_ge(s_wtp, q + 1)
                act.activation(WinT[:, 4 * q:4 * q + 4, :], PS[:, 2 + q % 2].rearrange("p (a b) -> p a b", a=4),
                               ACT.Copy).then_inc(s_wev, 1)
            for q in range(8):
                act.wait_ge(s_kps, q + 1)
                act.activation(Ksb[0:GH, 4 * q:4 * q + 4, :],
                               PS[0:GH, 2 + q % 2].rearrange("p (a b) -> p a b", a=4), ACT.Copy).then_inc(s_kev, 1)
            for m in range(U_V, U_GA):
                unit(m)
            for j in range(4):
                act.wait_ge(s_sin, j + 1)
                act.activation(S[:, 8 * j:8 * j + 8, :], PS[:, 4 + j].rearrange("p (a b) -> p a b", a=8),
                               ACT.Copy).then_inc(s_S, 1)
            for m in range(U_GA, U_END):
                unit(m)
            for j in range(4):
                act.wait_ge(s_y, j + 1)
                act.activation(Yc[:, 8 * j:8 * j + 8, :], PS[:, 4 + j].rearrange("p (a b) -> p a b", a=8),
                               ACT.Copy).then_inc(s_yc, 1)
            act.wait_ge(s_f, 1)
            act.activation(fT, fT, ACT.Ln).then_inc(s_lf, 1)
            act.wait_ge(s_yd, 1)
            act.activation(yT, yT, ACT.Gelu_apprx_tanh).then_inc(s_yg, 1)
            for m in range(CH):
                act.wait_ge(s_glu, m + 1)
                act.activation(zT[:, m], PS[:, m].rearrange("p (t c) -> p t c", t=L), ACT.Sigmoid,
                               bias=bgl[:, m:m + 1]).then_inc(s_z, 1)
            for lv in range(LEVELS + 2):
                act.wait_ge(s_df, lv + 1)
                act.activation(dec[lv % 2], dec[lv % 2], ACT.Exp).then_inc(s_de, 1)
            for h in range(CH):
                act.wait_ge(s_k0p, h + 1)
                act.activation(K0T[:, h], PS[:, h].rearrange("p (a b) -> p a b", a=NT), ACT.Copy).then_inc(s_k0e, 1)
            act.wait_ge(s_st, CH * (NT - 1))
            for h in range(CH):
                act.wait_ge(s_o, CH * (NT - 1) + h + 1)
                act.activation(oT[:, h], PS[:, 4 + h], ACT.Copy).then_inc(s_oe, 1)
                act.activation(qT[:, h], PS[:, 4 + h], ACT.Square).then_inc(s_oe, 1)
            for h in range(CH):
                act.wait_ge(s_ms, h + 1)
                act.activation(qT[:, h], PS[:, h], ACT.Sqrt, bias=eps[:, 1:2]).then_inc(s_rt, 1)
            for i in range(NT):
                act.wait_ge(s_lv, i + 1)
                act.activation(rstd[:, 0:1], mv[:, 1:2], ACT.Sqrt, bias=eps[:, 0:1]).then_inc(s_ls, 1)
                act.wait_ge(s_x1, i + 1)
                act.activation(yac[:, i], x1[:, i], ACT.Copy, scale=ALPHA).then_inc(s_y0, 1)

            def prepare(n, par):
                if not (isinstance(n, int) and n < 2):
                    act.wait_ge(m_dot, K * (n - 1))
                    act.nop(nofuse=True)
                tile = n // HEADS
                src = x1[:, tile, :] if isinstance(n, int) else \
                    x1[:, bass.ds(tile, 1), :].rearrange("p a d -> p (a d)")
                act.activation(x1c[par], src, ACT.Copy).then_inc(m_x1c, 1)

            def prepare_rest(n):
                for h in range(2):
                    act.wait_ge(m_xp, 2 * n + h + 1)
                    act.activation(x1Tc[:, 4 * h:4 * h + 4], PS[:, h].rearrange("p (a b) -> p a b", a=4),
                                   ACT.Copy).then_inc(m_xe, 1)
                act.wait_ge(m_q, n + 1)
                act.activation(qs, PS[:, 2, 0:256], ACT.Copy).then_inc(m_qe, 1)
                act.wait_ge(m_qt, n + 1)
                act.activation(qTs, PS[:, 3, 0:256].rearrange("p (a b) -> p a b", a=2), ACT.Copy).then_inc(m_qte, 1)

            def softmax_exp(n):
                act.wait_ge(m_tv, n + 1)
                act.activation(ex, tv, ACT.Exp, bias=nmax[:, 0:1], accum_out=esum[:, 0:1]).then_inc(m_ex, 1)

            def diagonals(n, par):
                act.wait_ge(m_co, n + 1)
                if not (isinstance(n, int) and n == 0):
                    act.wait_ge(m_v, K * n)
                for k in range(K):
                    act.activation(diag[:, k], ident, ACT.Copy, scale=coef[par][:, k:k + 1]).then_inc(m_dg, 1)

            def gelu(n, par):
                act.wait_ge(m_dot, K * (n + 1))
                act.activation(ga16, acts[par][:, :], ACT.Gelu_apprx_tanh).then_inc(m_ge, 1)

            def step(n, par, first=False, last=False):
                if not last:
                    prepare(n + 1, 1 - par)
                if not first:
                    diagonals(n - 1, 1 - par)
                if not last:
                    prepare_rest(n + 1)
                    softmax_exp(n + 1)
                gelu(n, par)

            act.wait_ge(s_x1, NT)
            act.wait_ge(s_mix, 2 * NT)
            prepare(0, 0)
            prepare_rest(0)
            softmax_exp(0)
            step(0, 0, first=True)
            step(1, 1)
            with act.Fori(2, BLOCKS - 2, 2) as n:
                step(n, 0)
                step(n + 1, 1)
            step(BLOCKS - 2, 0)
            step(BLOCKS - 1, 1, last=True)
            diagonals(BLOCKS - 1, 1)
            for i in range(NT):
                act.wait_ge(s_l2v, i + 1)
                act.activation(rstd[:, 0:1], mv[:, 1:2], ACT.Sqrt, bias=eps[:, 0:1]).then_inc(s_l2s, 1)

        @block.tensor
        def _(pe):
            def unit(m):
                if m == 0:
                    pe.wait_ge(s_xT, 16)
                if m % 2 == 0:
                    c = m // 2
                    pe.wait_ge(s_w[c % RING], 16 * (c // RING + 1))
                if m >= 2:
                    pe.wait_ge(s_pev, m - 1)
                w = ring[:, (m // 2) % RING]
                if U_V <= m < U_G:
                    for a in range(2):
                        t = 2 * (m % 2) + a
                        for k in range(KD):
                            last = pe.matmul(PS[:, m % 2, CHUNK * a:CHUNK * a + CHUNK],
                                             xTs[:, k, t * P:(t + 1) * P], w[:, k], start=k == 0, stop=k == KD - 1)
                else:
                    for k in range(KD):
                        last = pe.matmul(PS[:, m % 2], w[:, k, (m % 2) * P:(m % 2 + 1) * P], xTs[:, k],
                                         start=k == 0, stop=k == KD - 1)
                last.then_inc(s_proj, 1)

            for m in range(U_S5, U_V):
                unit(m)
            pe.wait_ge(s_cst, 16 * N_CST)
            for q in range(8):
                pe.wait_ge(s_wnat, q // 2 + 1)
                if q >= 2:
                    pe.wait_ge(s_wev, q - 1)
                for a in range(4):
                    last = pe.transpose(PS[:, 2 + q % 2, a * P:(a + 1) * P],
                                        Wnat[q // 2 % 2][:, 4 * (q % 2) + a].rearrange("p l h -> p (l h)"), ident)
                last.then_inc(s_wtp, 1)
            pe.wait_ge(s_wout, 4)
            for q in range(8):
                pe.wait_ge(s_wev, min(8, 7 + q))
                if q >= 2:
                    pe.wait_ge(s_kev, q - 1)
                for a in range(4):
                    g = 4 * q + a
                    last = pe.matmul(PS[0:GH, 2 + q % 2, a * P:(a + 1) * P], BB[:, g, :],
                                     Wout[:, g, 0:L, :].rearrange("p l h -> p (l h)"), start=True, stop=True)
                last.then_inc(s_kps, 1)
            for m in range(U_V, U_GA):
                unit(m)
            pe.wait_ge(s_uc, 16 * 64)
            for g in range(G):
                last = pe.matmul(PS[:, 4 + g // 8, (g % 8) * NC:(g % 8 + 1) * NC], WinT[:, g], Uc[:, g],
                                 start=True, stop=True)
                if g % 8 == 7:
                    last.then_inc(s_sin, 1)
            fill = list(range(U_GA, U_END))
            for lv in range(SCAN):
                for j in range(4):
                    if lv == 0:
                        pe.wait_ge(s_S, j + 1)
                    else:
                        pe.wait_ge(s_su, 4 * (lv - 1) + j + 1)
                    pe.matmul(PS[:, 4 + j], JT, S[:, 8 * j:8 * j + 8, :], start=True, stop=True).then_inc(s_js, 1)
                for _ in range(3 if lv < SCAN - 1 else 1):
                    unit(fill.pop(0))
            pe.wait_ge(s_toe, 16 * L)
            for g in range(G):
                pe.wait_ge(s_su, 4 * (SCAN - 1) + g // 8 + 1)
                c0 = (g % 8) * NC
                pe.matmul(PS[:, 4 + g // 8, c0:c0 + NC], Toe[:, g], Uc[:, g], start=True, stop=False,
                          skip_group_check=True)
                last = pe.matmul(PS[:, 4 + g // 8, c0 + 1:c0 + NC],
                                 Wout[:, g, 1:L + 1, :].rearrange("p l h -> p (l h)"),
                                 S[:, g, 0:NC - 1], start=False, stop=True, skip_group_check=True)
                if g % 8 == 7:
                    last.then_inc(s_y, 1)
            pe.wait_ge(s_wg, 16)
            pe.wait_ge(s_yg, 1)
            pe.wait_ge(s_pev, U_END)
            for m in range(CH):
                for k in range(CH):
                    last = pe.matmul(PS[:, m], wglu[:, k, m * P:(m + 1) * P],
                                     yT[:, k].rearrange("p t c -> p (t c)"), start=k == 0, stop=k == CH - 1)
                last.then_inc(s_glu, 1)
            pe.wait_ge(s_yc, 4)
            for lv in range(LEVELS + 1):
                pe.wait_ge(s_qk, lv + 1)
                for h in range(CH):
                    if lv:
                        pe.wait_ge(s_sc, CH * (lv - 1) + h + 1)
                    for i in range(NT):
                        ts = slice(i * P, (i + 1) * P)
                        if lv < LEVELS:
                            lhs = rhs = dec[lv % 2][:, h, ts]
                        else:
                            lhs, rhs = kT[:, h, ts], qT[:, h, ts]
                        last = pe.matmul(PS[:, 4 + h, ts], lhs, rhs, start=True, stop=True)
                    last.then_inc(s_sp, 1)
            pe.wait_ge(s_qk, LEVELS + 3)
            pe.wait_ge(s_z, CH)
            for h in range(CH):
                for i in range(NT):
                    last = pe.transpose(PS[:, h, i * P:(i + 1) * P], dec[0][:, h, i * P:(i + 1) * P], ident)
                last.then_inc(s_k0p, 1)
            pe.wait_ge(s_sc, CH * (LEVELS + 1))
            pe.wait_ge(s_k0e, CH)
            for i in range(NT):
                ts = slice(i * P, (i + 1) * P)
                for h in range(CH):
                    hs = slice(h * P, (h + 1) * P)
                    if i:
                        pe.wait_ge(s_st, CH * (i - 1) + h + 1)
                        pe.matmul(PS[:, 4 + h, ts], state[:, h], dec[1][:, h, ts], start=True, stop=False)
                    pe.matmul(PS[:, 4 + h, ts], vS[:, i, hs], sc[:, h, ts], start=i == 0, stop=True
                              ).then_inc(s_o, 1)
                    if i < NT - 1:
                        pe.matmul(PS[:, h, 0:P], K0T[:, h, i], vS[:, i, hs], start=True, stop=True
                                  ).then_inc(s_kv, 1)
            for h in range(CH):
                pe.wait_ge(s_oe, 2 * h + 2)
                pe.matmul(PS[:, h], mean, qT[:, h], start=True, stop=True).then_inc(s_ms, 1)
            pe.wait_ge(s_wab, 16)
            pe.wait_ge(s_ya, CH)
            pe.wait_ge(s_oe, 2 * CH)
            pe.wait_ge(s_rt, CH)
            for j in range(KD):
                for a, (w, y) in enumerate(((wpa, yaT), (wpb, oT))):
                    if j == 0 and a == 1:
                        pe.wait_ge(s_wbb, 16)
                        pe.wait_ge(s_yb, CH)
                    if j >= 2:
                        pe.wait_ge(s_m, j - 1)
                    for k in range(CH):
                        last = pe.matmul(PS[:, 4 + 2 * (j % 2) + a], w[:, k, j * P:(j + 1) * P], y[:, k],
                                         start=k == 0, stop=k == CH - 1)
                    last.then_inc(s_pa, 1)
            pe.wait_ge(s_wo, 16)
            for i in range(NT):
                for e in range(2):
                    if i == 0 and e == 0:
                        pe.wait_ge(s_m, KD)
                    if i >= 2:
                        pe.wait_ge(s_x1r, 2 * (i - 2) + e + 1)
                    for k in range(KD):
                        last = pe.matmul(PS[:, 2 * (i % 2) + e], mT[:, k, i * P:(i + 1) * P],
                                         wo[:, k, 512 * e:512 * e + 512], start=k == 0, stop=k == KD - 1)
                    last.then_inc(s_mix, 1)

            def queries(n, par):
                pe.wait_ge(m_x1c, n + 1)
                for h in range(2):
                    if not (isinstance(n, int) and n == 0):
                        pe.wait_ge(m_xe, 2 * (n - 1) + h + 1)
                    for a in range(4):
                        c = (4 * h + a) * P
                        last = pe.transpose(PS[:, h, a * P:(a + 1) * P], x1c[par][:, c:c + P], ident)
                    last.then_inc(m_xp, 1)
                pe.wait_ge(m_xe, 2 * n + 2)
                if not (isinstance(n, int) and n == 0):
                    pe.wait_ge(m_tk, n)
                head = n % HEADS
                for k in range(KD):
                    cols = wq[:, k, bass.ds(head * 256, 256)]
                    last = pe.matmul(PS[:, 2, 0:256], x1Tc[:, k], cols, start=k == 0, stop=k == KD - 1)
                last.then_inc(m_q, 1)

            def queries_turned(n):
                pe.wait_ge(m_qe, n + 1)
                for a in range(2):
                    last = pe.transpose(PS[:, 3, a * P:(a + 1) * P], qs[:, a * P:(a + 1) * P], ident)
                last.then_inc(m_qt, 1)

            def scores(n):
                pe.wait_ge(m_qte, n + 1)
                head = n % HEADS
                for a in range(2):
                    ks = keys[:, bass.ds(head * 2 + a, 1), :].rearrange("p a n -> p (a n)")
                    last = pe.matmul(PS[:, 2, a * P:(a + 1) * P], qTs[:, a], ks, start=True, stop=True)
                last.then_inc(m_s, 1)

            def mix_values(n, par, ks):
                for k in ks:
                    if k == 0 and not (isinstance(n, int) and n < 2):
                        pe.wait_ge(m_ya, n - 1)
                    pe.wait_ge(m_dg, K * n + k + 1)
                    pe.wait_ge(m_gV[k % NBUF], 16 * (2 * n + k // NBUF + 1))
                    for e in range(2):
                        last = pe.matmul(PS[:, 4 + 2 * par + e], diag[:, k], vbuf[k % NBUF][:, 512 * e:512 * e + 512],
                                         start=k == 0, stop=k == K - 1)
                    last.then_inc(m_v, 1)

            def step(n, par, first=False, last=False):
                if not last:
                    queries(n + 1, 1 - par)
                if not first:
                    mix_values(n - 1, 1 - par, range(0, 2))
                if not last:
                    queries_turned(n + 1)
                if not first:
                    mix_values(n - 1, 1 - par, range(2, 4))
                if not last:
                    scores(n + 1)
                if not first:
                    mix_values(n - 1, 1 - par, range(4, K))

            pe.wait_ge(s_wq, 16 * KD)
            pe.wait_ge(s_key, 16)
            pe.wait_ge(s_x1r, 2 * NT)
            queries(0, 0)
            queries_turned(0)
            scores(0)
            step(0, 0, first=True)
            step(1, 1)
            with pe.Fori(2, BLOCKS - 2, 2) as n:
                step(n, 0)
                step(n + 1, 1)
            step(BLOCKS - 2, 0)
            step(BLOCKS - 1, 1, last=True)
            mix_values(BLOCKS - 1, 1, range(K))

        @block.vector
        def _(dve):
            count = [0]

            def chain(ins):
                count[0] += 1
                ins.then_inc(s_dve, 1)
                dve.wait_ge(s_dve, count[0])

            def tt(o, a, b, op):
                return dve.tensor_tensor(o, a, b, op)

            def cmul(outr, outi, ar, ai, br, bi, t):
                chain(tt(t, ar, br, ALU.mult))
                chain(tt(outr, ai, bi, ALU.mult))
                chain(tt(outr, t, outr, ALU.subtract))
                chain(tt(t, ar, bi, ALU.mult))
                chain(tt(outi, ai, br, ALU.mult))
                chain(tt(outi, t, outi, ALU.add))

            dve.wait_ge(s_par, 16 * N_PAR)
            chain(tt(lb, lbl[:, 0, :], lbl[:, 1, :], ALU.max))
            tt(lbs[:, 2, :], lbl[:, 0, :], lb, ALU.subtract)
            tt(lbs[:, 3, :], lbl[:, 1, :], lb, ALU.subtract).then_inc(s_lbe, 1)
            dve.wait_ge(s_dt, 1)
            tt(sm(4), sm(0), sm(3), ALU.mult).then_inc(s_ath, 1)
            chain(tt(sm(5), sm(1), sm(3), ALU.mult))
            chain(dve.tensor_scalar(sm(6 + 3), sm(5), 1.0 / (2 * np.pi), None, ALU.mult))
            chain(dve.tensor_scalar(sm(9), sm(9), ROUND, None, ALU.add))
            chain(dve.tensor_scalar(sm(9), sm(9), ROUND, None, ALU.subtract))
            for c in (TWO_PI_A, TWO_PI_B, TWO_PI_C):
                chain(dve.scalar_tensor_tensor(sm(5), sm(9), -c, sm(5), ALU.mult, ALU.add))
            dve.tensor_scalar(sm(5), sm(5), PI, -PI, ALU.min, ALU.max).then_inc(s_ath, 1)
            dve.wait_ge(s_lbe, 2)
            chain(tt(olb, lbs[:, 2, :], lbs[:, 3, :], ALU.add))
            chain(dve.reciprocal(olb, olb))
            chain(tt(lb, lbs[:, 2, :], olb, ALU.mult))
            chain(dve.tensor_scalar(olb, lb, -1.0, 1.0, ALU.mult, ALU.add))
            dve.wait_ge(s_trig, 3)
            chain(tt(sm(9), sm(7), sm(7), ALU.mult))
            chain(dve.tensor_scalar(sm(9), sm(9), -2.0, 1.0, ALU.mult, ALU.add))
            dve.memset(prw[:, :, 0], 1.0)
            dve.memset(piw[:, :, 0], 0.0)
            chain(tt(prw[:, :, 1], sm(6), sm(9), ALU.mult))
            chain(tt(piw[:, :, 1], sm(6), sm(8), ALU.mult))
            tt(sm(3), sm(0), sm(0), ALU.mult)
            chain(tt(sm(4), sm(1), sm(1), ALU.mult))
            chain(tt(sm(3), sm(3), sm(4), ALU.add))
            chain(dve.reciprocal(sm(3), sm(3)))
            chain(dve.tensor_scalar(sm(4), prw[:, :, 1], -1.0, None, ALU.add))
            tt(sm(5), sm(4), sm(0), ALU.mult)
            chain(tt(sm(6), piw[:, :, 1], sm(1), ALU.mult))
            chain(tt(sm(5), sm(5), sm(6), ALU.add))
            tt(sm(6), piw[:, :, 1], sm(0), ALU.mult)
            chain(tt(sm(7), sm(4), sm(1), ALU.mult))
            chain(tt(sm(6), sm(6), sm(7), ALU.subtract))
            tt(sm(5), sm(5), sm(3), ALU.mult)
            chain(tt(sm(6), sm(6), sm(3), ALU.mult))
            chain(dve.tensor_scalar(sm(6), sm(6), sgn, None, ALU.mult))
            wr = sm(5).unsqueeze(2).to_broadcast([P, G, GH])
            wi = sm(6).unsqueeze(2).to_broadcast([P, G, GH])
            tmp = Wnat[0].rearrange("p a l h -> p (a l h)")[:, 0:G * GH].rearrange("p (g h) -> p g h", g=G)
            chain(tt(BB, X, wr, ALU.mult))
            chain(tt(tmp, Xs, wi, ALU.mult))
            chain(tt(BB, BB, tmp, ALU.add))
            chain(tt(BBs, Xs, wr, ALU.mult))
            chain(tt(tmp, X, wi, ALU.mult))
            chain(tt(BBs, BBs, tmp, ALU.subtract))
            chain(dve.tensor_scalar(CX, CX, nsgn, None, ALU.mult))
            for lo, n in ((1, 1), (2, 2), (4, 4)):
                def power(a, k0, kn):
                    return a[:, :, k0:k0 + kn]
                t3 = Wnat[1].rearrange("p a l h -> p (a l h)")[:, 0:G * n].rearrange("p (g k) -> p g k", g=G)
                br = prw[:, :, lo:lo + 1].to_broadcast([P, G, n])
                bi = piw[:, :, lo:lo + 1].to_broadcast([P, G, n])
                cmul(power(prw, lo + 1, n), power(piw, lo + 1, n), power(prw, 1, n), power(piw, 1, n), br, bi, t3)
            dve.tensor_copy(cp[:, 0, 0, :], prw[:, :, L])
            chain(dve.tensor_copy(cp[:, 1, 0, :], piw[:, :, L]))
            for lv in range(1, SCAN):
                a, b = cp[:, 0, lv - 1, :], cp[:, 1, lv - 1, :]
                cmul(cp[:, 0, lv, :], cp[:, 1, lv, :], a, b, a, b, sm(7))
            dve.engine_nop().then_inc(s_cp, 1)
            for q in range(4):
                gs = slice(8 * q, 8 * q + 8)
                if q >= 2:
                    dve.wait_ge(s_wtp, 2 * (q - 1))
                wt = wtmp[:, :, 0:L, :]
                full = [P, 8, L, GH]
                prb = prw[:, gs, 0:L].unsqueeze(3).to_broadcast(full)
                pib = piw[:, gs, 0:L].unsqueeze(3).to_broadcast(full)
                bb = BB[:, gs, :].unsqueeze(2).to_broadcast(full)
                bbs = BBs[:, gs, :].unsqueeze(2).to_broadcast(full)
                rev = Wnat[q % 2]
                for k in range(L):
                    one = [P, 8, GH]
                    tt(rev[:, :, L - 1 - k, :], BB[:, gs, :], prw[:, gs, k].unsqueeze(2).to_broadcast(one), ALU.mult)
                    tt(wt[:, :, L - 1 - k, :], BBs[:, gs, :], piw[:, gs, k].unsqueeze(2).to_broadcast(one), ALU.mult)
                chain(dve.engine_nop())
                chain(dve.tensor_scalar(wt, wt, sgn, None, ALU.mult))
                chain(tt(rev, rev, wt, ALU.add))
                dve.engine_nop().then_inc(s_wnat, 1)
                for k in range(L + 1):
                    one = [P, 8, GH]
                    tt(Wout[:, gs, k, :], CX[:, gs, :], prw[:, gs, k].unsqueeze(2).to_broadcast(one), ALU.mult)
                    tt(wtmp[:, :, k, :], CXs[:, gs, :], piw[:, gs, k].unsqueeze(2).to_broadcast(one), ALU.mult)
                chain(dve.engine_nop())
                chain(tt(Wout[:, gs], Wout[:, gs], wtmp, ALU.subtract))
                dve.engine_nop().then_inc(s_wout, 1)

            dve.wait_ge(s_pev, U_Q)
            for h in range(CH):
                last = dve.tensor_scalar(fT[:, h], fT[:, h], olb[:, h:h + 1], lb[:, h:h + 1], ALU.mult, ALU.add)
            chain(last)
            for lv in range(SCAN):
                w = 1 << lv
                for j in range(4):
                    gs = slice(8 * j, 8 * j + 8)
                    js = PS[:, 4 + j].rearrange("p (a b) -> p a b", a=8)
                    dve.wait_ge(s_js, 4 * lv + j + 1)
                    chain(tt(scan2[:, gs, w:], js[:, :, 0:NC - w],
                             cp[:, 1, lv, gs].unsqueeze(2).to_broadcast([P, 8, NC - w]), ALU.mult))
                    dve.wait_ge(s_t1, 4 * lv + j + 1)
                    chain(tt(scan2[:, gs, w:], scan2[:, gs, w:], scan1[:, gs, w:], ALU.add))
                    tt(S[:, gs, w:], S[:, gs, w:], scan2[:, gs, w:], ALU.add).then_inc(s_su, 1)
            dve.wait_ge(s_y, 4)
            chain(dve.tensor_scalar(kT, fT, -1.0, 1.0, ALU.mult, ALU.add))
            dve.engine_nop().then_inc(s_f, 1)
            dve.memset(sc, 0.0)
            ones = dec[0][:, 0, 0:P]
            chain(dve.memset(ones, 1.0))
            dve.wait_ge(s_lf, 1)
            for h in range(CH):
                for i in range(NT):
                    ts = slice(i * P, (i + 1) * P)
                    last = dve.tensor_tensor_scan(bT[:, h, ts], ones, fT[:, h, ts], 0.0, ALU.mult, ALU.add)
            chain(last)
            dve.wait_ge(s_yT, 16 * 64)
            for m in range(CH):
                last = dve.scalar_tensor_tensor(yT[:, m].rearrange("p t c -> p (t c)"),
                                                uT[:, m].rearrange("p t c -> p (t c)"), dsk[:, m:m + 1],
                                                yT[:, m].rearrange("p t c -> p (t c)"), ALU.mult, ALU.add)
            last.then_inc(s_yd, 1)

            def level(lv):
                B = P >> (lv + 1)
                nb = CH * T // (2 * B)
                v = bT.rearrange("p h (n a b) -> p (h n) a b", a=2, b=B)
                o = dec[lv % 2].rearrange("p h (n a b) -> p (h n) a b", a=2, b=B)
                if lv >= 2:
                    dve.wait_ge(s_sp, CH * (lv - 1))
                ref = v[:, :, 0, B - 1:B].to_broadcast([P, nb, B])
                tt(o[:, :, 0, :], ref, v[:, :, 0, :], ALU.subtract)
                tt(o[:, :, 1, :], v[:, :, 1, :], ref, ALU.subtract).then_inc(s_df, 1)

            def keyed(lv):
                B = P >> (lv + 1)
                o = dec[lv % 2].rearrange("p h (n a b) -> p (h n) a b", a=2, b=B)
                q4 = qT.rearrange("p h (n a b) -> p (h n) a b", a=2, b=B)
                k4 = kT.rearrange("p h (n a b) -> p (h n) a b", a=2, b=B)
                dve.wait_ge(s_de, lv + 1)
                tt(o[:, :, 0, :], o[:, :, 0, :], k4[:, :, 0, :], ALU.mult)
                tt(o[:, :, 1, :], o[:, :, 1, :], q4[:, :, 1, :], ALU.mult).then_inc(s_qk, 1)

            def place(lv):
                for h in range(CH):
                    dve.wait_ge(s_sp, CH * lv + h + 1)
                    dve.copy_predicated(sc[:, h].rearrange("p (a b) -> p a b", a=NT),
                                        masks[:, lv, :].unsqueeze(1).to_broadcast([P, NT, P]),
                                        PS[:, 4 + h].rearrange("p (a b) -> p a b", a=NT)).then_inc(s_sc, 1)

            dve.wait_ge(s_msk, 1)
            level(0)
            level(1)
            keyed(0)
            for lv in range(LEVELS):
                if lv + 1 < LEVELS:
                    keyed(lv + 1)
                else:
                    dve.engine_nop().then_inc(s_qk, 1)
                place(lv)
                if lv + 2 < LEVELS:
                    level(lv + 2)
            for m in range(CH):
                dve.wait_ge(s_z, m + 1)
                tt(yaT[:, m].rearrange("p (c t) -> p t c", t=L), yT[:, m], zT[:, m], ALU.mult).then_inc(s_ya, 1)
            place(LEVELS)
            dve.wait_ge(s_sp, CH * (LEVELS + 1))
            chain(dve.tensor_copy(dec[1], bT))
            dve.engine_nop().then_inc(s_df, 1)
            b4 = bT.rearrange("p h (i t) -> p (h i) t", t=P)
            tt(dec[0].rearrange("p h (i t) -> p (h i) t", t=P), b4[:, :, P - 1:P].to_broadcast([P, CH * NT, P]),
               b4, ALU.subtract).then_inc(s_df, 1)
            dve.wait_ge(s_df, LEVELS + 2)
            dve.wait_ge(s_de, LEVELS + 1)
            chain(dve.tensor_copy(bT[:, 0, 0:CH * NT].rearrange("p (h i) -> p h i", h=CH),
                                  dec[1].rearrange("p h (i t) -> p h i t", t=P)[:, :, :, P - 1]))
            tt(dec[1], dec[1], qT, ALU.mult).then_inc(s_qk, 1)
            dve.wait_ge(s_de, LEVELS + 2)
            tt(dec[0], dec[0], kT, ALU.mult).then_inc(s_qk, 1)
            dve.wait_ge(s_k0p, CH)
            for i in range(NT - 1):
                for h in range(CH):
                    dve.wait_ge(s_kv, CH * i + h + 1)
                    if i == 0:
                        dve.tensor_copy(state[:, h], PS[:, h, 0:P]).then_inc(s_st, 1)
                    else:
                        dve.wait_ge(s_o, CH * i + h + 1)
                        dve.scalar_tensor_tensor(state[:, h], state[:, h], bT[:, 0, h * NT + i:h * NT + i + 1],
                                                 PS[:, h, 0:P], ALU.mult, ALU.add).then_inc(s_st, 1)
            for h in range(CH):
                dve.wait_ge(s_oe, 2 * h + 1)
                dve.wait_ge(s_rt, h + 1)
                chain(dve.tensor_scalar(gT[:, h], gT[:, h], gnw[:, h:h + 1], None, ALU.mult))
                chain(dve.reciprocal(qT[:, h], qT[:, h]))
                chain(tt(oT[:, h], oT[:, h], qT[:, h], ALU.mult))
                tt(oT[:, h], oT[:, h], gT[:, h], ALU.mult).then_inc(s_yb, 1)
            for j in range(KD):
                dve.wait_ge(s_pa, 2 * j + 2)
                pa, pb = PS[:, 4 + 2 * (j % 2)], PS[:, 4 + 2 * (j % 2) + 1]
                tt(sga[:, j], pa, sga[:, j], ALU.mult)
                chain(tt(sgb[:, j], pb, sgb[:, j], ALU.mult))
                tt(mT[:, j], sga[:, j], sgb[:, j], ALU.add).then_inc(s_m, 1)

            def norm(src, dst, g, b, vsem, ssem, i, done):
                for e in range(2):
                    dve.bn_stats(stats[:, e, :], src[:, 512 * e:512 * e + 512])
                chain(dve.engine_nop())
                dve.bn_aggr(mv[:, :], stats[:, :, :].rearrange("p a b -> p (a b)")).then_inc(vsem, 1)
                dve.wait_ge(ssem, i + 1)
                chain(dve.reciprocal(rstd[:, 1:2], rstd[:, 0:1]))
                chain(dve.tensor_scalar(dst, src, mv[:, 0:1], rstd[:, 1:2], ALU.subtract, ALU.mult))
                chain(tt(dst, dst, g, ALU.mult))
                tt(dst, dst, b, ALU.add).then_inc(done, 1)

            dve.wait_ge(s_ln, 32)
            for i in range(NT):
                dve.wait_ge(s_xi[i % 2], 16 * (i // 2 + 1))
                for e in range(2):
                    es = slice(512 * e, 512 * e + 512)
                    dve.wait_ge(s_mix, 2 * i + e + 1)
                    dve.scalar_tensor_tensor(x1[:, i, es], xin[i % 2][:, es], ALPHA, PS[:, 2 * (i % 2) + e],
                                             ALU.mult, ALU.add).then_inc(s_x1r, 1)
                dve.wait_ge(s_x1r, 2 * i + 2)
                norm(x1[:, i], x1[:, i], g1, b1, s_lv, s_ls, i, s_x1)
            dve.wait_ge(s_y0, NT)
            dve.wait_ge(s_cst, 16 * N_CST)
            base = count[0]
            STEPS = 20

            def top16(values, indices, source, scratch, flat, link):
                link(dve.max(values[:, 0:8], source))
                dve.max_index(indices[:, 0:8], values[:, 0:8], source)
                link(dve.match_replace(scratch, values[:, 0:8], source, LOW))
                link(dve.max(values[:, 8:16], scratch))
                link(dve.max_index(indices[:, 8:16], values[:, 8:16], scratch))

            def retrieve(n, par):
                at = [0]

                def link(ins):
                    at[0] += 1
                    ins.then_inc(s_dve, 1)
                    dve.wait_ge(s_dve, n * STEPS + base + at[0])
                    dve.nop(nofuse=True)

                dve.wait_ge(m_s, n + 1)
                dve.nop(nofuse=True)
                for a in range(2):
                    top16(v16[:, a], i16[:, a, :], PS[:, 2, a * P:(a + 1) * P], srep, None, link)
                dve.engine_nop().then_inc(m_tk, 1)
                link(tt(cand, v16[:, 0].unsqueeze(2).to_broadcast([P, K, K]),
                        v16[:, 1].unsqueeze(1).to_broadcast([P, K, K]), ALU.add))
                top16(tv, ti[:, :], cand.rearrange("p a b -> p (a b)"), crep, None, link)
                dve.tensor_scalar(nmax[:, :], tv[:, 0:1], -1.0, None, ALU.mult).then_inc(m_tv, 1)
                dve.tensor_copy(i16f, i16[:, :, :])
                dve.tensor_scalar(ta[:, 0, :], ti[:, :], 4, None, ALU.logical_shift_right)
                link(dve.tensor_scalar(ta[:, 1, :], ti[:, :], 15, None, ALU.bitwise_and))
                link(dve.tensor_copy(taf, ta[:, :, :]))
                full = [P, 2, K, K]
                link(tt(eq, taf.unsqueeze(3).to_broadcast(full),
                        iot[:, :].unsqueeze(1).unsqueeze(1).to_broadcast(full), ALU.is_equal))
                link(tt(eq, eq, i16f.unsqueeze(2).to_broadcast(full), ALU.mult))
                link(dve.tensor_reduce(e12, eq, AX_X, ALU.add))
                dve.scalar_tensor_tensor(idxU[par][:, :], e12[:, 0], float(P), e12[:, 1], ALU.mult, ALU.add
                                         ).then_inc(m_idx, 1)
                dve.wait_ge(m_ex, n + 1)
                link(dve.reciprocal(erec[:, :], esum[:, :]))
                link(dve.tensor_scalar(gates[par][:, :], ex, erec[:, 0:1], None, ALU.mult))
                assert at[0] == STEPS, at[0]

            def dots(n, par, ks):
                for k in ks:
                    dve.wait_ge(m_gU[k % NBUF], 16 * (2 * n + k // NBUF + 1))
                    dve.tensor_tensor_reduce(ubuf[k % NBUF], ubuf[k % NBUF], x1c[par], 1.0, 0.0, ALU.mult, ALU.add,
                                             acts[par][:, k:k + 1]).then_inc(m_dot, 1)

            def coefficients(n, par):
                if not (isinstance(n, int) and n < 2):
                    dve.wait_ge(m_v, K * (n - 1))
                dve.tensor_copy(idxV[par][:, :], idxU[par][:, :])
                dve.wait_ge(m_ge, n + 1)
                tt(coef[par][:, :], ga16, gates[par][:, :], ALU.mult).then_inc(m_co, 1)

            def add_values(n, par):
                dve.wait_ge(m_v, K * (n + 1))
                tile = n // HEADS
                row = yac[:, tile, :] if isinstance(n, int) else \
                    yac[:, bass.ds(tile, 1), :].rearrange("p a d -> p (a d)")
                tt(row, row, PS[:, 4 + 2 * par:6 + 2 * par].rearrange("p a b -> p (a b)"), ALU.add).then_inc(m_ya, 1)

            def step(n, par, first=False, last=False):
                dots(n, par, range(0, 8))
                if not last:
                    retrieve(n + 1, 1 - par)
                dots(n, par, range(8, K))
                if not first:
                    if not (isinstance(n, int) and n < 2):
                        dve.wait_ge(m_ya, n - 1)
                    pass
                coefficients(n, par)

            def adds(n, par):
                add_values(n, par)

            retrieve(0, 0)
            step(0, 0, first=True)
            step(1, 1)
            with dve.Fori(2, BLOCKS - 2, 2) as n:
                adds(n - 2, 0)
                step(n, 0)
                adds(n - 1, 1)
                step(n + 1, 1)
            adds(BLOCKS - 4, 0)
            step(BLOCKS - 2, 0)
            adds(BLOCKS - 3, 1)
            step(BLOCKS - 1, 1, last=True)
            adds(BLOCKS - 2, 0)
            dve.wait_ge(m_ya, BLOCKS - 1)
            adds(BLOCKS - 1, 1)
            dve.wait_ge(s_ln2, 32)
            dve.wait_ge(m_ya, BLOCKS)
            count[0] = base + STEPS * BLOCKS
            for i in range(NT):
                norm(yac[:, i], yac[:, i], g2, b2, s_l2v, s_l2s, i, s_res)


_CALL = ["x", "xT", "w_in", "lam_re", "lam_im", "b_re", "b_im", "c_re", "c_im", "d_skip", "log_step", "w_glu", "b_glu",
         "lb_logits", "gnorm", "w_pa", "w_pb", "w_o", "ln1_g", "ln1_b", "w_pq", "keysT", "peer_u", "peer_v",
         "ln2_g", "ln2_b", "square_consts", "sign_consts", "iota16", "level_masks"]


def shape_constants():
    i = np.arange(P)
    ident = np.eye(P, dtype=np.float32)
    jt = np.zeros((P, P), np.float32)
    jt[NS + np.arange(NS), np.arange(NS)] = -1.0
    jt[np.arange(NS), NS + np.arange(NS)] = 1.0
    mean = np.full((P, P), 1.0 / P, np.float32)
    square = np.stack([ident, jt, mean], axis=1)
    sign = np.where(i < NS, -1.0, 1.0).astype(np.float32)
    masks = np.zeros((P, LEVELS + 1, P), np.float32)
    s, t = i[:, None], i[None, :]
    for lv in range(LEVELS):
        b = P >> (lv + 1)
        masks[:, lv] = (s // (2 * b) == t // (2 * b)) & (s % (2 * b) < b) & (t % (2 * b) >= b)
    masks[:, LEVELS] = s == t
    return {"square_consts": square, "sign_consts": np.stack([sign, -sign], axis=1),
            "iota16": np.tile(np.arange(K, dtype=np.float32), (P, 1)), "level_masks": masks}


def kernel(**inputs):
    import concourse.bacc as bacc
    from concourse.bass_utils import run_bass_kernel_spmd as run

    a = {k: np.asarray(v) for k, v in inputs.items()}

    def columns(v):
        return v.reshape(CH, P).T

    data = {
        "x": a["x"][0], "xT": a["x"][0].T, "w_in": a["w_in"][0],
        "lam_re": a["s5_lam_re"][0].T, "lam_im": a["s5_lam_im"][0].T,
        "b_re": a["s5_b_re"][0].transpose(1, 0, 2), "b_im": a["s5_b_im"][0].transpose(1, 0, 2),
        "c_re": a["s5_c_re"][0].transpose(2, 0, 1), "c_im": a["s5_c_im"][0].transpose(2, 0, 1),
        "d_skip": columns(a["s5_d"][0]), "log_step": a["s5_log_step"][0],
        "w_glu": a["s5_w_glu"][0], "b_glu": columns(a["s5_b_glu"][0]),
        "lb_logits": a["hgrn_lb_logits"].reshape(2, CH, P).transpose(2, 0, 1),
        "gnorm": columns(a["hgrn_gnorm_w"][0]),
        "w_pa": a["w_pa"][0], "w_pb": a["w_pb"][0], "w_o": a["w_o"][0],
        "ln1_g": a["ln1_g"][0], "ln1_b": a["ln1_b"][0], "w_pq": a["peer_w_q"][0],
        "keysT": a["peer_sub_keys"][0].reshape(2 * HEADS, P, P).transpose(2, 0, 1),
        "peer_u": a["peer_u"][0], "peer_v": a["peer_v"][0], "ln2_g": a["ln2_g"][0], "ln2_b": a["ln2_b"][0],
        **shape_constants(),
    }
    nc = bacc.Bacc("TRN2", target_bir_lowering=False, num_devices=1)
    arrays, args = {}, []
    for name in _CALL:
        v = np.ascontiguousarray(data[name])
        arrays[f"in_{name}"] = v
        args.append(nc.dram_tensor(f"in_{name}", v.shape, mybir.dt.from_np(v.dtype), kind="ExternalInput").ap())
    args.append(nc.dram_tensor("out", (T, D), F32, kind="ExternalOutput").ap())
    hybrid_layer(nc, *args)
    r = run(nc, [arrays], core_ids=[0])
    return r.results[0]["out"].reshape(1, T, D)
```

```python
from contextlib import ExitStack

import numpy as np
import concourse.bass as bass
from concourse import mybir

ALU = mybir.AluOpType
ACT = mybir.ActivationFunctionType
F32 = mybir.dt.float32
U32 = mybir.dt.uint32
U8 = mybir.dt.uint8
AX_X = mybir.AxisListType.X

P = 128
T = 512
D = 1024
NT = T // P
KD = D // P
W2 = 512
CH = W2 // P
G, NS, GH, L = 32, 64, 16, 8
NC = T // L
SCAN = 6
LEVELS = 7
HEADS = 8
K = 16
BLOCKS = NT * HEADS
FILL_SCAN, FILL_Y, FILL_LEVEL, GLU_AT, LATE = (2, 2, 1, 1, 1, 1), 4, (2, 1, 1, 1, 1, 1, 1, 0), 2, 2
NBUF = 8
ALPHA = 2.0 ** 0.25
LN_EPS = 1e-5
RMS_EPS = 1e-6
LOW = -3.0e38
ROUND = 1.5 * 2.0 ** 23
TWO_PI_A, TWO_PI_B, TWO_PI_C = 6.28125, 1.93500518798828125e-3, 3.0199159819e-7
PI = 3.1415925

CHUNK = 256
RING = 4
U_S5, U_F, U_Q, U_V, U_G, U_GA, U_GB, U_END = 0, 4, 8, 12, 16, 20, 28, 36
COL = {"u": 0, "q": 512, "f": 1024, "v": 1536, "g": 2048, "ga": 2560, "gb": 3584}
CHUNK_COLS = [COL[n] + CHUNK * i for n, m in
              (("u", 2), ("f", 2), ("q", 2), ("v", 2), ("g", 2), ("ga", 4), ("gb", 4)) for i in range(m)]


def hybrid_layer(nc, x, xT, w_in, lam_re, lam_im, b_re, b_im, c_re, c_im, d_skip, log_step, w_glu, b_glu,
                 lb_logits, gnorm, w_pa, w_pb, w_o, ln1_g, ln1_b, w_pq, keysT, peer_u, peer_v, ln2_g, ln2_b,
                 square_consts, sign_consts, iota16, level_masks, out):
    with ExitStack() as ctx:
        def sb(name, shape, dt=F32):
            return ctx.enter_context(nc.sbuf_tensor(name, shape, dt))

        def sem(name):
            return ctx.enter_context(nc.semaphore(name))

        arena = sb("arena", [P, 200 * 256])

        def part(kb, shape):
            n = int(np.prod(shape))
            v = arena[:, int(kb * 256):int(kb * 256) + n]
            if len(shape) == 1:
                return v
            names = "abcd"[:len(shape)]
            return v.rearrange(f"p ({' '.join(names)}) -> p {' '.join(names)}", **dict(zip(names, shape)))

        ring = part(0, [RING, KD, CHUNK])
        qT, fT, vS, gT = (part(32 + 8 * i, [CH, T]) for i in range(4))
        xTs = part(128, [KD, T])
        sga = part(144, [KD, T])
        sgb = part(160, [KD, T])
        WinT = part(64, [G, P])
        Toe = part(80, [G, P])
        Wout = part(96, [G, L + 1, GH])
        Uc = part(114, [G, NC])
        wtmp = part(122, [8, L + 1, GH])
        Ksb = part(144, [G, P])
        X, Xs, CX, CXs, BB, BBs = (part(160 + 2 * i, [G, GH]) for i in range(6))
        small = part(172, [G * 32])
        Wnat = [part(176 + 4 * i, [8, L, GH]) for i in range(2)]
        wsum = part(192, [8, L, GH])
        uT = part(184, [CH, L, NC])
        S = part(176, [G, NC])
        scan1 = part(64, [G, NC])
        scan2 = part(72, [G, NC])
        Yc = part(64, [G, NC])
        wglu = part(72, [CH, W2])
        yT = part(176, [CH, L, NC])
        zT = part(184, [CH, L, NC])
        yaT = part(192, [CH, T])
        masks_in = part(60, [LEVELS + 1, P])
        rpw = part(196, [2, G, L])
        rpr, rpi = rpw[:, 0], rpw[:, 1]
        kT = part(80, [CH, T])
        bT = part(88, [CH, T])
        dec = [part(96, [CH, T]), part(104, [CH, T])]
        K0T = part(112, [CH, NT, P])
        sc = part(120, [CH, T])
        oT = fT
        wpa = part(64, [CH, D])
        wpb = part(80, [CH, D])
        wo = part(96, [KD, D])
        mT = part(64, [KD, T])
        x1 = part(128, [NT, D])
        yac = part(144, [NT, D])
        g1, b1 = part(160, [D]), part(164, [D])
        wq = part(0, [KD, 2048])
        keys = part(192, [2 * HEADS, P])
        ubuf = [part(64 + 4 * ((i + 4) % NBUF), [D]) for i in range(NBUF)]
        vbuf = [part(96 + 4 * i, [D]) for i in range(NBUF)]
        diag = part(160, [K, P])
        x1c = [part(168, [D]), part(172, [D])]
        x1Tc = part(176, [KD, P])
        qs = part(180, [256])
        qTs = part(181, [2, P])
        srep = part(182, [P])
        cand = part(183, [K, K])
        crep = part(184, [K * K])
        eq = part(185, [2, K, K])
        v16 = part(187, [2, K])
        i16f = part(187.25, [2, K])
        taf = part(187.5, [2, K])
        e12 = part(187.75, [2, K])
        tv = part(188, [K])
        ex = part(188.25, [K])
        ga16 = part(188.5, [K])
        g2, b2 = x1[:, 0], x1[:, 1]
        i16 = sb("i16", [P, 2, K], U32)
        ti = sb("ti", [P, K], U32)
        ta = sb("ta", [P, 2, K], U32)
        idxU = [sb(f"idxU{i}", [P, K], U32) for i in range(2)]
        idxV = [sb(f"idxV{i}", [P, K], U32) for i in range(2)]
        gates = [sb(f"gates{i}", [P, K]) for i in range(2)]
        acts = [sb(f"acts{i}", [P, K]) for i in range(2)]
        coef = [sb(f"coef{i}", [P, K]) for i in range(2)]
        nmax = sb("nmax", [P, 1])
        esum = sb("esum", [P, 1])
        erec = sb("erec", [P, 1])
        sq = sb("sq", [P, 3, P])
        ident, JT, mean = sq[:, 0, :], sq[:, 1, :], sq[:, 2, :]
        sgn2 = sb("sgn2", [P, 2])
        sgn, nsgn = sgn2[:, 0:1], sgn2[:, 1:2]
        iot = sb("iot", [P, K])
        masks = sb("masks", [P, LEVELS + 1, P], U8)
        eps = sb("eps", [P, 2])
        dsk = sb("dsk", [P, CH])
        bgl = sb("bgl", [P, CH])
        gnw = sb("gnw", [P, CH])
        lbl = sb("lbl", [P, 2, CH])
        lbs = sb("lbs", [P, 4, CH])
        lb, olb = lbs[:, 0, :], lbs[:, 1, :]
        cp = sb("cp", [P, 2, SCAN, G])
        state = part(96, [CH, P])
        stats = sb("stats", [P, 2, 6])
        mv = sb("mv", [P, 2])
        rstd = sb("rstd", [P, 2])
        PS = ctx.enter_context(nc.psum_tensor("PS", [P, 8, 512], F32))

        def sm(i):
            return small[:, G * i:G * (i + 1)]

        zU = nc.dram_tensor("zU", [CH, P, L, NC], F32, kind="Internal").ap()
        zY = nc.dram_tensor("zY", [CH, P, L, NC], F32, kind="Internal").ap()

        def by_step(z, tau):
            return z.rearrange("q (j h) t c -> h t (q j) c", h=GH)[:, tau]

        pw = small[:, G * 10:G * 10 + 2 * G * (L + 1)].rearrange("p (a g k) -> p a g k", a=2, g=G)
        prw, piw = pw[:, 0], pw[:, 1]

        s_cst = sem("s_cst"); s_msk = sem("s_msk"); s_par = sem("s_par"); s_xT = [sem(f"s_xT{i}") for i in range(4)]; s_zu = sem("s_zu"); s_zy = sem("s_zy"); s_pow = sem("s_pow"); s_pam = sem("s_pam")
        s_w = [sem(f"s_w{i}") for i in range(RING)]
        s_proj = sem("s_proj"); s_pev = sem("s_pev")
        s_dve = sem("s_dve")
        s_rtv = sem("s_rtv")
        s_act = sem("s_act")
        s_dt = sem("s_dt"); s_ath = sem("s_ath"); s_trig = sem("s_trig")
        s_wnat = sem("s_wnat"); s_wp = sem("s_wp"); s_wtp = sem("s_wtp"); s_wev = sem("s_wev")
        s_wout = sem("s_wout"); s_kps = sem("s_kps"); s_kev = sem("s_kev")
        s_toe0 = sem("s_toe0"); s_toe = sem("s_toe"); s_uc = sem("s_uc")
        s_sin = sem("s_sin"); s_S = sem("s_S"); s_cp = sem("s_cp")
        s_js = sem("s_js"); s_t1 = sem("s_t1"); s_su = sem("s_su")
        s_y = sem("s_y"); s_yc = sem("s_yc"); s_yT = sem("s_yT"); s_yd = sem("s_yd"); s_yg = sem("s_yg")
        s_glu = sem("s_glu"); s_wg = sem("s_wg"); s_z = sem("s_z"); s_ya = sem("s_ya")
        s_lbe = sem("s_lbe"); s_f = sem("s_f"); s_lf = sem("s_lf"); s_b = sem("s_b");
        s_df = sem("s_df"); s_de = sem("s_de"); s_qk = sem("s_qk"); s_sp = sem("s_sp"); s_sc = sem("s_sc")
        s_k0p = sem("s_k0p"); s_k0e = sem("s_k0e"); s_o = sem("s_o"); s_kv = sem("s_kv"); s_st = sem("s_st")
        s_oe = sem("s_oe"); s_ms = sem("s_ms"); s_rt = sem("s_rt"); s_yb = sem("s_yb")
        s_wab = sem("s_wab"); s_wbb = sem("s_wbb"); s_wo = sem("s_wo")
        s_pa = sem("s_pa"); s_pb = sem("s_pb"); s_m = sem("s_m"); s_mix = sem("s_mix"); s_x1r = sem("s_x1r")
        s_ln = sem("s_ln"); s_xi = [sem(f"s_xi{i}") for i in range(NT)]; s_lv = sem("s_lv"); s_ls = sem("s_ls")
        s_x1 = sem("s_x1"); s_y0 = sem("s_y0")
        s_wq = sem("s_wq"); s_key = sem("s_key")
        m_x1c = sem("m_x1c"); m_xp = sem("m_xp"); m_xe = sem("m_xe"); m_q = sem("m_q"); m_qe = sem("m_qe")
        m_qt = sem("m_qt"); m_qte = sem("m_qte"); m_s = sem("m_s"); m_tk = sem("m_tk")
        m_tv = sem("m_tv"); m_ex = sem("m_ex"); m_idx = sem("m_idx")
        m_gU = [sem(f"m_gU{i}") for i in range(NBUF)]
        m_gV = [sem(f"m_gV{i}") for i in range(NBUF)]
        m_dot = sem("m_dot"); m_ge = sem("m_ge"); m_co = sem("m_co"); m_dg = sem("m_dg")
        m_v = sem("m_v"); m_ya = sem("m_ya")
        s_ln2 = sem("s_ln2"); s_l2v = sem("s_l2v"); s_l2s = sem("s_l2s"); s_res = sem("s_res"); s_out = sem("s_out")

        N_PAR = 4 + 8 + 2 + 4
        N_CST = 4

        block = ctx.enter_context(nc.Block())

        def kp(w):
            return w.rearrange("(k p) n -> p k n", p=P)

        @block.sync
        def _(sp):
            def load_chunk(c):
                if c >= RING:
                    sp.wait_ge(s_proj, 2 * (c - RING) + 2)
                col = CHUNK_COLS[c]
                sp.dma_start(ring[:, c % RING], kp(w_in[:, col:col + CHUNK])).then_inc(s_w[c % RING], 16)

            load_chunk(0)
            for i in range(4):
                sp.dma_start(xTs[:, 2 * i:2 * i + 2], kp(xT)[:, 2 * i:2 * i + 2]).then_inc(s_xT[i], 16)
            load_chunk(1)
            sp.dma_start(sq[:, :, :], square_consts).then_inc(s_cst, 16)
            sp.dma_start(iot[:, :], iota16).then_inc(s_cst, 16)
            sp.dma_start(masks_in, level_masks).then_inc(s_cst, 16)
            for c in range(2, len(CHUNK_COLS)):
                load_chunk(c)
            sp.wait_ge(s_su, 4 * SCAN)
            sp.dma_start(wglu, kp(w_glu)).then_inc(s_wg, 16)
            sp.wait_ge(s_glu, CH)
            sp.dma_start(wpa, kp(w_pa)).then_inc(s_wab, 16)
            sp.wait_ge(s_o, CH * NT)
            sp.wait_ge(s_k0e, CH)
            sp.wait_ge(s_st, CH * (NT - 1))
            sp.dma_start(wpb, kp(w_pb)).then_inc(s_wbb, 16)
            sp.dma_start(wo, kp(w_o)).then_inc(s_wo, 16)
            sp.wait_ge(s_proj, U_END)
            sp.dma_start(keys, keysT).then_inc(s_key, 16)
            for k in range(4):
                sp.dma_start(wq[:, k], w_pq[k * P:(k + 1) * P, :]).then_inc(s_wq, 16)
            sp.wait_ge(s_m, KD)
            for i in range(NT):
                sp.dma_start(yac[:, i], x[i * P:(i + 1) * P, :]).then_inc(s_xi[i], 16)
            sp.dma_start(g1, ln1_g.partition_broadcast(P)).then_inc(s_ln, 16)
            sp.dma_start(b1, ln1_b.partition_broadcast(P)).then_inc(s_ln, 16)
            for k in range(4, KD):
                sp.dma_start(wq[:, k], w_pq[k * P:(k + 1) * P, :]).then_inc(s_wq, 16)
            sp.wait_ge(m_x1c, 2 * HEADS + 1)
            sp.dma_start(g2, ln2_g.partition_broadcast(P)).then_inc(s_ln2, 16)
            sp.dma_start(b2, ln2_b.partition_broadcast(P)).then_inc(s_ln2, 16)
            for i in range(NT):
                sp.wait_ge(s_res, i + 1)
                sp.dma_start(out[i * P:(i + 1) * P, :], yac[:, i]).then_inc(s_out, 16)
            sp.wait_ge(s_out, 16 * NT)

        @block.gpsimd
        def _(pool):
            pool.memset(eps[:, 0:1], LN_EPS).then_inc(s_cst, 8)
            pool.memset(eps[:, 1:2], RMS_EPS).then_inc(s_cst, 8)
            pool.memset(Toe, 0.0).then_inc(s_toe0, 1)
            pool.wait_ge(s_cst, 16 * N_CST)
            pool.tensor_copy(masks[:, :, :], masks_in).then_inc(s_msk, 1)
            for q in range(CH):
                pool.wait_ge(s_pev, U_S5 + q + 1)
                pool.dma_start(zU[q], uT[:, q]).then_inc(s_zu, 16)
            pool.wait_ge(s_zu, 16 * CH)
            for tau in range(L):
                pool.dma_start(Uc[GH * tau:GH * tau + GH], by_step(zU, tau)).then_inc(s_uc, 16)
            pool.wait_ge(s_pow, 1)
            for q in range(4):
                gs = slice(8 * q, 8 * q + 8)
                if q >= 2:
                    pool.wait_ge(s_wtp, 2 * (q - 1))
                full = [P, 8, L, GH]
                bb = BB[:, gs, :].unsqueeze(2).to_broadcast(full)
                bbs = BBs[:, gs, :].unsqueeze(2).to_broadcast(full)
                pool.tensor_tensor(Wnat[q % 2], bb, rpr[:, gs].unsqueeze(3).to_broadcast(full), ALU.mult
                                   ).then_inc(s_wp, 1)
                pool.tensor_tensor(wsum, bbs, rpi[:, gs].unsqueeze(3).to_broadcast(full), ALU.mult
                                   ).then_inc(s_wp, 1)
                pool.wait_ge(s_wp, 2 * q + 2)
                pool.tensor_tensor(Wnat[q % 2], Wnat[q % 2], wsum, ALU.add).then_inc(s_wnat, 1)
                pool.wait_ge(s_wnat, q + 1)
            pool.wait_ge(s_toe0, 1)
            pool.wait_ge(s_kev, 8)
            for tau in range(L):
                n = GH * (L - tau)
                pool.dma_start(Toe[GH * tau:GH * tau + GH, :, GH * tau:P], Ksb[0:GH, :, 0:n]).then_inc(s_toe, 16)
            for lv in range(SCAN):
                w = 1 << lv
                for j in range(4):
                    gs = slice(8 * j, 8 * j + 8)
                    if lv == 0:
                        pool.wait_ge(s_S, j + 1)
                        pool.wait_ge(s_cp, 1)
                    else:
                        pool.wait_ge(s_su, 4 * (lv - 1) + j + 1)
                    pool.tensor_tensor(scan1[:, gs, w:], S[:, gs, 0:NC - w],
                                       cp[:, 0, lv, gs].unsqueeze(2).to_broadcast([P, 8, NC - w]),
                                       ALU.mult).then_inc(s_t1, 1)
            pool.wait_ge(s_yc, 4)
            for tau in range(L):
                pool.dma_start(by_step(zY, tau), Yc[GH * tau:GH * tau + GH]).then_inc(s_zy, 16)
            pool.wait_ge(s_zy, 16 * L)
            pool.dma_start(yT, zY.rearrange("q p t c -> p q t c")).then_inc(s_yT, 16)

            def until(s, value):
                pool.wait_ge(s, value)
                pool.nop(nofuse=True)

            def gather_u(n, par, k):
                if k == 0:
                    until(m_idx, n + 1)
                if isinstance(n, int) and n == 0 and k == 4:
                    pool.wait_ge(s_mix, 2 * NT)
                if not (isinstance(n, int) and n == 0 and k < NBUF):
                    until(m_dot, K * n + (k - NBUF + 1))
                pool.indirect_dma_start(ubuf[k % NBUF], None, peer_u,
                                        bass.IndirectOffsetOnAxis(idxU[par][:, k:k + 1], 0)
                                        ).then_inc(m_gU[k % NBUF], 16)

            def gather_v(n, par, k):
                if k == 0:
                    until(m_co, n + 1)
                if not (isinstance(n, int) and n == 0 and k < NBUF):
                    until(m_v, K * n + (k - NBUF + 1))
                pool.indirect_dma_start(vbuf[k % NBUF], None, peer_v,
                                        bass.IndirectOffsetOnAxis(idxV[par][:, k:k + 1], 0)
                                        ).then_inc(m_gV[k % NBUF], 16)

            def gathers(n, par, u=True, v=True):
                lead = 4
                for k in range(K + lead):
                    if u and k < K:
                        gather_u(n, par, k)
                    if v and k >= lead:
                        gather_v(n - 1, 1 - par, k - lead)

            pool.wait_ge(s_m, KD)
            gathers(0, 0, v=False)
            gathers(1, 1)
            with pool.Fori(2, BLOCKS, 2) as n:
                gathers(n, 0)
                gathers(n + 1, 1)
            gathers(BLOCKS, 0, u=False)

        @block.scalar
        def _(act):
            count = [0]

            def chain(ins):
                count[0] += 1
                ins.then_inc(s_act, 1)
                act.wait_ge(s_act, count[0])

            for half in range(2):
                rows = slice(NS * half, NS * half + NS)
                act.dma_start(sm(0)[rows, :], lam_re).then_inc(s_par, 16)
                act.dma_start(sm(1)[rows, :], lam_im).then_inc(s_par, 16)
                act.dma_start(X[rows], (b_re, b_im)[half]).then_inc(s_par, 16)
                act.dma_start(Xs[rows], (b_im, b_re)[half]).then_inc(s_par, 16)
                act.dma_start(CX[rows], (c_re, c_im)[half]).then_inc(s_par, 16)
                act.dma_start(CXs[rows], (c_im, c_re)[half]).then_inc(s_par, 16)
            act.dma_start(sm(2), log_step.partition_broadcast(P)).then_inc(s_par, 16)
            act.dma_start(lbl[:, :, :], lb_logits).then_inc(s_par, 16)
            act.dma_start(dsk[:, :], d_skip).then_inc(s_par, 16)
            act.dma_start(bgl[:, :], b_glu).then_inc(s_par, 16)
            act.dma_start(gnw[:, :], gnorm).then_inc(s_par, 16)
            act.dma_start(sgn2[:, :], sign_consts).then_inc(s_par, 16)
            act.wait_ge(s_par, 16 * N_PAR)
            act.activation(sm(3), sm(2), ACT.Exp).then_inc(s_dt, 1)
            act.wait_ge(s_lbe, 1)
            act.activation(lbs[:, 2:4, :], lbs[:, 2:4, :], ACT.Exp).then_inc(s_lbe, 1)
            act.wait_ge(s_ath, 1)
            act.activation(sm(6), sm(4), ACT.Exp).then_inc(s_trig, 1)
            act.wait_ge(s_ath, 2)
            act.activation(sm(7), sm(5), ACT.Sin, scale=0.5).then_inc(s_trig, 1)
            act.activation(sm(8), sm(5), ACT.Sin).then_inc(s_trig, 1)

            def unit(m):
                act.wait_ge(s_proj, m + 1)
                bank = PS[:, m % 2]
                if m < U_F:
                    act.activation(uT[:, m], bank.rearrange("p (c t) -> p t c", t=L), ACT.Copy).then_inc(s_pev, 1)
                elif m < U_Q:
                    act.activation(fT[:, m - U_F], bank, ACT.Sigmoid).then_inc(s_pev, 1)
                elif m < U_V:
                    act.activation(qT[:, m - U_Q], bank, ACT.Silu).then_inc(s_pev, 1)
                elif m < U_G:
                    c, th = (m - U_V) // 2, (m - U_V) % 2
                    act.activation(vS[:, 2 * th:2 * th + 2, CHUNK * c:CHUNK * c + CHUNK],
                                   bank.rearrange("p (a c) -> p a c", a=2), ACT.Copy).then_inc(s_pev, 1)
                elif m < U_GA:
                    act.activation(gT[:, m - U_G], bank, ACT.Silu).then_inc(s_pev, 1)
                elif m < U_GB:
                    if m == U_GA:
                        act.wait_ge(s_toe, 16 * L)
                    act.activation(sga[:, m - U_GA], bank, ACT.Sigmoid).then_inc(s_pev, 1)
                else:
                    if m == U_GB:
                        act.wait_ge(s_wout, 4)
                    act.activation(sgb[:, m - U_GB], bank, ACT.Sigmoid).then_inc(s_pev, 1)

            for m in range(U_S5, U_V):
                unit(m)
            for q in range(8):
                act.wait_ge(s_wtp, q + 1)
                act.activation(WinT[:, 4 * q:4 * q + 4, :], PS[:, 2 + q % 2].rearrange("p (a b) -> p a b", a=4),
                               ACT.Copy).then_inc(s_wev, 1)
            for q in range(8):
                act.wait_ge(s_kps, q + 1)
                act.activation(Ksb[0:GH, 4 * q:4 * q + 4, :],
                               PS[0:GH, 2 + q % 2].rearrange("p (a b) -> p a b", a=4), ACT.Copy).then_inc(s_kev, 1)
            for j in range(4):
                act.wait_ge(s_sin, j + 1)
                act.activation(S[:, 8 * j:8 * j + 8, :], PS[:, 4 + j].rearrange("p (a b) -> p a b", a=8),
                               ACT.Copy).then_inc(s_S, 1)
            fill = list(range(U_V, U_END))

            def fill_in(n):
                for _ in range(n):
                    unit(fill.pop(0))

            fill_in(1 + sum(FILL_SCAN))
            for j in range(4):
                act.wait_ge(s_y, j + 1)
                act.activation(Yc[:, 8 * j:8 * j + 8, :], PS[:, 4 + j].rearrange("p (a b) -> p a b", a=8),
                               ACT.Copy).then_inc(s_yc, 1)
            act.wait_ge(s_f, 1)
            act.activation(fT, fT, ACT.Ln).then_inc(s_lf, 1)
            fill_in(FILL_Y)
            for lv in range(LEVELS + 1):
                if lv < LEVELS:
                    act.wait_ge(s_df, lv + 1)
                    act.activation(dec[lv % 2], dec[lv % 2], ACT.Exp).then_inc(s_de, 1)
                if lv >= 1:
                    fill_in(FILL_LEVEL[lv - 1])
                if lv == 0:
                    act.wait_ge(s_yd, 1)
                    act.activation(yT, yT, ACT.Gelu_apprx_tanh).then_inc(s_yg, 1)
                if lv - 1 == GLU_AT:
                    for m in range(CH):
                        act.wait_ge(s_glu, m + 1)
                        act.activation(zT[:, m], PS[:, 2 + m % 2].rearrange("p (t c) -> p t c", t=L), ACT.Sigmoid,
                                       bias=bgl[:, m:m + 1]).then_inc(s_z, 1)
            fill_in(len(fill) - LATE)
            for lv in (LEVELS, LEVELS + 1):
                act.wait_ge(s_df, lv + 1)
                act.activation(dec[lv % 2], dec[lv % 2], ACT.Exp).then_inc(s_de, 1)
            for h in range(CH):
                act.wait_ge(s_k0p, h + 1)
                act.activation(K0T[:, h], PS[:, 2 + h % 2].rearrange("p (a b) -> p a b", a=NT), ACT.Copy
                               ).then_inc(s_k0e, 1)
            for h in range(CH):
                act.wait_ge(s_o, CH * (NT - 1) + h + 1)
                act.activation(oT[:, h], PS[:, 4 + h], ACT.Copy).then_inc(s_oe, 1)
                act.activation(qT[:, h], PS[:, 4 + h], ACT.Square).then_inc(s_oe, 1)
            for h in range(CH):
                act.wait_ge(s_ms, h + 1)
                act.activation(qT[:, h], PS[:, 2 + h % 2], ACT.Sqrt, bias=eps[:, 1:2]).then_inc(s_rt, 1)
            fill_in(LATE)
            def first_norm(i):
                act.wait_ge(s_lv, i + 1)
                act.activation(rstd[:, 0:1], mv[:, 1:2], ACT.Sqrt, bias=eps[:, 0:1]).then_inc(s_ls, 1)
                act.wait_ge(s_x1, i + 1)
                act.activation(yac[:, i], x1[:, i], ACT.Copy, scale=ALPHA).then_inc(s_y0, 1)

            def last_norm(i):
                act.wait_ge(s_l2v, i + 1)
                act.activation(rstd[:, 0:1], mv[:, 1:2], ACT.Sqrt, bias=eps[:, 0:1]).then_inc(s_l2s, 1)

            def prepare(n, par):
                if not (isinstance(n, int) and n < 2):
                    act.wait_ge(m_dot, K * (n - 1))
                    act.nop(nofuse=True)
                tile = n // HEADS
                src = x1[:, tile, :] if isinstance(n, int) else \
                    x1[:, bass.ds(tile, 1), :].rearrange("p a d -> p (a d)")
                act.activation(x1c[par], src, ACT.Copy).then_inc(m_x1c, 1)

            def prepare_rest(n):
                for h in range(2):
                    act.wait_ge(m_xp, 2 * n + h + 1)
                    act.activation(x1Tc[:, 4 * h:4 * h + 4], PS[:, h].rearrange("p (a b) -> p a b", a=4),
                                   ACT.Copy).then_inc(m_xe, 1)
                act.wait_ge(m_q, n + 1)
                act.activation(qs, PS[:, 2, 0:256], ACT.Copy).then_inc(m_qe, 1)
                act.wait_ge(m_qt, n + 1)
                act.activation(qTs, PS[:, 3, 0:256].rearrange("p (a b) -> p a b", a=2), ACT.Copy).then_inc(m_qte, 1)

            def softmax_exp(n):
                act.wait_ge(m_tv, n + 1)
                act.activation(ex, tv, ACT.Exp, bias=nmax[:, 0:1], accum_out=esum[:, 0:1]).then_inc(m_ex, 1)

            def diagonals(n, par):
                act.wait_ge(m_co, n + 1)
                if not (isinstance(n, int) and n == 0):
                    act.wait_ge(m_v, K * n)
                for k in range(K):
                    act.activation(diag[:, k], ident, ACT.Copy, scale=coef[par][:, k:k + 1]).then_inc(m_dg, 1)

            def gelu(n, par):
                act.wait_ge(m_dot, K * (n + 1))
                act.activation(ga16, acts[par][:, :], ACT.Gelu_apprx_tanh).then_inc(m_ge, 1)

            def step(n, par, first=False, last=False):
                if not last:
                    prepare(n + 1, 1 - par)
                if not first:
                    diagonals(n - 1, 1 - par)
                if not last:
                    prepare_rest(n + 1)
                    softmax_exp(n + 1)
                gelu(n, par)

            first_norm(0)
            prepare(0, 0)
            first_norm(1)
            prepare_rest(0)
            softmax_exp(0)
            first_norm(2)
            first_norm(3)
            step(0, 0, first=True)
            step(1, 1)
            with act.Fori(2, BLOCKS - 2, 2) as n:
                step(n, 0)
                step(n + 1, 1)
            last_norm(0)
            last_norm(1)
            step(BLOCKS - 2, 0)
            last_norm(2)
            step(BLOCKS - 1, 1, last=True)
            diagonals(BLOCKS - 1, 1)
            last_norm(3)

        @block.tensor
        def _(pe):
            def unit(m):
                if m % 2 == 0:
                    c = m // 2
                    pe.wait_ge(s_w[c % RING], 16 * (c // RING + 1))
                if m >= 2:
                    pe.wait_ge(s_pev, m - 1)
                w = ring[:, (m // 2) % RING]
                if U_V <= m < U_G:
                    for a in range(2):
                        t = 2 * (m % 2) + a
                        for k in range(KD):
                            last = pe.matmul(PS[:, m % 2, CHUNK * a:CHUNK * a + CHUNK],
                                             xTs[:, k, t * P:(t + 1) * P], w[:, k], start=k == 0, stop=k == KD - 1)
                else:
                    for k in range(KD):
                        if m == 0 and k % 2 == 0:
                            pe.wait_ge(s_xT[k // 2], 16)
                        last = pe.matmul(PS[:, m % 2], w[:, k, (m % 2) * P:(m % 2 + 1) * P], xTs[:, k],
                                         start=k == 0, stop=k == KD - 1)
                last.then_inc(s_proj, 1)

            for m in range(U_S5, U_V):
                unit(m)
            pe.wait_ge(s_cst, 16 * N_CST)
            for q in range(8):
                pe.wait_ge(s_wnat, q // 2 + 1)
                if q >= 2:
                    pe.wait_ge(s_wev, q - 1)
                for a in range(4):
                    last = pe.transpose(PS[:, 2 + q % 2, a * P:(a + 1) * P],
                                        Wnat[q // 2 % 2][:, 4 * (q % 2) + a].rearrange("p l h -> p (l h)"), ident)
                last.then_inc(s_wtp, 1)
            pe.wait_ge(s_wout, 4)
            for q in range(8):
                pe.wait_ge(s_wev, min(8, 7 + q))
                if q >= 2:
                    pe.wait_ge(s_kev, q - 1)
                for a in range(4):
                    g = 4 * q + a
                    last = pe.matmul(PS[0:GH, 2 + q % 2, a * P:(a + 1) * P], BB[:, g, :],
                                     Wout[:, g, 0:L, :].rearrange("p l h -> p (l h)"), start=True, stop=True)
                last.then_inc(s_kps, 1)
            pe.wait_ge(s_uc, 16 * L)
            for g in range(G):
                last = pe.matmul(PS[:, 4 + g // 8, (g % 8) * NC:(g % 8 + 1) * NC], WinT[:, g], Uc[:, g],
                                 start=True, stop=True)
                if g % 8 == 7:
                    last.then_inc(s_sin, 1)
            fill = list(range(U_V, U_END))

            def fill_in(n):
                for _ in range(n):
                    unit(fill.pop(0))

            fill_in(1)
            for lv in range(SCAN):
                for j in range(4):
                    if lv == 0:
                        pe.wait_ge(s_S, j + 1)
                    else:
                        pe.wait_ge(s_su, 4 * (lv - 1) + j + 1)
                    pe.matmul(PS[:, 4 + j], JT, S[:, 8 * j:8 * j + 8, :], start=True, stop=True).then_inc(s_js, 1)
                fill_in(FILL_SCAN[lv])
            pe.wait_ge(s_toe, 16 * L)
            for g in range(G):
                pe.wait_ge(s_su, 4 * (SCAN - 1) + g // 8 + 1)
                c0 = (g % 8) * NC
                pe.matmul(PS[:, 4 + g // 8, c0:c0 + NC], Toe[:, g], Uc[:, g], start=True, stop=False,
                          skip_group_check=True)
                last = pe.matmul(PS[:, 4 + g // 8, c0 + 1:c0 + NC],
                                 Wout[:, g, 1:L + 1, :].rearrange("p l h -> p (l h)"),
                                 S[:, g, 0:NC - 1], start=False, stop=True, skip_group_check=True)
                if g % 8 == 7:
                    last.then_inc(s_y, 1)
            fill_in(FILL_Y)
            pe.wait_ge(s_yc, 4)

            def glu():
                pe.wait_ge(s_wg, 16)
                pe.wait_ge(s_yg, 1)
                for m in range(CH):
                    if m >= 2:
                        pe.wait_ge(s_z, m - 1)
                    for k in range(CH):
                        last = pe.matmul(PS[:, 2 + m % 2], wglu[:, k, m * P:(m + 1) * P],
                                         yT[:, k].rearrange("p t c -> p (t c)"), start=k == 0, stop=k == CH - 1)
                    last.then_inc(s_glu, 1)

            for lv in range(LEVELS + 1):
                pe.wait_ge(s_qk, lv + 1)
                for h in range(CH):
                    if lv:
                        pe.wait_ge(s_sc, CH * (lv - 1) + h + 1)
                    for i in range(NT):
                        ts = slice(i * P, (i + 1) * P)
                        if lv < LEVELS:
                            lhs = rhs = dec[lv % 2][:, h, ts]
                        else:
                            lhs, rhs = kT[:, h, ts], qT[:, h, ts]
                        last = pe.matmul(PS[:, 4 + h, ts], lhs, rhs, start=True, stop=True)
                    last.then_inc(s_sp, 1)
                fill_in(FILL_LEVEL[lv])
                if lv == GLU_AT:
                    glu()
            fill_in(len(fill) - LATE)

            def project(j, w, y, done):
                for k in range(CH):
                    last = pe.matmul(PS[:, j % 2], w[:, k, j * P:(j + 1) * P], y[:, k],
                                     start=k == 0, stop=k == CH - 1)
                last.then_inc(done, 1)

            def project_a(j):
                if j == 0:
                    pe.wait_ge(s_wab, 16)
                    pe.wait_ge(s_ya, CH)
                    pe.wait_ge(s_pev, U_END - LATE)
                if j >= 2:
                    pe.wait_ge(s_pam, j - 1)
                project(j, wpa, yaT, s_pa)

            project_a(0)
            pe.wait_ge(s_qk, LEVELS + 3)
            for h in range(CH):
                if h >= 2:
                    pe.wait_ge(s_k0e, h - 1)
                for i in range(NT):
                    last = pe.transpose(PS[:, 2 + h % 2, i * P:(i + 1) * P], dec[0][:, h, i * P:(i + 1) * P], ident)
                last.then_inc(s_k0p, 1)
            project_a(1)
            pe.wait_ge(s_sc, CH * (LEVELS + 1))
            pe.wait_ge(s_k0e, CH)
            for i in range(NT):
                ts = slice(i * P, (i + 1) * P)
                for h in range(CH):
                    hs = slice(h * P, (h + 1) * P)
                    if i:
                        pe.wait_ge(s_st, CH * (i - 1) + h + 1)
                        pe.matmul(PS[:, 4 + h, ts], state[:, h], dec[1][:, h, ts], start=True, stop=False)
                    pe.matmul(PS[:, 4 + h, ts], vS[:, i, hs], sc[:, h, ts], start=i == 0, stop=True
                              ).then_inc(s_o, 1)
                if i < NT - 1:
                    for h in range(CH):
                        hs = slice(h * P, (h + 1) * P)
                        last = pe.matmul(PS[:, 3, hs], K0T[:, h, i], vS[:, i, hs], start=True, stop=True)
                    last.then_inc(s_kv, 1)
                    project_a(2 + i)
            project_a(5)
            for h in range(CH):
                pe.wait_ge(s_oe, 2 * h + 2)
                if h >= 2:
                    pe.wait_ge(s_rt, h - 1)
                pe.matmul(PS[:, 2 + h % 2], mean, qT[:, h], start=True, stop=True).then_inc(s_ms, 1)
            project_a(6)
            project_a(7)
            pe.wait_ge(s_pam, KD)
            fill_in(LATE)
            pe.wait_ge(s_wbb, 16)
            pe.wait_ge(s_yb, CH)
            for j in range(KD):
                if j < 2:
                    pe.wait_ge(s_pev, U_END - 1 + j)
                else:
                    pe.wait_ge(s_m, j - 1)
                project(j, wpb, oT, s_pb)
            def out_project(i, e):
                if i >= 2:
                    pe.wait_ge(s_x1r, 2 * (i - 2) + e + 1)
                for k in range(KD):
                    last = pe.matmul(PS[:, 4 + 2 * (i % 2) + e], mT[:, k, i * P:(i + 1) * P],
                                     wo[:, k, 512 * e:512 * e + 512], start=k == 0, stop=k == KD - 1)
                last.then_inc(s_mix, 1)

            def rows_turned(n, par):
                pe.wait_ge(m_x1c, n + 1)
                for h in range(2):
                    if not (isinstance(n, int) and n == 0):
                        pe.wait_ge(m_xe, 2 * (n - 1) + h + 1)
                    for a in range(4):
                        c = (4 * h + a) * P
                        last = pe.transpose(PS[:, h, a * P:(a + 1) * P], x1c[par][:, c:c + P], ident)
                    last.then_inc(m_xp, 1)

            def queries(n):
                pe.wait_ge(m_xe, 2 * n + 2)
                if not (isinstance(n, int) and n == 0):
                    pe.wait_ge(m_tk, n)
                head = n % HEADS
                for k in range(KD):
                    cols = wq[:, k, bass.ds(head * 256, 256)]
                    last = pe.matmul(PS[:, 2, 0:256], x1Tc[:, k], cols, start=k == 0, stop=k == KD - 1)
                last.then_inc(m_q, 1)

            def queries_turned(n):
                pe.wait_ge(m_qe, n + 1)
                for a in range(2):
                    last = pe.transpose(PS[:, 3, a * P:(a + 1) * P], qs[:, a * P:(a + 1) * P], ident)
                last.then_inc(m_qt, 1)

            def scores(n):
                pe.wait_ge(m_qte, n + 1)
                head = n % HEADS
                for a in range(2):
                    ks = keys[:, bass.ds(head * 2 + a, 1), :].rearrange("p a n -> p (a n)")
                    last = pe.matmul(PS[:, 2, a * P:(a + 1) * P], qTs[:, a], ks, start=True, stop=True)
                last.then_inc(m_s, 1)

            def mix_values(n, par, ks):
                for k in ks:
                    if k == 0 and not (isinstance(n, int) and n < 2):
                        pe.wait_ge(m_ya, n - 1)
                    pe.wait_ge(m_dg, K * n + k + 1)
                    pe.wait_ge(m_gV[k % NBUF], 16 * (2 * n + k // NBUF + 1))
                    for e in range(2):
                        last = pe.matmul(PS[:, 4 + 2 * par + e], diag[:, k], vbuf[k % NBUF][:, 512 * e:512 * e + 512],
                                         start=k == 0, stop=k == K - 1)
                    last.then_inc(m_v, 1)

            def step(n, par, first=False, last=False):
                if not last:
                    rows_turned(n + 1, 1 - par)
                    queries(n + 1)
                if not first:
                    mix_values(n - 1, 1 - par, range(0, 2))
                if not last:
                    queries_turned(n + 1)
                if not first:
                    mix_values(n - 1, 1 - par, range(2, 4))
                if not last:
                    scores(n + 1)
                if not first:
                    mix_values(n - 1, 1 - par, range(4, K))

            pe.wait_ge(s_wo, 16)
            pe.wait_ge(s_oe, 2 * CH)
            pe.wait_ge(s_m, KD)
            for i in range(2):
                out_project(i, 0)
                out_project(i, 1)
            rows_turned(0, 0)
            out_project(2, 0)
            pe.wait_ge(s_wq, 16 * KD)
            queries(0)
            out_project(2, 1)
            queries_turned(0)
            out_project(3, 0)
            pe.wait_ge(s_key, 16)
            scores(0)
            out_project(3, 1)
            pe.wait_ge(s_x1r, 2 * NT)
            step(0, 0, first=True)
            step(1, 1)
            with pe.Fori(2, BLOCKS - 2, 2) as n:
                step(n, 0)
                step(n + 1, 1)
            step(BLOCKS - 2, 0)
            step(BLOCKS - 1, 1, last=True)
            mix_values(BLOCKS - 1, 1, range(K))

        @block.vector
        def _(dve):
            count = [0]

            def chain(ins):
                count[0] += 1
                ins.then_inc(s_dve, 1)
                dve.wait_ge(s_dve, count[0])

            def tt(o, a, b, op):
                return dve.tensor_tensor(o, a, b, op)

            def cmul(outr, outi, ar, ai, br, bi, t):
                chain(tt(t, ar, br, ALU.mult))
                chain(tt(outr, ai, bi, ALU.mult))
                chain(tt(outr, t, outr, ALU.subtract))
                chain(tt(t, ar, bi, ALU.mult))
                chain(tt(outi, ai, br, ALU.mult))
                chain(tt(outi, t, outi, ALU.add))

            dve.wait_ge(s_par, 16 * N_PAR)
            chain(tt(lb, lbl[:, 0, :], lbl[:, 1, :], ALU.max))
            tt(lbs[:, 2, :], lbl[:, 0, :], lb, ALU.subtract)
            tt(lbs[:, 3, :], lbl[:, 1, :], lb, ALU.subtract).then_inc(s_lbe, 1)
            dve.wait_ge(s_dt, 1)
            tt(sm(4), sm(0), sm(3), ALU.mult).then_inc(s_ath, 1)
            chain(tt(sm(5), sm(1), sm(3), ALU.mult))
            chain(dve.tensor_scalar(sm(6 + 3), sm(5), 1.0 / (2 * np.pi), None, ALU.mult))
            chain(dve.tensor_scalar(sm(9), sm(9), ROUND, None, ALU.add))
            chain(dve.tensor_scalar(sm(9), sm(9), ROUND, None, ALU.subtract))
            for c in (TWO_PI_A, TWO_PI_B, TWO_PI_C):
                chain(dve.scalar_tensor_tensor(sm(5), sm(9), -c, sm(5), ALU.mult, ALU.add))
            dve.tensor_scalar(sm(5), sm(5), PI, -PI, ALU.min, ALU.max).then_inc(s_ath, 1)
            dve.wait_ge(s_lbe, 2)
            chain(tt(olb, lbs[:, 2, :], lbs[:, 3, :], ALU.add))
            chain(dve.reciprocal(olb, olb))
            chain(tt(lb, lbs[:, 2, :], olb, ALU.mult))
            chain(dve.tensor_scalar(olb, lb, -1.0, 1.0, ALU.mult, ALU.add))
            dve.wait_ge(s_trig, 3)
            chain(tt(sm(9), sm(7), sm(7), ALU.mult))
            chain(dve.tensor_scalar(sm(9), sm(9), -2.0, 1.0, ALU.mult, ALU.add))
            dve.memset(prw[:, :, 0], 1.0)
            dve.memset(piw[:, :, 0], 0.0)
            chain(tt(prw[:, :, 1], sm(6), sm(9), ALU.mult))
            chain(tt(piw[:, :, 1], sm(6), sm(8), ALU.mult))
            tt(sm(3), sm(0), sm(0), ALU.mult)
            chain(tt(sm(4), sm(1), sm(1), ALU.mult))
            chain(tt(sm(3), sm(3), sm(4), ALU.add))
            chain(dve.reciprocal(sm(3), sm(3)))
            chain(dve.tensor_scalar(sm(4), prw[:, :, 1], -1.0, None, ALU.add))
            tt(sm(5), sm(4), sm(0), ALU.mult)
            chain(tt(sm(6), piw[:, :, 1], sm(1), ALU.mult))
            chain(tt(sm(5), sm(5), sm(6), ALU.add))
            tt(sm(6), piw[:, :, 1], sm(0), ALU.mult)
            chain(tt(sm(7), sm(4), sm(1), ALU.mult))
            chain(tt(sm(6), sm(6), sm(7), ALU.subtract))
            tt(sm(5), sm(5), sm(3), ALU.mult)
            chain(tt(sm(6), sm(6), sm(3), ALU.mult))
            chain(dve.tensor_scalar(sm(6), sm(6), sgn, None, ALU.mult))
            wr = sm(5).unsqueeze(2).to_broadcast([P, G, GH])
            wi = sm(6).unsqueeze(2).to_broadcast([P, G, GH])
            tmp = Wnat[0].rearrange("p a l h -> p (a l h)")[:, 0:G * GH].rearrange("p (g h) -> p g h", g=G)
            chain(tt(BB, X, wr, ALU.mult))
            chain(tt(tmp, Xs, wi, ALU.mult))
            chain(tt(BB, BB, tmp, ALU.add))
            chain(tt(BBs, Xs, wr, ALU.mult))
            chain(tt(tmp, X, wi, ALU.mult))
            chain(tt(BBs, BBs, tmp, ALU.subtract))
            chain(dve.tensor_scalar(CX, CX, nsgn, None, ALU.mult))
            for lo, n in ((1, 1), (2, 2), (4, 4)):
                def power(a, k0, kn):
                    return a[:, :, k0:k0 + kn]
                t3 = Wnat[1].rearrange("p a l h -> p (a l h)")[:, 0:G * n].rearrange("p (g k) -> p g k", g=G)
                br = prw[:, :, lo:lo + 1].to_broadcast([P, G, n])
                bi = piw[:, :, lo:lo + 1].to_broadcast([P, G, n])
                cmul(power(prw, lo + 1, n), power(piw, lo + 1, n), power(prw, 1, n), power(piw, 1, n), br, bi, t3)
            for k in range(L):
                dve.tensor_copy(rpr[:, :, L - 1 - k], prw[:, :, k])
                last = dve.tensor_scalar(rpi[:, :, L - 1 - k], piw[:, :, k], sgn, None, ALU.mult)
            chain(last)
            dve.engine_nop().then_inc(s_pow, 1)
            dve.tensor_copy(cp[:, 0, 0, :], prw[:, :, L])
            chain(dve.tensor_copy(cp[:, 1, 0, :], piw[:, :, L]))
            for lv in range(1, SCAN):
                a, b = cp[:, 0, lv - 1, :], cp[:, 1, lv - 1, :]
                cmul(cp[:, 0, lv, :], cp[:, 1, lv, :], a, b, a, b, sm(7))
            dve.engine_nop().then_inc(s_cp, 1)
            for q in range(4):
                gs = slice(8 * q, 8 * q + 8)
                full = [P, 8, L + 1, GH]
                chain(tt(Wout[:, gs], CX[:, gs, :].unsqueeze(2).to_broadcast(full),
                         prw[:, gs].unsqueeze(3).to_broadcast(full), ALU.mult))
                chain(tt(wtmp, CXs[:, gs, :].unsqueeze(2).to_broadcast(full),
                         piw[:, gs].unsqueeze(3).to_broadcast(full), ALU.mult))
                tt(Wout[:, gs], Wout[:, gs], wtmp, ALU.subtract).then_inc(s_wout, 1)

            dve.wait_ge(s_pev, U_Q)
            for h in range(CH):
                last = dve.tensor_scalar(fT[:, h], fT[:, h], olb[:, h:h + 1], lb[:, h:h + 1], ALU.mult, ALU.add)
            chain(last)
            for lv in range(SCAN):
                w = 1 << lv
                for j in range(4):
                    gs = slice(8 * j, 8 * j + 8)
                    js = PS[:, 4 + j].rearrange("p (a b) -> p a b", a=8)
                    dve.wait_ge(s_js, 4 * lv + j + 1)
                    chain(tt(scan2[:, gs, w:], js[:, :, 0:NC - w],
                             cp[:, 1, lv, gs].unsqueeze(2).to_broadcast([P, 8, NC - w]), ALU.mult))
                    dve.wait_ge(s_t1, 4 * lv + j + 1)
                    chain(tt(scan2[:, gs, w:], scan2[:, gs, w:], scan1[:, gs, w:], ALU.add))
                    tt(S[:, gs, w:], S[:, gs, w:], scan2[:, gs, w:], ALU.add).then_inc(s_su, 1)
            dve.wait_ge(s_y, 4)
            chain(dve.tensor_scalar(kT, fT, -1.0, 1.0, ALU.mult, ALU.add))
            dve.engine_nop().then_inc(s_f, 1)
            dve.memset(sc, 0.0)
            ones = dec[0][:, 0, 0:P]
            chain(dve.memset(ones, 1.0))
            dve.wait_ge(s_lf, 1)
            for h in range(CH):
                for i in range(NT):
                    ts = slice(i * P, (i + 1) * P)
                    last = dve.tensor_tensor_scan(bT[:, h, ts], ones, fT[:, h, ts], 0.0, ALU.mult, ALU.add)
            chain(last)
            dve.wait_ge(s_yT, 16)
            for m in range(CH):
                last = dve.scalar_tensor_tensor(yT[:, m].rearrange("p t c -> p (t c)"),
                                                uT[:, m].rearrange("p t c -> p (t c)"), dsk[:, m:m + 1],
                                                yT[:, m].rearrange("p t c -> p (t c)"), ALU.mult, ALU.add)
            last.then_inc(s_yd, 1)

            def level(lv):
                B = P >> (lv + 1)
                nb = CH * T // (2 * B)
                v = bT.rearrange("p h (n a b) -> p (h n) a b", a=2, b=B)
                o = dec[lv % 2].rearrange("p h (n a b) -> p (h n) a b", a=2, b=B)
                if lv >= 2:
                    dve.wait_ge(s_sp, CH * (lv - 1))
                ref = v[:, :, 0, B - 1:B].to_broadcast([P, nb, B])
                tt(o[:, :, 0, :], ref, v[:, :, 0, :], ALU.subtract)
                tt(o[:, :, 1, :], v[:, :, 1, :], ref, ALU.subtract).then_inc(s_df, 1)

            def keyed(lv):
                B = P >> (lv + 1)
                o = dec[lv % 2].rearrange("p h (n a b) -> p (h n) a b", a=2, b=B)
                q4 = qT.rearrange("p h (n a b) -> p (h n) a b", a=2, b=B)
                k4 = kT.rearrange("p h (n a b) -> p (h n) a b", a=2, b=B)
                dve.wait_ge(s_de, lv + 1)
                tt(o[:, :, 0, :], o[:, :, 0, :], k4[:, :, 0, :], ALU.mult)
                tt(o[:, :, 1, :], o[:, :, 1, :], q4[:, :, 1, :], ALU.mult).then_inc(s_qk, 1)

            def place(lv):
                for h in range(CH):
                    dve.wait_ge(s_sp, CH * lv + h + 1)
                    dve.copy_predicated(sc[:, h].rearrange("p (a b) -> p a b", a=NT),
                                        masks[:, lv, :].unsqueeze(1).to_broadcast([P, NT, P]),
                                        PS[:, 4 + h].rearrange("p (a b) -> p a b", a=NT)).then_inc(s_sc, 1)

            dve.wait_ge(s_msk, 1)
            level(0)
            level(1)
            keyed(0)
            for lv in range(LEVELS):
                if lv + 1 < LEVELS:
                    keyed(lv + 1)
                else:
                    dve.engine_nop().then_inc(s_qk, 1)
                place(lv)
                if lv + 2 < LEVELS:
                    level(lv + 2)
                if lv == GLU_AT + 1:
                    for m in range(CH):
                        dve.wait_ge(s_z, m + 1)
                        tt(yaT[:, m].rearrange("p (c t) -> p t c", t=L), yT[:, m], zT[:, m], ALU.mult
                           ).then_inc(s_ya, 1)
            place(LEVELS)
            dve.wait_ge(s_sp, CH * (LEVELS + 1))
            chain(dve.tensor_copy(dec[1], bT))
            dve.engine_nop().then_inc(s_df, 1)
            b4 = bT.rearrange("p h (i t) -> p (h i) t", t=P)
            tt(dec[0].rearrange("p h (i t) -> p (h i) t", t=P), b4[:, :, P - 1:P].to_broadcast([P, CH * NT, P]),
               b4, ALU.subtract).then_inc(s_df, 1)
            dve.wait_ge(s_df, LEVELS + 2)
            dve.wait_ge(s_de, LEVELS + 1)
            chain(dve.tensor_copy(bT[:, 0, 0:CH * NT].rearrange("p (h i) -> p h i", h=CH),
                                  dec[1].rearrange("p h (i t) -> p h i t", t=P)[:, :, :, P - 1]))
            tt(dec[1], dec[1], qT, ALU.mult).then_inc(s_qk, 1)
            dve.wait_ge(s_de, LEVELS + 2)
            tt(dec[0], dec[0], kT, ALU.mult).then_inc(s_qk, 1)
            def gate_a(j):
                dve.wait_ge(s_pa, j + 1)
                tt(sga[:, j], PS[:, j % 2], sga[:, j], ALU.mult).then_inc(s_pam, 1)

            gate_a(0)
            gate_a(1)
            dve.wait_ge(s_k0p, CH)
            for i in range(NT - 1):
                for h in range(CH):
                    kv = PS[:, 3, h * P:(h + 1) * P]
                    dve.wait_ge(s_kv, i + 1)
                    if i == 0:
                        dve.tensor_copy(state[:, h], kv).then_inc(s_st, 1)
                    else:
                        dve.wait_ge(s_o, CH * i + h + 1)
                        dve.scalar_tensor_tensor(state[:, h], state[:, h], bT[:, 0, h * NT + i:h * NT + i + 1],
                                                 kv, ALU.mult, ALU.add).then_inc(s_st, 1)
                gate_a(2 + i)
            gate_a(5)
            for h in range(CH):
                last = dve.tensor_scalar(gT[:, h], gT[:, h], gnw[:, h:h + 1], None, ALU.mult)
            chain(last)
            for h in range(CH):
                if h < 2:
                    gate_a(6 + h)
                dve.wait_ge(s_oe, 2 * h + 1)
                dve.wait_ge(s_rt, h + 1)
                chain(dve.reciprocal(qT[:, h], qT[:, h]))
                chain(tt(oT[:, h], oT[:, h], qT[:, h], ALU.mult))
                tt(oT[:, h], oT[:, h], gT[:, h], ALU.mult).then_inc(s_yb, 1)
            for j in range(KD):
                dve.wait_ge(s_pb, j + 1)
                chain(tt(sgb[:, j], PS[:, j % 2], sgb[:, j], ALU.mult))
                tt(mT[:, j], sga[:, j], sgb[:, j], ALU.add).then_inc(s_m, 1)

            def norm(src, dst, g, b, vsem, ssem, i, done):
                for e in range(2):
                    dve.bn_stats(stats[:, e, :], src[:, 512 * e:512 * e + 512])
                chain(dve.engine_nop())
                dve.bn_aggr(mv[:, :], stats[:, :, :].rearrange("p a b -> p (a b)")).then_inc(vsem, 1)
                dve.wait_ge(ssem, i + 1)
                chain(dve.reciprocal(rstd[:, 1:2], rstd[:, 0:1]))
                chain(dve.tensor_scalar(dst, src, mv[:, 0:1], rstd[:, 1:2], ALU.subtract, ALU.mult))
                chain(tt(dst, dst, g, ALU.mult))
                tt(dst, dst, b, ALU.add).then_inc(done, 1)

            def first_norm(i):
                dve.wait_ge(s_xi[i], 16)
                for e in range(2):
                    es = slice(512 * e, 512 * e + 512)
                    dve.wait_ge(s_mix, 2 * i + e + 1)
                    dve.scalar_tensor_tensor(x1[:, i, es], yac[:, i, es], ALPHA, PS[:, 4 + 2 * (i % 2) + e],
                                             ALU.mult, ALU.add).then_inc(s_x1r, 1)
                dve.wait_ge(s_x1r, 2 * i + 2)
                norm(x1[:, i], x1[:, i], g1, b1, s_lv, s_ls, i, s_x1)
            dve.wait_ge(s_ln, 32)
            dve.wait_ge(s_cst, 16 * N_CST)
            first_norm(0)
            first_norm(1)
            STEPS = 20

            def top16(values, indices, source, scratch, flat, link):
                link(dve.max(values[:, 0:8], source))
                dve.max_index(indices[:, 0:8], values[:, 0:8], source)
                link(dve.match_replace(scratch, values[:, 0:8], source, LOW))
                link(dve.max(values[:, 8:16], scratch))
                link(dve.max_index(indices[:, 8:16], values[:, 8:16], scratch))

            def retrieve(n, par):
                at = [0]

                def link(ins):
                    at[0] += 1
                    ins.then_inc(s_rtv, 1)
                    dve.wait_ge(s_rtv, n * STEPS + at[0])
                    dve.nop(nofuse=True)

                dve.wait_ge(m_s, n + 1)
                dve.nop(nofuse=True)
                for a in range(2):
                    top16(v16[:, a], i16[:, a, :], PS[:, 2, a * P:(a + 1) * P], srep, None, link)
                dve.engine_nop().then_inc(m_tk, 1)
                link(tt(cand, v16[:, 0].unsqueeze(2).to_broadcast([P, K, K]),
                        v16[:, 1].unsqueeze(1).to_broadcast([P, K, K]), ALU.add))
                top16(tv, ti[:, :], cand.rearrange("p a b -> p (a b)"), crep, None, link)
                dve.tensor_scalar(nmax[:, :], tv[:, 0:1], -1.0, None, ALU.mult).then_inc(m_tv, 1)
                dve.tensor_copy(i16f, i16[:, :, :])
                dve.tensor_scalar(ta[:, 0, :], ti[:, :], 4, None, ALU.logical_shift_right)
                link(dve.tensor_scalar(ta[:, 1, :], ti[:, :], 15, None, ALU.bitwise_and))
                link(dve.tensor_copy(taf, ta[:, :, :]))
                full = [P, 2, K, K]
                link(tt(eq, taf.unsqueeze(3).to_broadcast(full),
                        iot[:, :].unsqueeze(1).unsqueeze(1).to_broadcast(full), ALU.is_equal))
                link(tt(eq, eq, i16f.unsqueeze(2).to_broadcast(full), ALU.mult))
                link(dve.tensor_reduce(e12, eq, AX_X, ALU.add))
                dve.scalar_tensor_tensor(idxU[par][:, :], e12[:, 0], float(P), e12[:, 1], ALU.mult, ALU.add
                                         ).then_inc(m_idx, 1)
                dve.wait_ge(m_ex, n + 1)
                link(dve.reciprocal(erec[:, :], esum[:, :]))
                link(dve.tensor_scalar(gates[par][:, :], ex, erec[:, 0:1], None, ALU.mult))
                assert at[0] == STEPS, at[0]

            def dots(n, par, ks):
                for k in ks:
                    dve.wait_ge(m_gU[k % NBUF], 16 * (2 * n + k // NBUF + 1))
                    dve.tensor_tensor_reduce(ubuf[k % NBUF], ubuf[k % NBUF], x1c[par], 1.0, 0.0, ALU.mult, ALU.add,
                                             acts[par][:, k:k + 1]).then_inc(m_dot, 1)

            def coefficients(n, par):
                if not (isinstance(n, int) and n < 2):
                    dve.wait_ge(m_v, K * (n - 1))
                dve.tensor_copy(idxV[par][:, :], idxU[par][:, :])
                dve.wait_ge(m_ge, n + 1)
                tt(coef[par][:, :], ga16, gates[par][:, :], ALU.mult).then_inc(m_co, 1)

            def add_values(n, par):
                dve.wait_ge(m_v, K * (n + 1))
                tile = n // HEADS
                row = yac[:, tile, :] if isinstance(n, int) else \
                    yac[:, bass.ds(tile, 1), :].rearrange("p a d -> p (a d)")
                tt(row, row, PS[:, 4 + 2 * par:6 + 2 * par].rearrange("p a b -> p (a b)"), ALU.add).then_inc(m_ya, 1)

            def step(n, par, first=False, last=False):
                dots(n, par, range(0, 8))
                if not last:
                    retrieve(n + 1, 1 - par)
                dots(n, par, range(8, K))
                if not first:
                    if not (isinstance(n, int) and n < 2):
                        dve.wait_ge(m_ya, n - 1)
                    pass
                coefficients(n, par)

            def adds(n, par):
                add_values(n, par)

            retrieve(0, 0)
            first_norm(2)
            first_norm(3)
            dve.wait_ge(s_y0, NT)
            step(0, 0, first=True)
            step(1, 1)
            with dve.Fori(2, BLOCKS - 2, 2) as n:
                adds(n - 2, 0)
                step(n, 0)
                adds(n - 1, 1)
                step(n + 1, 1)
            def last_norm(i):
                norm(yac[:, i], yac[:, i], g2, b2, s_l2v, s_l2s, i, s_res)

            adds(BLOCKS - 4, 0)
            dve.wait_ge(s_ln2, 32)
            last_norm(0)
            last_norm(1)
            step(BLOCKS - 2, 0)
            adds(BLOCKS - 3, 1)
            last_norm(2)
            step(BLOCKS - 1, 1, last=True)
            adds(BLOCKS - 2, 0)
            dve.wait_ge(m_ya, BLOCKS - 1)
            adds(BLOCKS - 1, 1)
            dve.wait_ge(m_ya, BLOCKS)
            last_norm(3)


_CALL = ["x", "xT", "w_in", "lam_re", "lam_im", "b_re", "b_im", "c_re", "c_im", "d_skip", "log_step", "w_glu", "b_glu",
         "lb_logits", "gnorm", "w_pa", "w_pb", "w_o", "ln1_g", "ln1_b", "w_pq", "keysT", "peer_u", "peer_v",
         "ln2_g", "ln2_b", "square_consts", "sign_consts", "iota16", "level_masks"]


def shape_constants():
    i = np.arange(P)
    ident = np.eye(P, dtype=np.float32)
    jt = np.zeros((P, P), np.float32)
    jt[NS + np.arange(NS), np.arange(NS)] = -1.0
    jt[np.arange(NS), NS + np.arange(NS)] = 1.0
    mean = np.full((P, P), 1.0 / P, np.float32)
    square = np.stack([ident, jt, mean], axis=1)
    sign = np.where(i < NS, -1.0, 1.0).astype(np.float32)
    masks = np.zeros((P, LEVELS + 1, P), np.float32)
    s, t = i[:, None], i[None, :]
    for lv in range(LEVELS):
        b = P >> (lv + 1)
        masks[:, lv] = (s // (2 * b) == t // (2 * b)) & (s % (2 * b) < b) & (t % (2 * b) >= b)
    masks[:, LEVELS] = s == t
    return {"square_consts": square, "sign_consts": np.stack([sign, -sign], axis=1),
            "iota16": np.tile(np.arange(K, dtype=np.float32), (P, 1)), "level_masks": masks}


def kernel(**inputs):
    import concourse.bacc as bacc
    from concourse.bass_utils import run_bass_kernel_spmd as run

    a = {k: np.asarray(v) for k, v in inputs.items()}

    def columns(v):
        return v.reshape(CH, P).T

    data = {
        "x": a["x"][0], "xT": a["x"][0].T, "w_in": a["w_in"][0],
        "lam_re": a["s5_lam_re"][0].T, "lam_im": a["s5_lam_im"][0].T,
        "b_re": a["s5_b_re"][0].transpose(1, 0, 2), "b_im": a["s5_b_im"][0].transpose(1, 0, 2),
        "c_re": a["s5_c_re"][0].transpose(2, 0, 1), "c_im": a["s5_c_im"][0].transpose(2, 0, 1),
        "d_skip": columns(a["s5_d"][0]), "log_step": a["s5_log_step"][0],
        "w_glu": a["s5_w_glu"][0], "b_glu": columns(a["s5_b_glu"][0]),
        "lb_logits": a["hgrn_lb_logits"].reshape(2, CH, P).transpose(2, 0, 1),
        "gnorm": columns(a["hgrn_gnorm_w"][0]),
        "w_pa": a["w_pa"][0], "w_pb": a["w_pb"][0], "w_o": a["w_o"][0],
        "ln1_g": a["ln1_g"][0], "ln1_b": a["ln1_b"][0], "w_pq": a["peer_w_q"][0],
        "keysT": a["peer_sub_keys"][0].reshape(2 * HEADS, P, P).transpose(2, 0, 1),
        "peer_u": a["peer_u"][0], "peer_v": a["peer_v"][0], "ln2_g": a["ln2_g"][0], "ln2_b": a["ln2_b"][0],
        **shape_constants(),
    }
    nc = bacc.Bacc("TRN2", target_bir_lowering=False, num_devices=1)
    arrays, args = {}, []
    for name in _CALL:
        v = np.ascontiguousarray(data[name])
        arrays[f"in_{name}"] = v
        args.append(nc.dram_tensor(f"in_{name}", v.shape, mybir.dt.from_np(v.dtype), kind="ExternalInput").ap())
    args.append(nc.dram_tensor("out", (T, D), F32, kind="ExternalOutput").ap())
    hybrid_layer(nc, *args)
    r = run(nc, [arrays], core_ids=[0])
    return r.results[0]["out"].reshape(1, T, D)
```

```python
from contextlib import ExitStack

import numpy as np
import concourse.bass as bass
from concourse import mybir

ALU = mybir.AluOpType
ACT = mybir.ActivationFunctionType
F32 = mybir.dt.float32
F32R = mybir.dt.float32r
U32 = mybir.dt.uint32
U8 = mybir.dt.uint8
AX_X = mybir.AxisListType.X

P = 128
T = 512
D = 1024
NT = T // P
KD = D // P
W2 = 512
CH = W2 // P
G, NS, GH, L = 32, 64, 16, 8
NC = T // L
SCAN = 6
LEVELS = 7
HEADS = 8
K = 16
BLOCKS = NT * HEADS
FILL_SCAN, FILL_Y, FILL_LEVEL, GLU_AT, LATE = (2, 1, 1, 1, 1, 1), 3, (2, 1, 1, 1, 1, 1, 1, 0), 1, 3
NBUF = 8
ADDED = (8, 10, 12, 14, 15)
assert min(ADDED) >= K - NBUF
ALPHA = 2.0 ** 0.25
LN_EPS = 1e-5
RMS_EPS = 1e-6
LOW = -3.0e38
ROUND = 1.5 * 2.0 ** 23
TWO_PI_A, TWO_PI_B, TWO_PI_C = 6.28125, 1.93500518798828125e-3, 3.0199159819e-7
PI = 3.1415925

RING = 4
TURN_AT = 10
AHEAD = 3
U_S5, U_F, U_Q, U_V, U_G, U_GA, U_GB, U_END = 0, 4, 8, 12, 16, 20, 28, 36
COL = {"u": 0, "q": 512, "f": 1024, "v": 1536, "g": 2048, "ga": 2560, "gb": 3584}
UNIT_COLS = [COL[n] + P * i for n, m in
             (("u", 4), ("f", 4), ("q", 4), ("v", 4), ("g", 4), ("ga", 8), ("gb", 8)) for i in range(m)]


def unit_scan(lv):
    return U_V + 1 + sum(FILL_SCAN[:lv])


def hybrid_layer(nc, x, xT, w_in, lam_re, lam_im, b_re, b_im, c_re, c_im, d_skip, log_step, w_glu, b_glu,
                 lb_logits, gnorm, w_pa, w_pb, w_o, ln1_g, ln1_b, w_pq, keysT, peer_u, peer_v, ln2_g, ln2_b,
                 square_consts, sign_consts, iota16, level_masks, out):
    with ExitStack() as ctx:
        def sb(name, shape, dt=F32):
            return ctx.enter_context(nc.sbuf_tensor(name, shape, dt))

        def sem(name):
            return ctx.enter_context(nc.semaphore(name))

        def rounded(name, kb, shape):
            with ExitStack() as given_back:
                if kb:
                    given_back.enter_context(nc.sbuf_tensor(name + "_before", [P, kb * 256], F32))
                return given_back.enter_context(nc.sbuf_tensor(name, [P, *shape], F32R))

        w_lo = [rounded(f"w_lo{i}", 4 * i, [KD, P]) for i in range(RING)]
        w_hi = [rounded(f"w_hi{i}", 4 * (RING + i), [KD, P]) for i in range(RING)]
        x_lo = [rounded(f"x_lo{i}", 128 + 4 * i, [2, T]) for i in range(KD // 2)]
        x_hi = [rounded(f"x_hi{i}", 160 + 4 * i, [2, T]) for i in range(KD // 2)]
        arena = sb("arena", [P, 200 * 256])

        def part(kb, shape):
            n = int(np.prod(shape))
            v = arena[:, int(kb * 256):int(kb * 256) + n]
            if len(shape) == 1:
                return v
            names = "abcd"[:len(shape)]
            return v.rearrange(f"p ({' '.join(names)}) -> p {' '.join(names)}", **dict(zip(names, shape)))

        w_in_s = part(0, [RING, KD, P])
        qT, fT, vS, gT = (part(32 + 8 * i, [CH, T]) for i in range(4))
        xTs = part(128, [KD, T])
        sga = part(144, [KD, T])
        sgb = part(176, [KD, T])
        WinT = part(64, [G, P])
        Toe = part(80, [G, P])
        Wout = part(96, [G, L + 1, GH])
        Uc = part(114, [G, NC])
        wtmp = part(122, [8, L + 1, GH])
        Ksb = part(144, [G, P])
        X, Xs, CX, CXs, BB, BBs = (part(48 + 2 * i, [G, GH]) for i in range(6))
        small = part(60, [G * 32])
        Wnat = [part(176 + 4 * i, [8, L, GH]) for i in range(2)]
        wsum = part(192, [8, L, GH])
        uT = part(184, [CH, L, NC])
        S = part(176, [G, NC])
        scan1 = part(64, [G, NC])
        scan2 = part(72, [G, NC])
        Yc = part(64, [G, NC])
        wglu = part(72, [CH, W2])
        yT = part(176, [CH, L, NC])
        zT = part(184, [CH, L, NC])
        yaT = part(192, [CH, T])
        masks_in = part(114, [LEVELS + 1, P])
        rpw = part(196, [2, G, L])
        rpr, rpi = rpw[:, 0], rpw[:, 1]
        kT = part(80, [CH, T])
        bT = part(88, [CH, T])
        dec = [part(96, [CH, T]), part(104, [CH, T])]
        K0T = part(112, [CH, NT, P])
        sc = part(120, [CH, T])
        oT = fT
        wpa = part(64, [CH, D])
        wpb = part(80, [CH, D])
        wo = part(96, [KD, D])
        mT = part(64, [NT, KD, P])
        x1 = part(128, [NT, D])
        yac = part(144, [NT, D])
        g1, b1 = part(160, [D]), part(164, [D])
        wq = part(0, [KD, 2048])
        keys = part(192, [2 * HEADS, P])
        ubuf = [part(64 + 4 * ((i + 4) % NBUF), [D]) for i in range(NBUF)]
        vbuf = [part(96 + 4 * i, [D]) for i in range(NBUF)]
        diag = part(160, [K, P])
        x1c = [part(168, [D]), part(172, [D])]
        x1Tc = part(176, [KD, P])
        qs = part(180, [256])
        qTs = part(181, [2, P])
        srep = part(182, [P])
        cand = part(183, [K, K])
        crep = part(184, [K * K])
        eq = part(185, [2, K, K])
        v16 = part(187, [2, K])
        i16f = part(187.25, [2, K])
        taf = part(187.5, [2, K])
        e12 = part(187.75, [2, K])
        tv = part(188, [K])
        ex = part(188.25, [K])
        ga16 = part(188.5, [K])
        g2, b2 = x1[:, 0], x1[:, 1]
        i16 = sb("i16", [P, 2, K], U32)
        ti = sb("ti", [P, K], U32)
        ta = sb("ta", [P, 2, K], U32)
        idxU = [sb(f"idxU{i}", [P, K], U32) for i in range(2)]
        idxV = [sb(f"idxV{i}", [P, K], U32) for i in range(2)]
        gates = [sb(f"gates{i}", [P, K]) for i in range(2)]
        acts = [sb(f"acts{i}", [P, K]) for i in range(2)]
        coef = [sb(f"coef{i}", [P, K]) for i in range(2)]
        nmax = sb("nmax", [P, 1])
        esum = sb("esum", [P, 1])
        erec = sb("erec", [P, 1])
        sq = sb("sq", [P, 3, P])
        ident, JT, mean = sq[:, 0, :], sq[:, 1, :], sq[:, 2, :]
        sgn2 = sb("sgn2", [P, 2])
        sgn, nsgn = sgn2[:, 0:1], sgn2[:, 1:2]
        iot = sb("iot", [P, K])
        masks = sb("masks", [P, LEVELS + 1, P], U8)
        eps = sb("eps", [P, 2])
        dsk = sb("dsk", [P, CH])
        bgl = sb("bgl", [P, CH])
        gnw = sb("gnw", [P, CH])
        lbl = sb("lbl", [P, 2, CH])
        lbs = sb("lbs", [P, 4, CH])
        lb, olb = lbs[:, 0, :], lbs[:, 1, :]
        cp = sb("cp", [P, 2, SCAN, G])
        state = part(96, [CH, P])
        stats = sb("stats", [P, 2, 6])
        mv = sb("mv", [P, 2])
        rstd = sb("rstd", [P, 2])
        PS = ctx.enter_context(nc.psum_tensor("PS", [P, 8, 512], F32))

        def bank_a(j):
            return PS[:, (U_END - LATE + j) % 2]

        def level_scores(lv, h):
            return PS[:, 4 + 2 * (lv % 2) + h // 2, T // 2 * (h % 2):T // 2 * (h % 2 + 1)]

        def sm(i):
            return small[:, G * i:G * (i + 1)]

        zU = nc.dram_tensor("zU", [CH, P, L, NC], F32, kind="Internal").ap()
        zY = nc.dram_tensor("zY", [CH, P, L, NC], F32, kind="Internal").ap()

        def by_step(z, tau):
            return z.rearrange("q (j h) t c -> h t (q j) c", h=GH)[:, tau]

        pw = small[:, G * 10:G * 10 + 2 * G * (L + 1)].rearrange("p (a g k) -> p a g k", a=2, g=G)
        prw, piw = pw[:, 0], pw[:, 1]

        constants_loaded = sem("constants_loaded")
        masks_ready = sem("masks_ready")
        params_loaded = sem("params_loaded")
        xT_loaded = [sem(f"xT_loaded{i}") for i in range(4)]
        zu_stored = sem("zu_stored")
        zy_stored = sem("zy_stored")
        powers_ready = sem("powers_ready")
        gated_a = sem("gated_a")
        w_in_loaded = [sem(f"w_in_loaded{i}") for i in range(RING)]
        x_high_ready = sem("x_high_ready")
        x_low_ready = sem("x_low_ready")
        first_w_high = sem("first_w_high")
        w_high_ready = sem("w_high_ready")
        w_low_ready = sem("w_low_ready")
        unit_computed = sem("unit_computed")
        unit_taken = sem("unit_taken")
        dve_step = sem("dve_step")
        retrieval_step = sem("retrieval_step")
        step_sizes = sem("step_sizes")
        angles_ready = sem("angles_ready")
        trig_ready = sem("trig_ready")
        in_matrices = sem("in_matrices")
        in_products = sem("in_products")
        in_turned = sem("in_turned")
        in_taken = sem("in_taken")
        out_matrices = sem("out_matrices")
        kernels_computed = sem("kernels_computed")
        kernels_taken = sem("kernels_taken")
        toeplitz_zeroed = sem("toeplitz_zeroed")
        toeplitz_placed = sem("toeplitz_placed")
        chunks_loaded = sem("chunks_loaded")
        chunk_states = sem("chunk_states")
        states_taken = sem("states_taken")
        scan_powers = sem("scan_powers")
        state_turned = sem("state_turned")
        scan_part = sem("scan_part")
        scan_step = sem("scan_step")
        s5_computed = sem("s5_computed")
        s5_taken = sem("s5_taken")
        s5_loaded = sem("s5_loaded")
        skip_added = sem("skip_added")
        gelu_done = sem("gelu_done")
        glu_computed = sem("glu_computed")
        w_glu_loaded = sem("w_glu_loaded")
        glu_gate = sem("glu_gate")
        mixer_a_ready = sem("mixer_a_ready")
        bound_exps = sem("bound_exps")
        forget_ready = sem("forget_ready")
        log_forget = sem("log_forget")
        decay_logs = sem("decay_logs")
        decays_ready = sem("decays_ready")
        keyed_ready = sem("keyed_ready")
        level_scored = sem("level_scored")
        level_placed = sem("level_placed")
        end_keys_turned = sem("end_keys_turned")
        end_keys_taken = sem("end_keys_taken")
        hgrn_computed = sem("hgrn_computed")
        update_computed = sem("update_computed")
        state_ready = sem("state_ready")
        hgrn_taken = sem("hgrn_taken")
        mean_square = sem("mean_square")
        root_ready = sem("root_ready")
        mixer_b_ready = sem("mixer_b_ready")
        w_pa_loaded = sem("w_pa_loaded")
        w_pb_loaded = sem("w_pb_loaded")
        w_o_loaded = sem("w_o_loaded")
        a_projected = sem("a_projected")
        b_projected = sem("b_projected")
        merged = sem("merged")
        out_projected = sem("out_projected")
        x_added = sem("x_added")
        ln1_loaded = sem("ln1_loaded")
        x_loaded = [sem(f"x_loaded{i}") for i in range(NT)]
        ln1_var = sem("ln1_var")
        ln1_root = sem("ln1_root")
        x1_ready = sem("x1_ready")
        x1_scaled = sem("x1_scaled")
        w_pq_loaded = sem("w_pq_loaded")
        keys_loaded = sem("keys_loaded")
        block_copied = sem("block_copied")
        block_turned = sem("block_turned")
        block_taken = sem("block_taken")
        q_computed = sem("q_computed")
        q_taken = sem("q_taken")
        q_turned = sem("q_turned")
        q_turned_taken = sem("q_turned_taken")
        key_scores = sem("key_scores")
        key_scores_read = sem("key_scores_read")
        top_found = sem("top_found")
        exps_ready = sem("exps_ready")
        experts_found = sem("experts_found")
        u_gathered = [sem(f"u_gathered{i}") for i in range(NBUF)]
        v_gathered = [sem(f"v_gathered{i}") for i in range(NBUF)]
        u_dotted = sem("u_dotted")
        acts_gelu = sem("acts_gelu")
        coef_ready = sem("coef_ready")
        diag_ready = sem("diag_ready")
        v_mixed = sem("v_mixed")
        values_added = sem("values_added")
        ln2_loaded = sem("ln2_loaded")
        ln2_var = sem("ln2_var")
        ln2_root = sem("ln2_root")
        result_ready = sem("result_ready")
        out_stored = sem("out_stored")

        N_PAR = 4 + 8 + 2 + 4
        N_CST = 4

        block = ctx.enter_context(nc.Block())

        def kp(w):
            return w.rearrange("(k p) n -> p k n", p=P)

        @block.sync
        def _(sp):
            def load_unit(m):
                if m >= RING:
                    sp.wait_ge(unit_computed, m - RING + 1)
                col = UNIT_COLS[m]
                sp.dma_start(w_in_s[:, m % RING], kp(w_in[:, col:col + P])).then_inc(w_in_loaded[m % RING], 16)

            load_unit(0)
            for i in range(4):
                sp.dma_start(xTs[:, 2 * i:2 * i + 2], kp(xT)[:, 2 * i:2 * i + 2]).then_inc(xT_loaded[i], 16)
            load_unit(1)
            load_unit(2)
            sp.dma_start(sq[:, :, :], square_consts).then_inc(constants_loaded, 16)
            sp.dma_start(iot[:, :], iota16).then_inc(constants_loaded, 16)
            sp.dma_start(masks_in, level_masks).then_inc(constants_loaded, 16)
            for m in range(3, U_END):
                load_unit(m)
                if m == unit_scan(SCAN) + 2:
                    sp.wait_ge(scan_step, 4 * SCAN)
                    sp.dma_start(wglu, kp(w_glu)).then_inc(w_glu_loaded, 16)
                if m == U_END - RING - 1:
                    sp.wait_ge(glu_computed, CH)
                    sp.dma_start(wpa, kp(w_pa)).then_inc(w_pa_loaded, 16)
            sp.wait_ge(hgrn_computed, CH * NT)
            sp.wait_ge(end_keys_taken, CH)
            sp.wait_ge(state_ready, CH * (NT - 1))
            sp.dma_start(wpb, kp(w_pb)).then_inc(w_pb_loaded, 16)
            sp.dma_start(wo, kp(w_o)).then_inc(w_o_loaded, 16)
            sp.wait_ge(unit_computed, U_END)
            for i in range(NT):
                sp.dma_start(x1[:, i], x[i * P:(i + 1) * P, :]).then_inc(x_loaded[i], 16)
            sp.dma_start(g1, ln1_g.partition_broadcast(P)).then_inc(ln1_loaded, 16)
            sp.dma_start(b1, ln1_b.partition_broadcast(P)).then_inc(ln1_loaded, 16)
            for k in range(4):
                sp.dma_start(wq[:, k], w_pq[k * P:(k + 1) * P, :]).then_inc(w_pq_loaded, 16)
            sp.dma_start(keys, keysT).then_inc(keys_loaded, 16)
            sp.wait_ge(mixer_b_ready, CH)
            for k in (4, 6, 7):
                sp.dma_start(wq[:, k], w_pq[k * P:(k + 1) * P, :]).then_inc(w_pq_loaded, 16)
            sp.wait_ge(b_projected, 2 * NT)
            sp.dma_start(wq[:, 5], w_pq[5 * P:6 * P, :]).then_inc(w_pq_loaded, 16)
            sp.wait_ge(block_copied, 2 * HEADS + 1)
            sp.dma_start(g2, ln2_g.partition_broadcast(P)).then_inc(ln2_loaded, 16)
            sp.dma_start(b2, ln2_b.partition_broadcast(P)).then_inc(ln2_loaded, 16)
            for i in range(NT):
                for e in range(2):
                    es = slice(512 * e, 512 * e + 512)
                    sp.wait_ge(result_ready, 2 * i + e + 1)
                    sp.dma_start(out[i * P:(i + 1) * P, es], yac[:, i, es]).then_inc(out_stored, 16)
            sp.wait_ge(out_stored, 16 * 2 * NT)

        @block.gpsimd
        def _(pool):
            pool.memset(eps[:, 0:1], LN_EPS).then_inc(constants_loaded, 8)
            pool.memset(eps[:, 1:2], RMS_EPS).then_inc(constants_loaded, 8)
            for m in range(1, AHEAD):
                pool.wait_ge(first_w_high, m + 1)
                pool.tensor_tensor(w_lo[m][:, :, :], w_in_s[:, m], w_hi[m][:, :, :], ALU.subtract).then_inc(w_low_ready, 1)
            split = [AHEAD]

            def split_low(upto):
                while split[0] < min(upto, U_END):
                    m = split[0]
                    pool.wait_ge(w_high_ready, m - AHEAD + 1)
                    pool.tensor_tensor(w_lo[m % RING][:, :, :], w_in_s[:, m % RING], w_hi[m % RING][:, :, :],
                                       ALU.subtract).then_inc(w_low_ready, 1)
                    split[0] += 1

            pool.memset(Toe, 0.0).then_inc(toeplitz_zeroed, 1)
            pool.wait_ge(constants_loaded, 16 * N_CST)
            pool.tensor_copy(masks[:, :, :], masks_in).then_inc(masks_ready, 1)
            for q in range(CH):
                pool.wait_ge(unit_taken, U_S5 + q + 1)
                pool.dma_start(zU[q], uT[:, q]).then_inc(zu_stored, 16)
                split_low(AHEAD + q + 1)
            pool.wait_ge(zu_stored, 16 * CH)
            pool.wait_ge(masks_ready, 1)
            for tau in range(L):
                pool.dma_start(Uc[GH * tau:GH * tau + GH], by_step(zU, tau)).then_inc(chunks_loaded, 16)
            split_low(U_Q + 1)
            pool.wait_ge(powers_ready, 1)
            for q in range(4):
                gs = slice(8 * q, 8 * q + 8)
                if q >= 2:
                    pool.wait_ge(in_turned, 2 * (q - 1))
                full = [P, 8, L, GH]
                bb = BB[:, gs, :].unsqueeze(2).to_broadcast(full)
                bbs = BBs[:, gs, :].unsqueeze(2).to_broadcast(full)
                pool.tensor_tensor(Wnat[q % 2], bb, rpr[:, gs].unsqueeze(3).to_broadcast(full), ALU.mult
                                   ).then_inc(in_products, 1)
                pool.tensor_tensor(wsum, bbs, rpi[:, gs].unsqueeze(3).to_broadcast(full), ALU.mult
                                   ).then_inc(in_products, 1)
                pool.wait_ge(in_products, 2 * q + 2)
                pool.tensor_tensor(Wnat[q % 2], Wnat[q % 2], wsum, ALU.add).then_inc(in_matrices, 1)
                split_low(U_Q + 2 if q == 0 else U_V)
                pool.wait_ge(in_matrices, q + 1)
            split_low(U_V + AHEAD)
            pool.wait_ge(toeplitz_zeroed, 1)
            pool.wait_ge(kernels_taken, 8)
            for tau in range(L):
                n = GH * (L - tau)
                pool.dma_start(Toe[GH * tau:GH * tau + GH, :, GH * tau:P], Ksb[0:GH, :, 0:n]).then_inc(toeplitz_placed, 16)
            for lv in range(SCAN):
                w = 1 << lv
                for j in range(4):
                    gs = slice(8 * j, 8 * j + 8)
                    if lv == 0:
                        pool.wait_ge(states_taken, j + 1)
                        pool.wait_ge(scan_powers, 1)
                    else:
                        pool.wait_ge(scan_step, 4 * (lv - 1) + j + 1)
                    pool.tensor_tensor(scan1[:, gs, w:], S[:, gs, 0:NC - w],
                                       cp[:, 0, lv, gs].unsqueeze(2).to_broadcast([P, 8, NC - w]),
                                       ALU.mult).then_inc(scan_part, 1)
                split_low(unit_scan(lv) + AHEAD)
            split_low(unit_scan(SCAN) + AHEAD)
            pool.wait_ge(s5_taken, 4)
            for tau in range(L):
                pool.dma_start(by_step(zY, tau), Yc[GH * tau:GH * tau + GH]).then_inc(zy_stored, 16)
            split_low(unit_scan(SCAN) + AHEAD + 1)
            pool.wait_ge(zy_stored, 16 * L)
            pool.dma_start(yT, zY.rearrange("q p t c -> p q t c")).then_inc(s5_loaded, 16)
            split_low(U_END)

            def until(s, value):
                pool.wait_ge(s, value)
                pool.nop(nofuse=True)

            def gather_u(n, par, k):
                if k == 0:
                    until(experts_found, n + 1)
                if isinstance(n, int) and n == 0 and NBUF - NT <= k < NBUF:
                    pool.wait_ge(out_projected, 2 * (k - (NBUF - NT)) + 2)
                if not (isinstance(n, int) and n == 0 and k < NBUF):
                    until(u_dotted, K * n + (k - NBUF + 1))
                pool.indirect_dma_start(ubuf[k % NBUF], None, peer_u,
                                        bass.IndirectOffsetOnAxis(idxU[par][:, k:k + 1], 0)
                                        ).then_inc(u_gathered[k % NBUF], 16)

            def gather_v(n, par, k):
                if isinstance(n, int) and n == 0 and k < NBUF:
                    pool.indirect_dma_start(vbuf[k], None, peer_v, bass.IndirectOffsetOnAxis(idxU[0][:, k:k + 1], 0)
                                            ).then_inc(v_gathered[k], 16)
                    return
                if k == (NBUF if isinstance(n, int) and n == 0 else 0):
                    until(coef_ready, n + 1)
                until(v_mixed, K * n + (k - NBUF + 1))
                pool.indirect_dma_start(vbuf[k % NBUF], None, peer_v,
                                        bass.IndirectOffsetOnAxis(idxV[par][:, k:k + 1], 0)
                                        ).then_inc(v_gathered[k % NBUF], 16)

            def gathers(n, par, u=True, v=True):
                lead = 4
                for k in range(K + lead):
                    if u and k < K:
                        gather_u(n, par, k)
                    if v and k >= lead and not (isinstance(n, int) and n == 1 and k - lead < NBUF):
                        gather_v(n - 1, 1 - par, k - lead)

            pool.wait_ge(b_projected, 2 * NT)
            gathers(0, 0, v=False)
            for k in range(NBUF):
                gather_v(0, 0, k)
            gathers(1, 1)
            with pool.Fori(2, BLOCKS, 2) as n:
                gathers(n, 0)
                gathers(n + 1, 1)
            gathers(BLOCKS, 0, u=False)

        @block.scalar
        def _(act):
            for half in range(2):
                rows = slice(NS * half, NS * half + NS)
                act.dma_start(sm(0)[rows, :], lam_re).then_inc(params_loaded, 16)
                act.dma_start(sm(1)[rows, :], lam_im).then_inc(params_loaded, 16)
                act.dma_start(X[rows], (b_re, b_im)[half]).then_inc(params_loaded, 16)
                act.dma_start(Xs[rows], (b_im, b_re)[half]).then_inc(params_loaded, 16)
                act.dma_start(CX[rows], (c_re, c_im)[half]).then_inc(params_loaded, 16)
                act.dma_start(CXs[rows], (c_im, c_re)[half]).then_inc(params_loaded, 16)
            act.dma_start(sm(2), log_step.partition_broadcast(P)).then_inc(params_loaded, 16)
            act.dma_start(lbl[:, :, :], lb_logits).then_inc(params_loaded, 16)
            act.dma_start(dsk[:, :], d_skip).then_inc(params_loaded, 16)
            act.dma_start(bgl[:, :], b_glu).then_inc(params_loaded, 16)
            act.dma_start(gnw[:, :], gnorm).then_inc(params_loaded, 16)
            act.dma_start(sgn2[:, :], sign_consts).then_inc(params_loaded, 16)
            act.wait_ge(params_loaded, 16 * N_PAR)
            act.activation(sm(3), sm(2), ACT.Exp).then_inc(step_sizes, 1)
            act.wait_ge(bound_exps, 1)
            act.activation(lbs[:, 2:4, :], lbs[:, 2:4, :], ACT.Exp).then_inc(bound_exps, 1)
            act.wait_ge(angles_ready, 1)
            act.activation(sm(6), sm(4), ACT.Exp).then_inc(trig_ready, 1)
            act.wait_ge(angles_ready, 2)
            act.activation(sm(7), sm(5), ACT.Sin, scale=0.5).then_inc(trig_ready, 1)
            act.activation(sm(8), sm(5), ACT.Sin).then_inc(trig_ready, 1)

            def unit(m):
                act.wait_ge(unit_computed, m + 1)
                bank = PS[:, m % 2]
                if m < U_F:
                    act.activation(uT[:, m], bank.rearrange("p (c t) -> p t c", t=L), ACT.Copy).then_inc(unit_taken, 1)
                elif m < U_Q:
                    act.activation(fT[:, m - U_F], bank, ACT.Sigmoid).then_inc(unit_taken, 1)
                elif m < U_V:
                    act.activation(qT[:, m - U_Q], bank, ACT.Silu).then_inc(unit_taken, 1)
                elif m < U_G:
                    if m == U_V:
                        act.wait_ge(out_matrices, 4)
                    c = P * (m - U_V)
                    act.activation(vS[:, :, c:c + P], bank.rearrange("p (a c) -> p a c", a=NT), ACT.Copy
                                   ).then_inc(unit_taken, 1)
                elif m < U_GA:
                    if m == U_G:
                        act.wait_ge(scan_powers, 1)
                    act.activation(gT[:, m - U_G], bank, ACT.Silu).then_inc(unit_taken, 1)
                elif m < U_GB:
                    if m == U_GA:
                        act.wait_ge(toeplitz_placed, 16 * L)
                    act.activation(sga[:, m - U_GA], bank, ACT.Sigmoid).then_inc(unit_taken, 1)
                else:
                    if m == U_GB:
                        act.wait_ge(mixer_a_ready, CH)
                    act.activation(sgb[:, m - U_GB], bank, ACT.Sigmoid).then_inc(unit_taken, 1)
                m += AHEAD
                if m < U_END:
                    act.wait_ge(w_in_loaded[m % RING], 16 * (m // RING + 1))
                    act.activation(w_hi[m % RING][:, :, :], w_in_s[:, m % RING], ACT.Copy).then_inc(w_high_ready, 1)

            for m in range(U_S5, TURN_AT):
                unit(m)
            for q in range(8):
                if q == 4:
                    for m in range(TURN_AT, U_V):
                        unit(m)
                act.wait_ge(in_turned, q + 1)
                act.activation(WinT[:, 4 * q:4 * q + 4, :], PS[:, 2 + q % 2].rearrange("p (a b) -> p a b", a=4),
                               ACT.Copy).then_inc(in_taken, 1)
            for q in range(8):
                act.wait_ge(kernels_computed, q + 1)
                act.activation(Ksb[0:GH, 4 * q:4 * q + 4, :],
                               PS[0:GH, 2 + q % 2].rearrange("p (a b) -> p a b", a=4), ACT.Copy).then_inc(kernels_taken, 1)
            for j in range(4):
                act.wait_ge(chunk_states, j + 1)
                act.activation(S[:, 8 * j:8 * j + 8, :], PS[:, 4 + j].rearrange("p (a b) -> p a b", a=8),
                               ACT.Copy).then_inc(states_taken, 1)
            fill = list(range(U_V, U_END))

            def fill_in(n):
                for _ in range(n):
                    unit(fill.pop(0))

            fill_in(1 + sum(FILL_SCAN))
            for j in range(4):
                act.wait_ge(s5_computed, j + 1)
                act.activation(Yc[:, 8 * j:8 * j + 8, :], PS[:, 4 + j].rearrange("p (a b) -> p a b", a=8),
                               ACT.Copy).then_inc(s5_taken, 1)
            act.wait_ge(forget_ready, 1)
            act.activation(fT, fT, ACT.Ln).then_inc(log_forget, 1)
            fill_in(FILL_Y - 1)
            for lv in range(LEVELS + 1):
                if lv < LEVELS:
                    act.wait_ge(decay_logs, lv + 1)
                    act.activation(dec[lv % 2], dec[lv % 2], ACT.Exp).then_inc(decays_ready, 1)
                fill_in(FILL_LEVEL[lv - 1] if lv else 1)
                if lv == 1:
                    act.wait_ge(skip_added, 1)
                    act.activation(yT, yT, ACT.Gelu_apprx_tanh).then_inc(gelu_done, 1)
                if lv - 1 == GLU_AT:
                    for m in range(CH):
                        act.wait_ge(glu_computed, m + 1)
                        act.activation(zT[:, m], PS[:, 2 + m % 2].rearrange("p (t c) -> p t c", t=L), ACT.Sigmoid,
                                       bias=bgl[:, m:m + 1]).then_inc(glu_gate, 1)
            fill_in(1)
            for lv in (LEVELS, LEVELS + 1):
                act.wait_ge(decay_logs, lv + 1)
                act.activation(dec[lv % 2], dec[lv % 2], ACT.Exp).then_inc(decays_ready, 1)
            fill_in(len(fill) - LATE)
            for h in range(CH):
                act.wait_ge(end_keys_turned, h + 1)
                act.activation(K0T[:, h], PS[:, 2 + h % 2].rearrange("p (a b) -> p a b", a=NT), ACT.Copy
                               ).then_inc(end_keys_taken, 1)
            for h in range(CH):
                act.wait_ge(hgrn_computed, CH * (NT - 1) + h + 1)
                act.activation(oT[:, h], PS[:, 4 + h], ACT.Copy).then_inc(hgrn_taken, 1)
                act.activation(qT[:, h], PS[:, 4 + h], ACT.Square).then_inc(hgrn_taken, 1)
            for h in range(CH):
                act.wait_ge(mean_square, h + 1)
                act.activation(qT[:, h], PS[:, 2 + h % 2], ACT.Sqrt, bias=eps[:, 1:2]).then_inc(root_ready, 1)
            fill_in(LATE)

            def first_norm(i):
                act.wait_ge(ln1_var, i + 1)
                act.activation(rstd[:, 0:1], mv[:, 1:2], ACT.Sqrt, bias=eps[:, 0:1]).then_inc(ln1_root, 1)

            def residual(i):
                act.wait_ge(x1_ready, 2 * i + 2)
                act.activation(yac[:, i], x1[:, i], ACT.Copy, scale=ALPHA).then_inc(x1_scaled, 1)

            def last_norm(i):
                act.wait_ge(ln2_var, i + 1)
                act.activation(rstd[:, 0:1], mv[:, 1:2], ACT.Sqrt, bias=eps[:, 0:1]).then_inc(ln2_root, 1)

            def prepare(n, par):
                if not (isinstance(n, int) and n < 2):
                    act.wait_ge(u_dotted, K * (n - 1))
                    act.nop(nofuse=True)
                tile = n // HEADS
                src = x1[:, tile, :] if isinstance(n, int) else \
                    x1[:, bass.ds(tile, 1), :].rearrange("p a d -> p (a d)")
                act.activation(x1c[par], src, ACT.Copy).then_inc(block_copied, 1)

            def prepare_rest(n):
                for h in range(2):
                    act.wait_ge(block_turned, 2 * n + h + 1)
                    act.activation(x1Tc[:, 4 * h:4 * h + 4], PS[:, h].rearrange("p (a b) -> p a b", a=4),
                                   ACT.Copy).then_inc(block_taken, 1)
                act.wait_ge(q_computed, n + 1)
                act.activation(qs, PS[:, 2, 0:256], ACT.Copy).then_inc(q_taken, 1)
                act.wait_ge(q_turned, n + 1)
                act.activation(qTs, PS[:, 3, 0:256].rearrange("p (a b) -> p a b", a=2), ACT.Copy).then_inc(q_turned_taken, 1)

            def softmax_exp(n):
                act.wait_ge(top_found, n + 1)
                act.activation(ex, tv, ACT.Exp, bias=nmax[:, 0:1], accum_out=esum[:, 0:1]).then_inc(exps_ready, 1)

            def diagonals(n, par):
                act.wait_ge(coef_ready, n + 1)
                if not (isinstance(n, int) and n == 0):
                    act.wait_ge(v_mixed, K * n)
                for k in range(K):
                    act.activation(diag[:, k], ident, ACT.Copy, scale=coef[par][:, k:k + 1]).then_inc(diag_ready, 1)

            def gelu(n, par):
                act.wait_ge(u_dotted, K * (n + 1))
                act.activation(ga16, acts[par][:, :], ACT.Gelu_apprx_tanh).then_inc(acts_gelu, 1)

            def step(n, par, last=False, copied=False):
                if not last and not copied:
                    prepare(n + 1, 1 - par)
                diagonals(n - 1, 1 - par)
                if not last:
                    prepare_rest(n + 1)
                    softmax_exp(n + 1)
                gelu(n, par)

            first_norm(0)
            act.wait_ge(x1_ready, 2)
            prepare(0, 0)
            prepare_rest(0)
            softmax_exp(0)
            first_norm(1)
            act.wait_ge(merged, 2 * NT)
            residual(0)
            residual(1)
            first_norm(2)
            prepare(1, 1)
            prepare_rest(1)
            softmax_exp(1)
            gelu(0, 0)
            prepare(2, 0)
            residual(2)
            first_norm(3)
            residual(3)
            step(1, 1, copied=True)
            with act.Fori(2, BLOCKS - 2, 2) as n:
                step(n, 0)
                step(n + 1, 1)
            last_norm(0)
            last_norm(1)
            step(BLOCKS - 2, 0)
            last_norm(2)
            step(BLOCKS - 1, 1, last=True)
            diagonals(BLOCKS - 1, 1)
            last_norm(3)

        @block.tensor
        def _(pe):
            def unit(m):
                pe.wait_ge(w_low_ready, m + 1)
                if m >= 2:
                    pe.wait_ge(unit_taken, m - 1)
                wl, wh = w_lo[m % RING], w_hi[m % RING]
                if U_V <= m < U_G:
                    for t in range(NT):
                        ts = slice(t * P, (t + 1) * P)
                        for k in range(KD):
                            xl, xh = x_lo[k // 2], x_hi[k // 2]
                            for n, (a, b) in enumerate(((xh, wl), (xl, wh), (xh, wh))):
                                last = pe.matmul(PS[:, m % 2, ts], a[:, k % 2, ts], b[:, k],
                                                 start=k == 0 and n == 0, stop=k == KD - 1 and n == 2)
                else:
                    for k in range(KD):
                        if m == 0 and k % 2 == 0:
                            pe.wait_ge(x_low_ready, k // 2 + 1)
                        xl, xh = x_lo[k // 2], x_hi[k // 2]
                        for n, (a, b) in enumerate(((wl, xh), (wh, xl), (wh, xh))):
                            last = pe.matmul(PS[:, m % 2], a[:, k], b[:, k % 2],
                                             start=k == 0 and n == 0, stop=k == KD - 1 and n == 2)
                last.then_inc(unit_computed, 1)

            for m in range(U_S5, TURN_AT):
                unit(m)
            pe.wait_ge(constants_loaded, 16 * N_CST)
            for q in range(8):
                if q == 4:
                    for m in range(TURN_AT, U_V):
                        unit(m)
                pe.wait_ge(in_matrices, q // 2 + 1)
                if q >= 2:
                    pe.wait_ge(in_taken, q - 1)
                for a in range(4):
                    last = pe.transpose(PS[:, 2 + q % 2, a * P:(a + 1) * P],
                                        Wnat[q // 2 % 2][:, 4 * (q % 2) + a].rearrange("p l h -> p (l h)"), ident)
                last.then_inc(in_turned, 1)
            pe.wait_ge(out_matrices, 4)
            for q in range(8):
                pe.wait_ge(in_taken, min(8, 7 + q))
                if q >= 2:
                    pe.wait_ge(kernels_taken, q - 1)
                for a in range(4):
                    g = 4 * q + a
                    last = pe.matmul(PS[0:GH, 2 + q % 2, a * P:(a + 1) * P], BB[:, g, :],
                                     Wout[:, g, 0:L, :].rearrange("p l h -> p (l h)"), start=True, stop=True)
                last.then_inc(kernels_computed, 1)
            pe.wait_ge(chunks_loaded, 16 * L)
            for g in range(G):
                last = pe.matmul(PS[:, 4 + g // 8, (g % 8) * NC:(g % 8 + 1) * NC], WinT[:, g], Uc[:, g],
                                 start=True, stop=True)
                if g % 8 == 7:
                    last.then_inc(chunk_states, 1)
            fill = list(range(U_V, U_END))

            def fill_in(n):
                for _ in range(n):
                    unit(fill.pop(0))

            fill_in(1)
            for lv in range(SCAN):
                for j in range(4):
                    if lv == 0:
                        pe.wait_ge(states_taken, j + 1)
                    else:
                        pe.wait_ge(scan_step, 4 * (lv - 1) + j + 1)
                    shifted = NC - (1 << lv)
                    pe.matmul(PS[:, 4 + j].rearrange("p (a b) -> p a b", a=8)[:, :, 0:shifted], JT,
                              S[:, 8 * j:8 * j + 8, 0:shifted], start=True, stop=True).then_inc(state_turned, 1)
                fill_in(FILL_SCAN[lv])
            pe.wait_ge(toeplitz_placed, 16 * L)
            for q in range(4):
                pe.wait_ge(scan_step, 4 * (SCAN - 1) + q + 1)
                for a in range(8):
                    g, c0 = 8 * q + a, a * NC
                    pe.matmul(PS[:, 4 + q, c0:c0 + NC], Toe[:, g], Uc[:, g], start=a == 0, stop=False,
                              skip_group_check=True)
                for a in range(8):
                    g, c0 = 8 * q + a, a * NC
                    last = pe.matmul(PS[:, 4 + q, c0 + 1:c0 + NC],
                                     Wout[:, g, 1:L + 1, :].rearrange("p l h -> p (l h)"),
                                     S[:, g, 0:NC - 1], start=False, stop=True, skip_group_check=True)
                last.then_inc(s5_computed, 1)
            fill_in(FILL_Y)
            pe.wait_ge(s5_taken, 4)

            def glu():
                pe.wait_ge(w_glu_loaded, 16)
                pe.wait_ge(gelu_done, 1)
                for m in range(CH):
                    if m >= 2:
                        pe.wait_ge(glu_gate, m - 1)
                    for k in range(CH):
                        last = pe.matmul(PS[:, 2 + m % 2], wglu[:, k, m * P:(m + 1) * P],
                                         yT[:, k].rearrange("p t c -> p (t c)"), start=k == 0, stop=k == CH - 1)
                    last.then_inc(glu_computed, 1)

            for lv in range(LEVELS + 1):
                pe.wait_ge(keyed_ready, lv + 1)
                for h in range(CH):
                    if lv == LEVELS:
                        latest = h // 2 == (LEVELS - 1) % 2
                        pe.wait_ge(level_placed, CH * (LEVELS if latest else LEVELS - 1))
                    elif lv >= 2 and h % 2 == 0:
                        pe.wait_ge(level_placed, CH * (lv - 2) + h + 2)
                    for i in range(NT):
                        ts = slice(i * P, (i + 1) * P)
                        if lv < LEVELS:
                            lhs = dec[lv % 2][:, h, ts]
                            rhs = lhs.rearrange("p (n a b) -> p n a b", a=2, b=P >> (lv + 1))[:, :, 1, :]
                            last = pe.matmul(level_scores(lv, h)[:, i * P // 2:(i + 1) * P // 2], lhs, rhs,
                                             start=True, stop=True)
                        else:
                            last = pe.matmul(PS[:, 4 + h, ts], kT[:, h, ts], qT[:, h, ts], start=True, stop=True)
                    last.then_inc(level_scored, 1)
                fill_in(FILL_LEVEL[lv])
                if lv == GLU_AT:
                    glu()
            fill_in(len(fill) - LATE)

            def project_a(j):
                if j == 0:
                    pe.wait_ge(w_pa_loaded, 16)
                    pe.wait_ge(mixer_a_ready, CH)
                if j < 2:
                    pe.wait_ge(unit_taken, U_END - LATE - 1 + j)
                else:
                    pe.wait_ge(gated_a, j - 1)
                for k in range(CH):
                    last = pe.matmul(bank_a(j), wpa[:, k, j * P:(j + 1) * P], yaT[:, k],
                                     start=k == 0, stop=k == CH - 1)
                last.then_inc(a_projected, 1)

            project_a(0)
            pe.wait_ge(keyed_ready, LEVELS + 3)
            for h in range(CH):
                if h >= 2:
                    pe.wait_ge(end_keys_taken, h - 1)
                for i in range(NT):
                    last = pe.transpose(PS[:, 2 + h % 2, i * P:(i + 1) * P], dec[0][:, h, i * P:(i + 1) * P], ident)
                last.then_inc(end_keys_turned, 1)
            project_a(1)
            pe.wait_ge(level_placed, CH * (LEVELS + 1))
            pe.wait_ge(end_keys_taken, CH)
            for i in range(NT):
                ts = slice(i * P, (i + 1) * P)
                for h in range(CH):
                    hs = slice(h * P, (h + 1) * P)
                    if i:
                        pe.wait_ge(state_ready, CH * (i - 1) + h + 1)
                        pe.matmul(PS[:, 4 + h, ts], state[:, h], dec[1][:, h, ts], start=True, stop=False)
                    pe.matmul(PS[:, 4 + h, ts], vS[:, i, hs], sc[:, h, ts], start=i == 0, stop=True
                              ).then_inc(hgrn_computed, 1)
                if i < NT - 1:
                    for h in range(CH):
                        hs = slice(h * P, (h + 1) * P)
                        last = pe.matmul(PS[:, 3, hs], K0T[:, h, i], vS[:, i, hs], start=True, stop=True)
                    last.then_inc(update_computed, 1)
                    project_a(2 + i)
            project_a(5)
            for h in range(CH):
                pe.wait_ge(hgrn_taken, 2 * h + 2)
                if h >= 2:
                    pe.wait_ge(root_ready, h - 1)
                pe.matmul(PS[:, 2 + h % 2], mean, qT[:, h], start=True, stop=True).then_inc(mean_square, 1)
            project_a(6)
            project_a(7)
            pe.wait_ge(gated_a, KD - 1)
            fill_in(1)
            pe.wait_ge(gated_a, KD)
            fill_in(LATE - 1)
            pe.wait_ge(w_pb_loaded, 16)
            pe.wait_ge(mixer_b_ready, CH)

            def project_b(i, g):
                n = 2 * i + g
                if n < 2:
                    pe.wait_ge(unit_taken, U_END - 1 + n)
                elif n >= 4:
                    pe.wait_ge(merged, n - 3)
                for a in range(KD // 2):
                    j = KD // 2 * g + a
                    for k in range(CH):
                        last = pe.matmul(PS[:, n % 4, a * P:(a + 1) * P], wpb[:, k, j * P:(j + 1) * P],
                                         oT[:, k, i * P:(i + 1) * P], start=k == 0, stop=k == CH - 1)
                last.then_inc(b_projected, 1)

            def out_project(i, e):
                if e == 0:
                    pe.wait_ge(merged, 2 * i + 2)
                if i >= 2:
                    pe.wait_ge(x_added, 2 * (i - 2) + e + 1)
                for k in range(KD):
                    last = pe.matmul(PS[:, 4 + 2 * (i % 2) + e], mT[:, i, k],
                                     wo[:, k, 512 * e:512 * e + 512], start=k == 0, stop=k == KD - 1)
                last.then_inc(out_projected, 1)

            def rows_turned(n, par):
                pe.wait_ge(block_copied, n + 1)
                for h in range(2):
                    if not (isinstance(n, int) and n == 0):
                        pe.wait_ge(block_taken, 2 * (n - 1) + h + 1)
                    for a in range(4):
                        c = (4 * h + a) * P
                        last = pe.transpose(PS[:, h, a * P:(a + 1) * P], x1c[par][:, c:c + P], ident)
                    last.then_inc(block_turned, 1)

            def queries(n):
                pe.wait_ge(block_taken, 2 * n + 2)
                if not (isinstance(n, int) and n == 0):
                    pe.wait_ge(key_scores_read, n)
                head = n % HEADS
                for k in range(KD):
                    cols = wq[:, k, bass.ds(head * 256, 256)]
                    last = pe.matmul(PS[:, 2, 0:256], x1Tc[:, k], cols, start=k == 0, stop=k == KD - 1)
                last.then_inc(q_computed, 1)

            def queries_turned(n):
                pe.wait_ge(q_taken, n + 1)
                for a in range(2):
                    last = pe.transpose(PS[:, 3, a * P:(a + 1) * P], qs[:, a * P:(a + 1) * P], ident)
                last.then_inc(q_turned, 1)

            def scores(n):
                pe.wait_ge(q_turned_taken, n + 1)
                head = n % HEADS
                for a in range(2):
                    ks = keys[:, bass.ds(head * 2 + a, 1), :].rearrange("p a n -> p (a n)")
                    last = pe.matmul(PS[:, 2, a * P:(a + 1) * P], qTs[:, a], ks, start=True, stop=True)
                last.then_inc(key_scores, 1)

            def mix_values(n, par, ks, final=K - 1):
                for k in ks:
                    if k == 0 and not (isinstance(n, int) and n < 2):
                        pe.wait_ge(values_added, n - 1)
                    pe.wait_ge(diag_ready, K * n + k + 1)
                    pe.wait_ge(v_gathered[k % NBUF], 16 * (2 * n + k // NBUF + 1))
                    for e in range(2):
                        last = pe.matmul(PS[:, 4 + 2 * par + e], diag[:, k], vbuf[k % NBUF][:, 512 * e:512 * e + 512],
                                         start=k == 0, stop=k == final)
                    last.then_inc(v_mixed, 1)

            def step(n, par, first=False, last=False):
                if not last:
                    rows_turned(n + 1, 1 - par)
                    queries(n + 1)
                if not first:
                    mix_values(n - 1, 1 - par, range(0, 2))
                if not last:
                    queries_turned(n + 1)
                if not first:
                    mix_values(n - 1, 1 - par, range(2, 4))
                if not last:
                    scores(n + 1)
                if not first:
                    mix_values(n - 1, 1 - par, range(4, K))

            project_b(0, 0)
            project_b(0, 1)
            project_b(1, 0)
            project_b(1, 1)
            pe.wait_ge(w_o_loaded, 16)
            pe.wait_ge(hgrn_taken, 2 * CH)
            out_project(0, 0)
            out_project(0, 1)
            project_b(2, 0)
            project_b(2, 1)
            project_b(3, 0)
            project_b(3, 1)
            out_project(1, 0)
            pe.wait_ge(merged, 2 * NT)
            rows_turned(0, 0)
            pe.wait_ge(w_pq_loaded, 16 * KD)
            queries(0)
            queries_turned(0)
            pe.wait_ge(keys_loaded, 16)
            scores(0)
            out_project(1, 1)
            for i in (2, 3):
                out_project(i, 0)
                out_project(i, 1)
            step(0, 0, first=True)
            pe.wait_ge(x_added, 2 * NT)
            step(1, 1)
            with pe.Fori(2, BLOCKS - 2, 2) as n:
                step(n, 0)
                step(n + 1, 1)
            step(BLOCKS - 2, 0)
            step(BLOCKS - 1, 1, last=True)
            mixed_last = [k for k in range(K) if k not in ADDED]
            mix_values(BLOCKS - 1, 1, mixed_last, final=mixed_last[-1])

        @block.vector
        def _(dve):
            count = [0]

            def chain(ins):
                count[0] += 1
                ins.then_inc(dve_step, 1)
                dve.wait_ge(dve_step, count[0])

            def tt(o, a, b, op):
                return dve.tensor_tensor(o, a, b, op)

            def cmul(outr, outi, ar, ai, br, bi, t):
                chain(tt(t, ar, br, ALU.mult))
                chain(tt(outr, ai, bi, ALU.mult))
                chain(tt(outr, t, outr, ALU.subtract))
                chain(tt(t, ar, bi, ALU.mult))
                chain(tt(outi, ai, br, ALU.mult))
                chain(tt(outi, t, outi, ALU.add))

            def split_high(m):
                dve.wait_ge(w_in_loaded[m], 16)
                dve.tensor_copy(w_hi[m][:, :, :], w_in_s[:, m]).then_inc(first_w_high, 1)

            split_high(0)
            dve.wait_ge(first_w_high, 1)
            tt(w_lo[0][:, :, :], w_in_s[:, 0], w_hi[0][:, :, :], ALU.subtract).then_inc(w_low_ready, 1)
            for i in range(4):
                ks = slice(2 * i, 2 * i + 2)
                dve.wait_ge(xT_loaded[i], 16)
                dve.tensor_copy(x_hi[i][:, :, :], xTs[:, ks]).then_inc(x_high_ready, 1)
                dve.wait_ge(x_high_ready, i + 1)
                tt(x_lo[i][:, :, :], xTs[:, ks], x_hi[i][:, :, :], ALU.subtract).then_inc(x_low_ready, 1)
            for m in range(1, AHEAD):
                split_high(m)
            dve.wait_ge(params_loaded, 16 * N_PAR)
            chain(tt(lb, lbl[:, 0, :], lbl[:, 1, :], ALU.max))
            tt(lbs[:, 2, :], lbl[:, 0, :], lb, ALU.subtract)
            tt(lbs[:, 3, :], lbl[:, 1, :], lb, ALU.subtract).then_inc(bound_exps, 1)
            dve.wait_ge(step_sizes, 1)
            tt(sm(4), sm(0), sm(3), ALU.mult).then_inc(angles_ready, 1)
            chain(tt(sm(5), sm(1), sm(3), ALU.mult))
            chain(dve.tensor_scalar(sm(6 + 3), sm(5), 1.0 / (2 * np.pi), None, ALU.mult))
            chain(dve.tensor_scalar(sm(9), sm(9), ROUND, None, ALU.add))
            chain(dve.tensor_scalar(sm(9), sm(9), ROUND, None, ALU.subtract))
            for c in (TWO_PI_A, TWO_PI_B, TWO_PI_C):
                chain(dve.scalar_tensor_tensor(sm(5), sm(9), -c, sm(5), ALU.mult, ALU.add))
            dve.tensor_scalar(sm(5), sm(5), PI, -PI, ALU.min, ALU.max).then_inc(angles_ready, 1)
            dve.wait_ge(bound_exps, 2)
            chain(tt(olb, lbs[:, 2, :], lbs[:, 3, :], ALU.add))
            chain(dve.reciprocal(olb, olb))
            chain(tt(lb, lbs[:, 2, :], olb, ALU.mult))
            chain(dve.tensor_scalar(olb, lb, -1.0, 1.0, ALU.mult, ALU.add))
            dve.wait_ge(trig_ready, 3)
            chain(tt(sm(9), sm(7), sm(7), ALU.mult))
            chain(dve.tensor_scalar(sm(9), sm(9), -2.0, 1.0, ALU.mult, ALU.add))
            dve.memset(prw[:, :, 0], 1.0)
            dve.memset(piw[:, :, 0], 0.0)
            chain(tt(prw[:, :, 1], sm(6), sm(9), ALU.mult))
            chain(tt(piw[:, :, 1], sm(6), sm(8), ALU.mult))
            tt(sm(3), sm(0), sm(0), ALU.mult)
            chain(tt(sm(4), sm(1), sm(1), ALU.mult))
            chain(tt(sm(3), sm(3), sm(4), ALU.add))
            chain(dve.reciprocal(sm(3), sm(3)))
            chain(dve.tensor_scalar(sm(4), prw[:, :, 1], -1.0, None, ALU.add))
            tt(sm(5), sm(4), sm(0), ALU.mult)
            chain(tt(sm(6), piw[:, :, 1], sm(1), ALU.mult))
            chain(tt(sm(5), sm(5), sm(6), ALU.add))
            tt(sm(6), piw[:, :, 1], sm(0), ALU.mult)
            chain(tt(sm(7), sm(4), sm(1), ALU.mult))
            chain(tt(sm(6), sm(6), sm(7), ALU.subtract))
            tt(sm(5), sm(5), sm(3), ALU.mult)
            chain(tt(sm(6), sm(6), sm(3), ALU.mult))
            chain(dve.tensor_scalar(sm(6), sm(6), sgn, None, ALU.mult))
            wr = sm(5).unsqueeze(2).to_broadcast([P, G, GH])
            wi = sm(6).unsqueeze(2).to_broadcast([P, G, GH])
            tmp = Wnat[0].rearrange("p a l h -> p (a l h)")[:, 0:G * GH].rearrange("p (g h) -> p g h", g=G)
            chain(tt(BB, X, wr, ALU.mult))
            chain(tt(tmp, Xs, wi, ALU.mult))
            chain(tt(BB, BB, tmp, ALU.add))
            chain(tt(BBs, Xs, wr, ALU.mult))
            chain(tt(tmp, X, wi, ALU.mult))
            chain(tt(BBs, BBs, tmp, ALU.subtract))
            chain(dve.tensor_scalar(CX, CX, nsgn, None, ALU.mult))
            for lo, n in ((1, 1), (2, 2), (4, 4)):
                def power(a, k0, kn):
                    return a[:, :, k0:k0 + kn]
                t3 = Wnat[1].rearrange("p a l h -> p (a l h)")[:, 0:G * n].rearrange("p (g k) -> p g k", g=G)
                br = prw[:, :, lo:lo + 1].to_broadcast([P, G, n])
                bi = piw[:, :, lo:lo + 1].to_broadcast([P, G, n])
                cmul(power(prw, lo + 1, n), power(piw, lo + 1, n), power(prw, 1, n), power(piw, 1, n), br, bi, t3)
            for k in range(L):
                dve.tensor_copy(rpr[:, :, L - 1 - k], prw[:, :, k])
                last = dve.tensor_scalar(rpi[:, :, L - 1 - k], piw[:, :, k], sgn, None, ALU.mult)
            chain(last)
            dve.engine_nop().then_inc(powers_ready, 1)
            dve.tensor_copy(cp[:, 0, 0, :], prw[:, :, L])
            chain(dve.tensor_copy(cp[:, 1, 0, :], piw[:, :, L]))
            for lv in range(1, SCAN):
                a, b = cp[:, 0, lv - 1, :], cp[:, 1, lv - 1, :]
                cmul(cp[:, 0, lv, :], cp[:, 1, lv, :], a, b, a, b, sm(7))
            dve.engine_nop().then_inc(scan_powers, 1)
            for q in range(4):
                gs = slice(8 * q, 8 * q + 8)
                full = [P, 8, L + 1, GH]
                chain(tt(Wout[:, gs], CX[:, gs, :].unsqueeze(2).to_broadcast(full),
                         prw[:, gs].unsqueeze(3).to_broadcast(full), ALU.mult))
                chain(tt(wtmp, CXs[:, gs, :].unsqueeze(2).to_broadcast(full),
                         piw[:, gs].unsqueeze(3).to_broadcast(full), ALU.mult))
                tt(Wout[:, gs], Wout[:, gs], wtmp, ALU.subtract).then_inc(out_matrices, 1)

            dve.wait_ge(unit_taken, U_Q)
            for h in range(CH):
                last = dve.tensor_scalar(fT[:, h], fT[:, h], olb[:, h:h + 1], lb[:, h:h + 1], ALU.mult, ALU.add)
            chain(last)
            for lv in range(SCAN):
                w = 1 << lv
                for j in range(4):
                    gs = slice(8 * j, 8 * j + 8)
                    js = PS[:, 4 + j].rearrange("p (a b) -> p a b", a=8)
                    dve.wait_ge(state_turned, 4 * lv + j + 1)
                    chain(tt(scan2[:, gs, w:], js[:, :, 0:NC - w],
                             cp[:, 1, lv, gs].unsqueeze(2).to_broadcast([P, 8, NC - w]), ALU.mult))
                    dve.wait_ge(scan_part, 4 * lv + j + 1)
                    chain(tt(scan2[:, gs, w:], scan2[:, gs, w:], scan1[:, gs, w:], ALU.add))
                    tt(S[:, gs, w:], S[:, gs, w:], scan2[:, gs, w:], ALU.add).then_inc(scan_step, 1)
            dve.wait_ge(s5_computed, 4)
            chain(dve.tensor_scalar(kT, fT, -1.0, 1.0, ALU.mult, ALU.add))
            dve.engine_nop().then_inc(forget_ready, 1)
            dve.memset(sc, 0.0)
            ones = dec[0][:, 0, 0:P]
            chain(dve.memset(ones, 1.0))
            dve.wait_ge(log_forget, 1)
            for h in range(CH):
                for i in range(NT):
                    ts = slice(i * P, (i + 1) * P)
                    last = dve.tensor_tensor_scan(bT[:, h, ts], ones, fT[:, h, ts], 0.0, ALU.mult, ALU.add)
            chain(last)

            def level(lv):
                B = P >> (lv + 1)
                nb = CH * T // (2 * B)
                v = bT.rearrange("p h (n a b) -> p (h n) a b", a=2, b=B)
                o = dec[lv % 2].rearrange("p h (n a b) -> p (h n) a b", a=2, b=B)
                if lv >= 2:
                    dve.wait_ge(level_scored, CH * (lv - 1))
                ref = v[:, :, 0, B - 1:B].to_broadcast([P, nb, B])
                tt(o[:, :, 0, :], ref, v[:, :, 0, :], ALU.subtract)
                tt(o[:, :, 1, :], v[:, :, 1, :], ref, ALU.subtract).then_inc(decay_logs, 1)

            def keyed(lv):
                B = P >> (lv + 1)
                o = dec[lv % 2].rearrange("p h (n a b) -> p (h n) a b", a=2, b=B)
                q4 = qT.rearrange("p h (n a b) -> p (h n) a b", a=2, b=B)
                k4 = kT.rearrange("p h (n a b) -> p (h n) a b", a=2, b=B)
                dve.wait_ge(decays_ready, lv + 1)
                tt(o[:, :, 0, :], o[:, :, 0, :], k4[:, :, 0, :], ALU.mult)
                tt(o[:, :, 1, :], o[:, :, 1, :], q4[:, :, 1, :], ALU.mult).then_inc(keyed_ready, 1)

            def place(lv):
                B = P >> (lv + 1)
                if lv:
                    dve.wait_ge(level_placed, CH * lv)
                for h in range(CH):
                    dve.wait_ge(level_scored, CH * lv + (2 * (h // 2) + 2 if lv < LEVELS else h + 1))
                    if lv < LEVELS:
                        m = masks[:, lv, :].rearrange("p (n a b) -> p n a b", a=2, b=B)[:, :, 1, :]
                        dve.copy_predicated(
                            sc[:, h].rearrange("p (i n a b) -> p i n a b", i=NT, a=2, b=B)[:, :, :, 1, :],
                            m.unsqueeze(1).to_broadcast([P, NT, P // (2 * B), B]),
                            level_scores(lv, h).rearrange("p (i n b) -> p i n b", i=NT, b=B)).then_inc(level_placed, 1)
                        continue
                    dve.copy_predicated(sc[:, h].rearrange("p (a b) -> p a b", a=NT),
                                        masks[:, lv, :].unsqueeze(1).to_broadcast([P, NT, P]),
                                        PS[:, 4 + h].rearrange("p (a b) -> p a b", a=NT)).then_inc(level_placed, 1)

            dve.wait_ge(masks_ready, 1)
            level(0)
            level(1)
            keyed(0)
            dve.wait_ge(s5_loaded, 16)
            for m in range(CH):
                last = dve.scalar_tensor_tensor(yT[:, m].rearrange("p t c -> p (t c)"),
                                                uT[:, m].rearrange("p t c -> p (t c)"), dsk[:, m:m + 1],
                                                yT[:, m].rearrange("p t c -> p (t c)"), ALU.mult, ALU.add)
            last.then_inc(skip_added, 1)
            for lv in range(LEVELS):
                if lv + 1 < LEVELS:
                    keyed(lv + 1)
                else:
                    dve.engine_nop().then_inc(keyed_ready, 1)
                place(lv)
                if lv + 2 < LEVELS:
                    level(lv + 2)
                if lv == GLU_AT + 1:
                    for m in range(CH):
                        dve.wait_ge(glu_gate, m + 1)
                        tt(yaT[:, m].rearrange("p (c t) -> p t c", t=L), yT[:, m], zT[:, m], ALU.mult
                           ).then_inc(mixer_a_ready, 1)
            place(LEVELS)
            dve.wait_ge(level_scored, CH * (LEVELS + 1))
            chain(dve.tensor_copy(dec[1], bT))
            dve.engine_nop().then_inc(decay_logs, 1)
            b4 = bT.rearrange("p h (i t) -> p (h i) t", t=P)
            tt(dec[0].rearrange("p h (i t) -> p (h i) t", t=P), b4[:, :, P - 1:P].to_broadcast([P, CH * NT, P]),
               b4, ALU.subtract).then_inc(decay_logs, 1)
            dve.wait_ge(decay_logs, LEVELS + 2)
            dve.wait_ge(decays_ready, LEVELS + 1)
            chain(dve.tensor_copy(bT[:, 0, 0:CH * NT].rearrange("p (h i) -> p h i", h=CH),
                                  dec[1].rearrange("p h (i t) -> p h i t", t=P)[:, :, :, P - 1]))
            tt(dec[1], dec[1], qT, ALU.mult).then_inc(keyed_ready, 1)
            dve.wait_ge(decays_ready, LEVELS + 2)
            tt(dec[0], dec[0], kT, ALU.mult).then_inc(keyed_ready, 1)
            def gate_a(j):
                dve.wait_ge(a_projected, j + 1)
                tt(sga[:, j], bank_a(j), sga[:, j], ALU.mult).then_inc(gated_a, 1)

            gate_a(0)
            gate_a(1)
            dve.wait_ge(end_keys_turned, CH)
            for i in range(NT - 1):
                for h in range(CH):
                    kv = PS[:, 3, h * P:(h + 1) * P]
                    dve.wait_ge(update_computed, i + 1)
                    if i == 0:
                        dve.tensor_copy(state[:, h], kv).then_inc(state_ready, 1)
                    else:
                        dve.wait_ge(hgrn_computed, CH * i + h + 1)
                        dve.scalar_tensor_tensor(state[:, h], state[:, h], bT[:, 0, h * NT + i:h * NT + i + 1],
                                                 kv, ALU.mult, ALU.add).then_inc(state_ready, 1)
                gate_a(2 + i)
            gate_a(5)
            for h in range(CH):
                last = dve.tensor_scalar(gT[:, h], gT[:, h], gnw[:, h:h + 1], None, ALU.mult)
            chain(last)
            for h in range(CH):
                dve.wait_ge(hgrn_taken, 2 * h + 1)
                dve.wait_ge(root_ready, h + 1)
                chain(dve.reciprocal(qT[:, h], qT[:, h]))
                chain(tt(oT[:, h], oT[:, h], qT[:, h], ALU.mult))
                tt(oT[:, h], oT[:, h], gT[:, h], ALU.mult).then_inc(mixer_b_ready, 1)
                if h < 2:
                    gate_a(6 + h)
            def merge(i):
                ts = slice(i * P, (i + 1) * P)
                for g in range(2):
                    js = slice(KD // 2 * g, KD // 2 * (g + 1))
                    n = 2 * i + g
                    dve.wait_ge(b_projected, n + 1)
                    chain(tt(sgb[:, js, ts], PS[:, n % 4].rearrange("p (a b) -> p a b", b=P), sgb[:, js, ts], ALU.mult))
                    tt(mT[:, i, js], sga[:, js, ts], sgb[:, js, ts], ALU.add).then_inc(merged, 1)

            def norm(row, g, b, vsem, ssem, i, done):
                for e in range(2):
                    dve.bn_stats(stats[:, e, :], row[:, 512 * e:512 * e + 512])
                chain(dve.engine_nop())
                dve.bn_aggr(mv[:, :], stats[:, :, :].rearrange("p a b -> p (a b)")).then_inc(vsem, 1)
                dve.wait_ge(ssem, i + 1)
                chain(dve.reciprocal(rstd[:, 1:2], rstd[:, 0:1]))
                for e in range(2):
                    es = slice(512 * e, 512 * e + 512)
                    last = dve.scalar_tensor_tensor(row[:, es], row[:, es], mv[:, 0:1], g[:, es],
                                                    ALU.subtract, ALU.mult)
                chain(last)
                for e in range(2):
                    es = slice(512 * e, 512 * e + 512)
                    dve.scalar_tensor_tensor(row[:, es], row[:, es], rstd[:, 1:2], b[:, es], ALU.mult, ALU.add
                                             ).then_inc(done, 1)

            def mixed(i):
                dve.wait_ge(x_loaded[i], 16)
                for e in range(2):
                    es = slice(512 * e, 512 * e + 512)
                    dve.wait_ge(out_projected, 2 * i + e + 1)
                    dve.scalar_tensor_tensor(x1[:, i, es], x1[:, i, es], ALPHA, PS[:, 4 + 2 * (i % 2) + e],
                                             ALU.mult, ALU.add).then_inc(x_added, 1)

            def first_norm(i):
                dve.wait_ge(x_added, 2 * i + 2)
                norm(x1[:, i], g1, b1, ln1_var, ln1_root, i, x1_ready)

            dve.wait_ge(constants_loaded, 16 * N_CST)
            merge(0)
            merge(1)
            mixed(0)
            dve.wait_ge(ln1_loaded, 32)
            first_norm(0)
            merge(2)
            merge(3)
            STEPS = 20

            def top16(values, indices, source, scratch, flat, link):
                link(dve.max(values[:, 0:8], source))
                dve.max_index(indices[:, 0:8], values[:, 0:8], source)
                link(dve.match_replace(scratch, values[:, 0:8], source, LOW))
                link(dve.max(values[:, 8:16], scratch))
                link(dve.max_index(indices[:, 8:16], values[:, 8:16], scratch))

            def retrieve(n, par):
                at = [0]

                def link(ins):
                    at[0] += 1
                    ins.then_inc(retrieval_step, 1)
                    dve.wait_ge(retrieval_step, n * STEPS + at[0])
                    dve.nop(nofuse=True)

                dve.wait_ge(key_scores, n + 1)
                dve.nop(nofuse=True)
                for a in range(2):
                    top16(v16[:, a], i16[:, a, :], PS[:, 2, a * P:(a + 1) * P], srep, None, link)
                dve.engine_nop().then_inc(key_scores_read, 1)
                link(tt(cand, v16[:, 0].unsqueeze(2).to_broadcast([P, K, K]),
                        v16[:, 1].unsqueeze(1).to_broadcast([P, K, K]), ALU.add))
                top16(tv, ti[:, :], cand.rearrange("p a b -> p (a b)"), crep, None, link)
                dve.tensor_scalar(nmax[:, :], tv[:, 0:1], -1.0, None, ALU.mult).then_inc(top_found, 1)
                dve.tensor_copy(i16f, i16[:, :, :])
                dve.tensor_scalar(ta[:, 0, :], ti[:, :], 4, None, ALU.logical_shift_right)
                link(dve.tensor_scalar(ta[:, 1, :], ti[:, :], 15, None, ALU.bitwise_and))
                link(dve.tensor_copy(taf, ta[:, :, :]))
                full = [P, 2, K, K]
                link(tt(eq, taf.unsqueeze(3).to_broadcast(full),
                        iot[:, :].unsqueeze(1).unsqueeze(1).to_broadcast(full), ALU.is_equal))
                link(tt(eq, eq, i16f.unsqueeze(2).to_broadcast(full), ALU.mult))
                link(dve.tensor_reduce(e12, eq, AX_X, ALU.add))
                dve.scalar_tensor_tensor(idxU[par][:, :], e12[:, 0], float(P), e12[:, 1], ALU.mult, ALU.add
                                         ).then_inc(experts_found, 1)
                dve.wait_ge(exps_ready, n + 1)
                link(dve.reciprocal(erec[:, :], esum[:, :]))
                link(dve.tensor_scalar(gates[par][:, :], ex, erec[:, 0:1], None, ALU.mult))
                assert at[0] == STEPS, at[0]

            def dots(n, par, ks):
                for k in ks:
                    dve.wait_ge(u_gathered[k % NBUF], 16 * (2 * n + k // NBUF + 1))
                    dve.tensor_tensor_reduce(ubuf[k % NBUF], ubuf[k % NBUF], x1c[par], 1.0, 0.0, ALU.mult, ALU.add,
                                             acts[par][:, k:k + 1]).then_inc(u_dotted, 1)

            def coefficients(n, par):
                if not (isinstance(n, int) and n < 2):
                    dve.wait_ge(v_mixed, K * (n - 1))
                dve.tensor_copy(idxV[par][:, :], idxU[par][:, :])
                dve.wait_ge(acts_gelu, n + 1)
                tt(coef[par][:, :], ga16, gates[par][:, :], ALU.mult).then_inc(coef_ready, 1)

            def add_values(n, par, mixed_in=None):
                dve.wait_ge(v_mixed, K * (n + 1) if mixed_in is None else mixed_in)
                tile = n // HEADS
                row = yac[:, tile, :] if isinstance(n, int) else \
                    yac[:, bass.ds(tile, 1), :].rearrange("p a d -> p (a d)")
                tt(row, row, PS[:, 4 + 2 * par:6 + 2 * par].rearrange("p a b -> p (a b)"), ALU.add).then_inc(values_added, 1)

            def step(n, par, last=False):
                dots(n, par, range(0, 8))
                if isinstance(n, int) and n == 1:
                    for k in range(NBUF):
                        dve.wait_ge(v_gathered[k], 16)
                if not last:
                    retrieve(n + 1, 1 - par)
                dots(n, par, range(8, K))
                if not (isinstance(n, int) and n < 2):
                    dve.wait_ge(values_added, n - 1)
                coefficients(n, par)

            def adds(n, par):
                add_values(n, par)

            retrieve(0, 0)
            mixed(1)
            first_norm(1)
            mixed(2)
            first_norm(2)
            dots(0, 0, range(0, 8))
            retrieve(1, 1)
            mixed(3)
            dots(0, 0, range(8, K))
            first_norm(3)
            coefficients(0, 0)
            step(1, 1)
            dve.wait_ge(x1_scaled, NT)
            with dve.Fori(2, BLOCKS - 2, 2) as n:
                adds(n - 2, 0)
                step(n, 0)
                adds(n - 1, 1)
                step(n + 1, 1)
            def last_norm(i):
                norm(yac[:, i], g2, b2, ln2_var, ln2_root, i, result_ready)

            adds(BLOCKS - 4, 0)
            dve.wait_ge(ln2_loaded, 32)
            last_norm(0)
            last_norm(1)
            step(BLOCKS - 2, 0)
            adds(BLOCKS - 3, 1)
            last_norm(2)
            step(BLOCKS - 1, 1, last=True)
            adds(BLOCKS - 2, 0)
            def added(i, k):
                dve.wait_ge(values_added, BLOCKS - 1 + i)
                dve.wait_ge(v_gathered[k % NBUF], 16 * (2 * BLOCKS - 1 + k // NBUF))
                dve.scalar_tensor_tensor(yac[:, NT - 1], vbuf[k % NBUF], coef[1][:, k:k + 1], yac[:, NT - 1],
                                         ALU.mult, ALU.add).then_inc(values_added, 1)

            before = len(ADDED) - 2
            for i in range(before):
                added(i, ADDED[i])
            dve.wait_ge(values_added, BLOCKS - 1 + before)
            add_values(BLOCKS - 1, 1, K * BLOCKS - len(ADDED))
            for i in range(before, len(ADDED)):
                added(i + 1, ADDED[i])
            dve.wait_ge(values_added, BLOCKS + len(ADDED))
            last_norm(3)


_CALL = ["x", "xT", "w_in", "lam_re", "lam_im", "b_re", "b_im", "c_re", "c_im", "d_skip", "log_step", "w_glu", "b_glu",
         "lb_logits", "gnorm", "w_pa", "w_pb", "w_o", "ln1_g", "ln1_b", "w_pq", "keysT", "peer_u", "peer_v",
         "ln2_g", "ln2_b", "square_consts", "sign_consts", "iota16", "level_masks"]


def shape_constants():
    i = np.arange(P)
    ident = np.eye(P, dtype=np.float32)
    jt = np.zeros((P, P), np.float32)
    jt[NS + np.arange(NS), np.arange(NS)] = -1.0
    jt[np.arange(NS), NS + np.arange(NS)] = 1.0
    mean = np.full((P, P), 1.0 / P, np.float32)
    square = np.stack([ident, jt, mean], axis=1)
    sign = np.where(i < NS, -1.0, 1.0).astype(np.float32)
    masks = np.zeros((P, LEVELS + 1, P), np.float32)
    s, t = i[:, None], i[None, :]
    for lv in range(LEVELS):
        b = P >> (lv + 1)
        masks[:, lv] = (s // (2 * b) == t // (2 * b)) & (s % (2 * b) < b) & (t % (2 * b) >= b)
    masks[:, LEVELS] = s == t
    return {"square_consts": square, "sign_consts": np.stack([sign, -sign], axis=1),
            "iota16": np.tile(np.arange(K, dtype=np.float32), (P, 1)), "level_masks": masks}


def kernel(**inputs):
    import concourse.bacc as bacc
    from concourse.bass_utils import run_bass_kernel_spmd as run

    a = {k: np.asarray(v) for k, v in inputs.items()}

    def columns(v):
        return v.reshape(CH, P).T

    data = {
        "x": a["x"][0], "xT": a["x"][0].T, "w_in": a["w_in"][0],
        "lam_re": a["s5_lam_re"][0].T, "lam_im": a["s5_lam_im"][0].T,
        "b_re": a["s5_b_re"][0].transpose(1, 0, 2), "b_im": a["s5_b_im"][0].transpose(1, 0, 2),
        "c_re": a["s5_c_re"][0].transpose(2, 0, 1), "c_im": a["s5_c_im"][0].transpose(2, 0, 1),
        "d_skip": columns(a["s5_d"][0]), "log_step": a["s5_log_step"][0],
        "w_glu": a["s5_w_glu"][0], "b_glu": columns(a["s5_b_glu"][0]),
        "lb_logits": a["hgrn_lb_logits"].reshape(2, CH, P).transpose(2, 0, 1),
        "gnorm": columns(a["hgrn_gnorm_w"][0]),
        "w_pa": a["w_pa"][0], "w_pb": a["w_pb"][0], "w_o": a["w_o"][0],
        "ln1_g": a["ln1_g"][0], "ln1_b": a["ln1_b"][0], "w_pq": a["peer_w_q"][0],
        "keysT": a["peer_sub_keys"][0].reshape(2 * HEADS, P, P).transpose(2, 0, 1),
        "peer_u": a["peer_u"][0], "peer_v": a["peer_v"][0], "ln2_g": a["ln2_g"][0], "ln2_b": a["ln2_b"][0],
        **shape_constants(),
    }
    nc = bacc.Bacc("TRN2", target_bir_lowering=False, num_devices=1)
    arrays, args = {}, []
    for name in _CALL:
        v = np.ascontiguousarray(data[name])
        arrays[f"in_{name}"] = v
        args.append(nc.dram_tensor(f"in_{name}", v.shape, mybir.dt.from_np(v.dtype), kind="ExternalInput").ap())
    args.append(nc.dram_tensor("out", (T, D), F32, kind="ExternalOutput").ap())
    hybrid_layer(nc, *args)
    r = run(nc, [arrays], core_ids=[0])
    return r.results[0]["out"].reshape(1, T, D)
```
